# Optimizing a Trainium2 kernel written in Bass

```python
import math
import jax, jax.numpy as jnp
from jax import lax
import numpy as np
import jax
import jax.numpy as jnp

D_MODEL = 1024
BATCH = 1
SEQ = 512
DEPTH = 2

MEM_LEN = 256
MIX_W = D_MODEL
GROUP_W = MIX_W // 4
N_FOX_HEADS = 4
N_SB_HEADS = 4
N_MLA_HEADS = 4
N_MEM_HEADS = 4
HEAD_DIM = GROUP_W // 4
MLA_Q_RANK = 256
MLA_KV_RANK = 128
MLA_NOPE = HEAD_DIM
MLA_ROPE = 32
MLA_V = GROUP_W // N_MLA_HEADS
ROPE_THETA = 10000.0
BLOCK_Q = 128
LN_EPS = 1e-5
RMS_EPS = 1e-6
FOX_FORGET_BIAS_INIT = 3.0
DEEPNORM_ALPHA = (2 * DEPTH) ** 0.25
DEEPNORM_BETA = (8 * DEPTH) ** -0.25
SPLIT_SIZES = (GROUP_W, GROUP_W, GROUP_W, N_FOX_HEADS,
               GROUP_W, GROUP_W, GROUP_W,
               MLA_Q_RANK, MLA_KV_RANK, MLA_ROPE,
               GROUP_W,
               MIX_W)
IN_COLS = sum(SPLIT_SIZES)


def _layer_norm(x, g, b):
    xf = x.astype(jnp.float32)
    mu = jnp.mean(xf, axis=-1, keepdims=True)
    var = jnp.mean(jnp.square(xf - mu), axis=-1, keepdims=True)
    y = (xf - mu) * lax.rsqrt(var + LN_EPS) * g.astype(jnp.float32) + b.astype(jnp.float32)
    return y.astype(x.dtype)

def _rms_norm(x, g):
    xf = x.astype(jnp.float32)
    y = xf * lax.rsqrt(jnp.mean(jnp.square(xf), axis=-1, keepdims=True) + RMS_EPS)
    return (y * g.astype(jnp.float32)).astype(x.dtype)

def _heads(t, n):
    b, s, _ = t.shape
    return t.reshape(b, s, n, -1).transpose(0, 2, 1, 3)

def _merge(t):
    b, h, s, d = t.shape
    return t.transpose(0, 2, 1, 3).reshape(b, s, h * d)

def _rope(x, positions):
    half = x.shape[-1] // 2
    inv_freq = ROPE_THETA ** (-jnp.arange(half, dtype=jnp.float32) / half)
    ang = positions.astype(jnp.float32)[:, None] * inv_freq[None, :]
    ang = ang.reshape((ang.shape[0],) + (1,) * (x.ndim - 3) + (half,))
    cos, sin = jnp.cos(ang), jnp.sin(ang)
    xf = x.astype(jnp.float32)
    x1, x2 = xf[..., :half], xf[..., half:]
    return jnp.concatenate([x1 * cos - x2 * sin, x1 * sin + x2 * cos], axis=-1).astype(x.dtype)

def _sweep_query_blocks(block_fn, per_query):
    b, h, s = per_query[0].shape[:3]
    nb = s // BLOCK_Q
    blocks = tuple(jnp.moveaxis(a.reshape((b, h, nb, BLOCK_Q) + a.shape[3:]), 2, 0) for a in per_query)
    out = lax.map(lambda args: block_fn(args[0], *args[1:]), (jnp.arange(nb),) + blocks)
    out = jnp.moveaxis(out, 0, 2)
    return out.reshape(b, h, s, out.shape[-1])

def _causal_softmax_attention(q, k, v, scale, log_forget_cum=None):
    key_pos = jnp.arange(k.shape[2])

    def block(i, qb, *fq):
        q_pos = i * BLOCK_Q + jnp.arange(BLOCK_Q)
        logits = jnp.einsum('bhqd,bhkd->bhqk', qb, k).astype(jnp.float32) * scale
        if log_forget_cum is not None:
            logits = logits + fq[0][..., :, None] - log_forget_cum[:, :, None, :]
        mask = key_pos[None, :] <= q_pos[:, None]
        probs = jax.nn.softmax(jnp.where(mask, logits, -jnp.inf), axis=-1)
        return jnp.einsum('bhqk,bhkd->bhqd', probs.astype(v.dtype), v)

    per_query = (q,) if log_forget_cum is None else (q, log_forget_cum)
    return _sweep_query_blocks(block, per_query)

def _stick_breaking_attention(q, k, v, scale):
    key_pos = jnp.arange(k.shape[2])

    def block(i, qb):
        q_pos = i * BLOCK_Q + jnp.arange(BLOCK_Q)
        valid = key_pos[None, :] < q_pos[:, None]
        z = jnp.einsum('bhqd,bhkd->bhqk', qb, k).astype(jnp.float32) * scale
        log_keep = jnp.where(valid, jax.nn.log_sigmoid(-z), 0.0)
        log_tail = lax.cumsum(log_keep, axis=3, reverse=True) - log_keep
        w = jnp.where(valid, jnp.exp(jax.nn.log_sigmoid(z) + log_tail), 0.0)
        return jnp.einsum('bhqk,bhkd->bhqd', w.astype(v.dtype), v)

    return _sweep_query_blocks(block, (q,))

def first_inputs(seed: int = 0) -> dict:
    key = jax.random.key(seed)
    ks = jax.random.split(key, 18)
    f32 = jnp.float32
    nrm = lambda k, shape: jax.random.normal(k, shape, f32)
    return {
        'x': nrm(ks[0], (BATCH, SEQ, D_MODEL)),
        'mem': nrm(ks[1], (BATCH, MEM_LEN, D_MODEL)),
        'ln_in_g': 1.0 + 0.02 * nrm(ks[2], (D_MODEL,)),
        'ln_in_b': 0.02 * nrm(ks[3], (D_MODEL,)),
        'mem_ln_g': 1.0 + 0.02 * nrm(ks[4], (D_MODEL,)),
        'mem_ln_b': 0.02 * nrm(ks[5], (D_MODEL,)),
        'w_in': nrm(ks[6], (DEPTH, D_MODEL, IN_COLS)) * D_MODEL ** -0.5,
        'b_forget': FOX_FORGET_BIAS_INIT + 0.1 * nrm(ks[7], (DEPTH, N_FOX_HEADS)),
        'mla_q_norm_g': 1.0 + 0.02 * nrm(ks[8], (DEPTH, MLA_Q_RANK)),
        'w_mla_q_up': nrm(ks[9], (DEPTH, MLA_Q_RANK, N_MLA_HEADS * (MLA_NOPE + MLA_ROPE))) * MLA_Q_RANK ** -0.5,
        'mla_kv_norm_g': 1.0 + 0.02 * nrm(ks[10], (DEPTH, MLA_KV_RANK)),
        'w_mla_kv_up': nrm(ks[11], (DEPTH, MLA_KV_RANK, N_MLA_HEADS * (MLA_NOPE + MLA_V))) * MLA_KV_RANK ** -0.5,
        'w_mem_kv': nrm(ks[12], (DEPTH, D_MODEL, 2 * GROUP_W)) * D_MODEL ** -0.5,
        'w_out': nrm(ks[13], (DEPTH, MIX_W, D_MODEL)) * (MIX_W ** -0.5 * DEEPNORM_BETA),
        'ln_g': 1.0 + 0.02 * nrm(ks[14], (DEPTH, D_MODEL)),
        'ln_b': 0.02 * nrm(ks[15], (DEPTH, D_MODEL)),
    }

def first_block(x, mem, ln_in_g, ln_in_b, mem_ln_g, mem_ln_b, w_in, b_forget,
              mla_q_norm_g, w_mla_q_up, mla_kv_norm_g, w_mla_kv_up, w_mem_kv,
              w_out, ln_g, ln_b):
    b, s, _ = x.shape
    positions = jnp.arange(s)
    offsets = [int(o) for o in np.cumsum(SPLIT_SIZES)[:-1]]
    head_scale = HEAD_DIM ** -0.5
    mla_scale = (MLA_NOPE + MLA_ROPE) ** -0.5

    h_res = _layer_norm(x, ln_in_g, ln_in_b)
    mem_n = _layer_norm(mem, mem_ln_g, mem_ln_b)

    for l in range(DEPTH):
        proj = jnp.einsum('bsd,dc->bsc', h_res, w_in[l])
        (fq, fk, fv, f_logit, sq, sk, sv, c_q, c_kv, k_rot, mq, gate) = jnp.split(proj, offsets, axis=-1)

        log_f = jax.nn.log_sigmoid((f_logit + b_forget[l]).astype(jnp.float32))
        f_cum = jnp.cumsum(log_f, axis=1).transpose(0, 2, 1)
        out_fox = _causal_softmax_attention(_heads(fq, N_FOX_HEADS), _heads(fk, N_FOX_HEADS),
                                            _heads(fv, N_FOX_HEADS), head_scale, f_cum)

        out_sb = _stick_breaking_attention(_heads(sq, N_SB_HEADS), _heads(sk, N_SB_HEADS),
                                           _heads(sv, N_SB_HEADS), head_scale)

        q_mla = jnp.einsum('bsr,rc->bsc', _rms_norm(c_q, mla_q_norm_g[l]), w_mla_q_up[l])
        q_mla = q_mla.reshape(b, s, N_MLA_HEADS, MLA_NOPE + MLA_ROPE)
        q_full = jnp.concatenate([q_mla[..., :MLA_NOPE], _rope(q_mla[..., MLA_NOPE:], positions)], axis=-1)
        kv_mla = jnp.einsum('bsr,rc->bsc', _rms_norm(c_kv, mla_kv_norm_g[l]), w_mla_kv_up[l])
        kv_mla = kv_mla.reshape(b, s, N_MLA_HEADS, MLA_NOPE + MLA_V)
        k_rope = jnp.broadcast_to(_rope(k_rot, positions)[:, :, None, :], (b, s, N_MLA_HEADS, MLA_ROPE))
        k_full = jnp.concatenate([kv_mla[..., :MLA_NOPE], k_rope], axis=-1)
        v_mla = kv_mla[..., MLA_NOPE:]
        out_mla = _causal_softmax_attention(q_full.transpose(0, 2, 1, 3), k_full.transpose(0, 2, 1, 3),
                                            v_mla.transpose(0, 2, 1, 3), mla_scale)

        mkv = jnp.einsum('bmd,dc->bmc', mem_n, w_mem_kv[l])
        mk, mv = _heads(mkv[..., :GROUP_W], N_MEM_HEADS), _heads(mkv[..., GROUP_W:], N_MEM_HEADS)
        mem_logits = jnp.einsum('bhsd,bhmd->bhsm', _heads(mq, N_MEM_HEADS), mk).astype(jnp.float32) * head_scale
        mem_p = jax.nn.softmax(mem_logits, axis=-1)
        out_mem = jnp.einsum('bhsm,bhmd->bhsd', mem_p.astype(mv.dtype), mv)

        mixed = jnp.concatenate([_merge(out_fox), _merge(out_sb), _merge(out_mla), _merge(out_mem)], axis=-1)
        y = jnp.einsum('bsc,cd->bsd', mixed * jax.nn.silu(gate), w_out[l])

        h_res = _layer_norm(DEEPNORM_ALPHA * h_res + y, ln_g[l], ln_b[l])

    return h_res


GRID_W = 64
CTX_LEN = 256
HEAD_DIM_2 = 64
A_Q_HEADS = 8
A_KV_HEADS = 2
A_GROUP = A_Q_HEADS // A_KV_HEADS
A_WINDOW = 128
A_BLOCK = 128
B_HEADS = 4
NA_ROWS = 8
NA_COLS = 16
C_CHANNELS = 256
C_CONV_WIDTH = 31
A_Q_W = A_Q_HEADS * HEAD_DIM_2
A_KV_W = A_KV_HEADS * HEAD_DIM_2
B_W = B_HEADS * HEAD_DIM_2
MIX_WIDTH = A_Q_W + B_W + C_CHANNELS
IN_WIDTH = A_Q_W + 2 * A_KV_W + 3 * B_W + 2 * C_CHANNELS
OFF_AQ = 0
OFF_AK = OFF_AQ + A_Q_W
OFF_AV = OFF_AK + A_KV_W
OFF_BQ = OFF_AV + A_KV_W
OFF_BK = OFF_BQ + B_W
OFF_BV = OFF_BK + B_W
OFF_C = OFF_BV + B_W
N_EXPERTS = 16
EXPERT_FF = 1024
EC_CAPACITY = 2
ROPE_BASE = 10000.0
LN_EPS_2 = 1e-6
N_MOD = 6
MOD_INIT = 0.5
DEEPNORM_ALPHA_2 = (2 * DEPTH) ** 0.25
DEEPNORM_BETA_2 = (8 * DEPTH) ** -0.25
NEG_INF = -1e30


def layer_norm(x, g=None, b=None):
    xf = x.astype(jnp.float32)
    mu = jnp.mean(xf, axis=-1, keepdims=True)
    var = jnp.mean(jnp.square(xf - mu), axis=-1, keepdims=True)
    y = (xf - mu) * lax.rsqrt(var + LN_EPS_2)
    if g is not None:
        y = y * g.astype(jnp.float32) + b.astype(jnp.float32)
    return y.astype(x.dtype)

def modulate(x, shift, scale):
    return layer_norm(x) * (1 + scale) + shift

def adaln(cond, w_mod_l, b_mod_l, n_chunks):
    m = jax.nn.silu(cond) @ w_mod_l[:, :n_chunks * D_MODEL] + b_mod_l[:n_chunks * D_MODEL]
    return jnp.split(m, n_chunks, axis=-1)

def split_heads(t, n_heads):
    return t.reshape(t.shape[:-1] + (n_heads, HEAD_DIM_2))

def axial_rope(n_tokens, dtype):
    t = jnp.arange(n_tokens, dtype=jnp.int32)
    row = (t // GRID_W).astype(jnp.float32)[:, None]
    col = (t % GRID_W).astype(jnp.float32)[:, None]
    n_freq = HEAD_DIM_2 // 4
    inv_freq = ROPE_BASE ** (-jnp.arange(n_freq, dtype=jnp.float32) / n_freq)
    ang_r = row * inv_freq
    ang_c = col * inv_freq
    return (jnp.cos(ang_r)[:, None, :].astype(dtype), jnp.sin(ang_r)[:, None, :].astype(dtype),
            jnp.cos(ang_c)[:, None, :].astype(dtype), jnp.sin(ang_c)[:, None, :].astype(dtype))

def rope_half(x, cos, sin):
    x1, x2 = jnp.split(x, 2, axis=-1)
    return jnp.concatenate([x1 * cos - x2 * sin, x2 * cos + x1 * sin], axis=-1)

def apply_axial_rope(x, cos_r, sin_r, cos_c, sin_c):
    xr, xc = jnp.split(x, 2, axis=-1)
    return jnp.concatenate([rope_half(xr, cos_r, sin_r), rope_half(xc, cos_c, sin_c)], axis=-1)

def window_gqa_latent(q, k, v, kc, vc, sink):
    bsz, n_lat = q.shape[:2]
    n_blk = n_lat // A_BLOCK
    span = A_BLOCK + 2 * A_WINDOW
    pad = ((0, 0), (A_WINDOW, A_WINDOW), (0, 0), (0, 0))
    kp = jnp.pad(k, pad)
    vp = jnp.pad(v, pad)
    scale = HEAD_DIM_2 ** -0.5
    sink_l = sink.reshape(1, A_KV_HEADS, A_GROUP, 1, 1).astype(jnp.float32)
    q_off = jnp.arange(A_BLOCK)
    k_off = jnp.arange(span) - A_WINDOW
    band = jnp.abs(k_off[None, :] - q_off[:, None]) <= A_WINDOW

    def block(i):
        start = i * A_BLOCK
        qb = lax.dynamic_slice_in_dim(q, start, A_BLOCK, axis=1)
        kb = lax.dynamic_slice_in_dim(kp, start, span, axis=1)
        vb = lax.dynamic_slice_in_dim(vp, start, span, axis=1)
        kpos = start + k_off
        valid = band & ((kpos >= 0) & (kpos < n_lat))[None, :]
        s_win = jnp.einsum('bqhgd,bkhd->bhgqk', qb, kb).astype(jnp.float32) * scale
        s_win = jnp.where(valid, s_win, NEG_INF)
        s_ctx = jnp.einsum('bqhgd,bkhd->bhgqk', qb, kc).astype(jnp.float32) * scale
        s_sink = jnp.broadcast_to(sink_l, s_win.shape[:-1] + (1,))
        p = jax.nn.softmax(jnp.concatenate([s_win, s_ctx, s_sink], axis=-1), axis=-1).astype(q.dtype)
        return (jnp.einsum('bhgqk,bkhd->bqhgd', p[..., :span], vb)
                + jnp.einsum('bhgqk,bkhd->bqhgd', p[..., span:span + kc.shape[1]], vc))

    out = lax.map(block, jnp.arange(n_blk))
    return jnp.moveaxis(out, 0, 1).reshape(bsz, n_lat, A_Q_W)

def context_gqa(qc, kc, vc, sink):
    s = jnp.einsum('bqhgd,bkhd->bhgqk', qc, kc).astype(jnp.float32) * HEAD_DIM_2 ** -0.5
    s_sink = jnp.broadcast_to(sink.reshape(1, A_KV_HEADS, A_GROUP, 1, 1).astype(jnp.float32), s.shape[:-1] + (1,))
    p = jax.nn.softmax(jnp.concatenate([s, s_sink], axis=-1), axis=-1).astype(qc.dtype)
    o = jnp.einsum('bhgqk,bkhd->bqhgd', p[..., :-1], vc)
    return o.reshape(qc.shape[0], qc.shape[1], A_Q_W)

def neighbourhood_latent(q, k, v, kc, vc, rel_bias):
    bsz, n_lat = q.shape[:2]
    rows = n_lat // GRID_W
    kr_n = min(NA_ROWS, rows)
    n_keys = kr_n * GRID_W
    scale = HEAD_DIM_2 ** -0.5
    qg = q.reshape(bsz, rows, GRID_W, B_HEADS, HEAD_DIM_2)
    kg = k.reshape(bsz, rows, GRID_W, B_HEADS, HEAD_DIM_2)
    vg = v.reshape(bsz, rows, GRID_W, B_HEADS, HEAD_DIM_2)
    cols = jnp.arange(GRID_W)
    c_start = jnp.clip(cols - NA_COLS // 2, 0, GRID_W - NA_COLS)
    col_mask = (cols[None, :] >= c_start[:, None]) & (cols[None, :] < c_start[:, None] + NA_COLS)
    mask = jnp.broadcast_to(col_mask[:, None, :], (GRID_W, kr_n, GRID_W)).reshape(GRID_W, n_keys)
    dc = jnp.clip(cols[None, :] - cols[:, None], -(NA_COLS - 1), NA_COLS - 1) + NA_COLS - 1

    def row(r):
        r_start = jnp.clip(r - kr_n // 2, 0, rows - kr_n)
        qr = lax.dynamic_index_in_dim(qg, r, axis=1, keepdims=False)
        kr = lax.dynamic_slice_in_dim(kg, r_start, kr_n, axis=1).reshape(bsz, n_keys, B_HEADS, HEAD_DIM_2)
        vr = lax.dynamic_slice_in_dim(vg, r_start, kr_n, axis=1).reshape(bsz, n_keys, B_HEADS, HEAD_DIM_2)
        dr = r_start + jnp.arange(kr_n) - r + NA_ROWS - 1
        bias = rel_bias[:, dr[None, :, None], dc[:, None, :]].reshape(B_HEADS, GRID_W, n_keys)
        s_nb = jnp.einsum('bqhd,bkhd->bhqk', qr, kr).astype(jnp.float32) * scale + bias.astype(jnp.float32)
        s_nb = jnp.where(mask, s_nb, NEG_INF)
        s_ctx = jnp.einsum('bqhd,bkhd->bhqk', qr, kc).astype(jnp.float32) * scale
        p = jax.nn.softmax(jnp.concatenate([s_nb, s_ctx], axis=-1), axis=-1).astype(q.dtype)
        return (jnp.einsum('bhqk,bkhd->bqhd', p[..., :n_keys], vr)
                + jnp.einsum('bhqk,bkhd->bqhd', p[..., n_keys:], vc))

    out = lax.map(row, jnp.arange(rows))
    return jnp.moveaxis(out, 0, 1).reshape(bsz, n_lat, B_W)

def context_mha(qc, kc, vc):
    s = jnp.einsum('bqhd,bkhd->bhqk', qc, kc).astype(jnp.float32) * HEAD_DIM_2 ** -0.5
    p = jax.nn.softmax(s, axis=-1).astype(qc.dtype)
    o = jnp.einsum('bhqk,bkhd->bqhd', p, vc)
    return o.reshape(qc.shape[0], qc.shape[1], B_W)

def conformer_conv(u, conv_w, conv_b, ln_g, ln_b):
    a, gate = jnp.split(u, 2, axis=-1)
    h = a * jax.nn.sigmoid(gate)
    half = C_CONV_WIDTH // 2
    h = lax.conv_general_dilated(h, conv_w[:, None, :], window_strides=(1,), padding=((half, half),),
                                 dimension_numbers=('NWC', 'WIO', 'NWC'),
                                 feature_group_count=C_CHANNELS) + conv_b
    return jax.nn.silu(layer_norm(h, ln_g, ln_b))

def ec_moe(h, w_router, w_gate, w_up, w_down):
    bsz, n_tok, d = h.shape
    cap = EC_CAPACITY * n_tok // N_EXPERTS
    aff = jax.nn.softmax(jnp.einsum('bnd,de->bne', h, w_router).astype(jnp.float32), axis=-1)
    g, idx = lax.top_k(jnp.swapaxes(aff, 1, 2), cap)
    xs = jax.vmap(lambda hb, ib: hb[ib])(h, idx)
    hid = jax.nn.silu(jnp.einsum('becd,edf->becf', xs, w_gate)) * jnp.einsum('becd,edf->becf', xs, w_up)
    ye = jnp.einsum('becf,efd->becd', hid, w_down) * g[..., None].astype(h.dtype)
    return jax.vmap(lambda yb, ib: jnp.zeros((n_tok, d), h.dtype).at[ib.reshape(-1)].add(yb.reshape(-1, d)))(ye, idx)

def context_kv(hc, w_in_l):
    ka, va = jnp.split(hc @ w_in_l[:, OFF_AK:OFF_BQ], 2, axis=-1)
    kb, vb = jnp.split(hc @ w_in_l[:, OFF_BK:OFF_C], 2, axis=-1)
    return (split_heads(ka, A_KV_HEADS), split_heads(va, A_KV_HEADS),
            split_heads(kb, B_HEADS), split_heads(vb, B_HEADS))

def second_inputs(seed: int = 0) -> dict:
    key = jax.random.key(seed)
    ks = jax.random.split(key, 22)
    L, D = DEPTH, D_MODEL

    def nrm(k, shape, s):
        return s * jax.random.normal(k, shape, jnp.float32)

    return {
        'x': nrm(ks[0], (BATCH, SEQ, D), 1.0),
        'c': nrm(ks[1], (BATCH, D), 1.0),
        'ctx': nrm(ks[2], (BATCH, CTX_LEN, D), 1.0),
        'c_ctx': nrm(ks[3], (D,), 1.0),
        'w_mod': nrm(ks[4], (L, D, N_MOD * D), MOD_INIT * D ** -0.5),
        'b_mod': nrm(ks[5], (L, N_MOD * D), 0.02),
        'w_in': nrm(ks[6], (L, D, IN_WIDTH), D ** -0.5),
        'a_sink': nrm(ks[7], (L, A_Q_HEADS), 0.5),
        'nat_bias': nrm(ks[8], (L, B_HEADS, 2 * NA_ROWS - 1, 2 * NA_COLS - 1), 0.1),
        'conv_w': nrm(ks[9], (L, C_CONV_WIDTH, C_CHANNELS), C_CONV_WIDTH ** -0.5),
        'conv_b': nrm(ks[10], (L, C_CHANNELS), 0.02),
        'conv_ln_g': 1.0 + nrm(ks[11], (L, C_CHANNELS), 0.05),
        'conv_ln_b': nrm(ks[12], (L, C_CHANNELS), 0.02),
        'w_out': nrm(ks[13], (L, MIX_WIDTH, D), DEEPNORM_BETA_2 * MIX_WIDTH ** -0.5),
        'ln1_g': 1.0 + nrm(ks[14], (L, D), 0.05),
        'ln1_b': nrm(ks[15], (L, D), 0.02),
        'w_router': nrm(ks[16], (L, D, N_EXPERTS), D ** -0.5),
        'w_gate': nrm(ks[17], (L, N_EXPERTS, D, EXPERT_FF), D ** -0.5),
        'w_up': nrm(ks[18], (L, N_EXPERTS, D, EXPERT_FF), D ** -0.5),
        'w_down': nrm(ks[19], (L, N_EXPERTS, EXPERT_FF, D), DEEPNORM_BETA_2 * EXPERT_FF ** -0.5),
        'ln2_g': 1.0 + nrm(ks[20], (L, D), 0.05),
        'ln2_b': nrm(ks[21], (L, D), 0.02),
    }

def second_block(x, c, ctx, c_ctx, w_mod, b_mod, w_in, a_sink, nat_bias, conv_w, conv_b, conv_ln_g, conv_ln_b,
              w_out, ln1_g, ln1_b, w_router, w_gate, w_up, w_down, ln2_g, ln2_b):
    bsz, n_lat, _ = x.shape
    n_ctx = ctx.shape[1]
    rope = axial_rope(n_lat, x.dtype)
    for l in range(DEPTH):
        last = l == DEPTH - 1
        w_in_l = w_in[l]
        sh1, sc1, g1, sh2, sc2, g2 = [m[:, None, :] for m in adaln(c, w_mod[l], b_mod[l], N_MOD)]

        ctx_mod = adaln(c_ctx, w_mod[l], b_mod[l], 2 if last else N_MOD)
        hc = modulate(ctx, ctx_mod[0], ctx_mod[1])
        kc_a, vc_a, kc_b, vc_b = context_kv(hc, w_in_l)
        if not last:
            qc_a = split_heads(hc @ w_in_l[:, OFF_AQ:OFF_AK], A_Q_HEADS).reshape(bsz, n_ctx, A_KV_HEADS, A_GROUP, HEAD_DIM_2)
            qc_b = split_heads(hc @ w_in_l[:, OFF_BQ:OFF_BK], B_HEADS)
            oc = jnp.concatenate([
                context_gqa(qc_a, kc_a, vc_a, a_sink[l]),
                context_mha(qc_b, kc_b, vc_b),
                conformer_conv(hc @ w_in_l[:, OFF_C:], conv_w[l], conv_b[l], conv_ln_g[l], conv_ln_b[l]),
            ], axis=-1) @ w_out[l]
            ctx_new = layer_norm(DEEPNORM_ALPHA_2 * ctx + ctx_mod[2] * oc, ln1_g[l], ln1_b[l])
            hc2 = modulate(ctx_new, ctx_mod[3], ctx_mod[4])
            ctx_new = layer_norm(DEEPNORM_ALPHA_2 * ctx_new + ctx_mod[5] * ec_moe(hc2, w_router[l], w_gate[l], w_up[l], w_down[l]),
                                 ln2_g[l], ln2_b[l])

        h = modulate(x, sh1, sc1)
        u = h @ w_in_l
        q_a = apply_axial_rope(split_heads(u[..., OFF_AQ:OFF_AK], A_Q_HEADS), *rope)
        k_a = apply_axial_rope(split_heads(u[..., OFF_AK:OFF_AV], A_KV_HEADS), *rope)
        v_a = split_heads(u[..., OFF_AV:OFF_BQ], A_KV_HEADS)
        q_b = split_heads(u[..., OFF_BQ:OFF_BK], B_HEADS)
        k_b = split_heads(u[..., OFF_BK:OFF_BV], B_HEADS)
        v_b = split_heads(u[..., OFF_BV:OFF_C], B_HEADS)
        o_a = window_gqa_latent(q_a.reshape(bsz, n_lat, A_KV_HEADS, A_GROUP, HEAD_DIM_2), k_a, v_a, kc_a, vc_a, a_sink[l])
        o_b = neighbourhood_latent(q_b, k_b, v_b, kc_b, vc_b, nat_bias[l])
        o_c = conformer_conv(u[..., OFF_C:], conv_w[l], conv_b[l], conv_ln_g[l], conv_ln_b[l])
        o = jnp.concatenate([o_a, o_b, o_c], axis=-1) @ w_out[l]
        x = layer_norm(DEEPNORM_ALPHA_2 * x + g1 * o, ln1_g[l], ln1_b[l])
        h2 = modulate(x, sh2, sc2)
        x = layer_norm(DEEPNORM_ALPHA_2 * x + g2 * ec_moe(h2, w_router[l], w_gate[l], w_up[l], w_down[l]),
                       ln2_g[l], ln2_b[l])
        if not last:
            ctx = ctx_new
    return x


def setup_inputs(seed=0):
    out = dict(first_inputs(seed))
    for name, value in second_inputs(seed + 1).items():
        if name != "x":
            out[name + "_2"] = value
    return out


def reference(
    x, mem, ln_in_g, ln_in_b, mem_ln_g, mem_ln_b, w_in, b_forget, mla_q_norm_g, w_mla_q_up,
    mla_kv_norm_g, w_mla_kv_up, w_mem_kv, w_out, ln_g, ln_b, c_2, ctx_2, c_ctx_2, w_mod_2,
    b_mod_2, w_in_2, a_sink_2, nat_bias_2, conv_w_2, conv_b_2, conv_ln_g_2, conv_ln_b_2,
    w_out_2, ln1_g_2, ln1_b_2, w_router_2, w_gate_2, w_up_2, w_down_2, ln2_g_2, ln2_b_2,
):
    x = first_block(
        x, mem, ln_in_g, ln_in_b, mem_ln_g, mem_ln_b, w_in, b_forget, mla_q_norm_g, w_mla_q_up,
        mla_kv_norm_g, w_mla_kv_up, w_mem_kv, w_out, ln_g, ln_b,
    )
    return second_block(
        x, c_2, ctx_2, c_ctx_2, w_mod_2, b_mod_2, w_in_2, a_sink_2, nat_bias_2, conv_w_2,
        conv_b_2, conv_ln_g_2, conv_ln_b_2, w_out_2, ln1_g_2, ln1_b_2, w_router_2, w_gate_2,
        w_up_2, w_down_2, ln2_g_2, ln2_b_2,
    )


_drawn_inputs = setup_inputs


def setup_inputs(seed=0):
    import zlib

    import numpy as np

    out = dict(_drawn_inputs(seed))
    spreads = {}
    factors = {'mem': 3.756,
     'ln_in_g': 2.74,
     'ln_in_b': 2.899,
     'mem_ln_g': 8.0,
     'mem_ln_b': 8.0,
     'b_forget': 64.0,
     'mla_q_norm_g': 8.0,
     'w_mla_q_up': 2.838,
     'mla_kv_norm_g': 8.0,
     'w_mem_kv': 3.435,
     'ctx_2': 200.0,
     'b_mod_2': 8.0,
     'a_sink_2': 195.213,
     'nat_bias_2': 64.0,
     'conv_b_2': 8.0,
     'conv_ln_g_2': 8.0,
     'conv_ln_b_2': 44.87,
     'c_ctx_2': 4.021}
    for name, (base, spread) in spreads.items():
        noise = np.random.default_rng([zlib.crc32(name.encode()), seed]).standard_normal(out[name].shape)
        drawn = base * np.exp(spread * noise) if base else spread * noise
        out[name] = jnp.asarray(drawn.astype(out[name].dtype))
    for name, factor in factors.items():
        out[name] = (out[name] * factor).astype(out[name].dtype)
    return out
```

```python
from contextlib import ExitStack

import numpy as np

import concourse.bass as bass
from concourse import mybir

F32 = mybir.dt.float32
I32 = mybir.dt.int32
U32 = mybir.dt.uint32
ALU = mybir.AluOpType
ACT = mybir.ActivationFunctionType
AX = mybir.AxisListType.X

P = 128
D = 1024
KD = D // P
SEQ = 512
NT = SEQ // P
CTX = 256
NC = CTX // P
DEPTH = 2
HEADS = 4
HD = 64
ROPE = 32
MLA_QK = HD + ROPE
QR = 256
KVR = 128
ALPHA = (2 * DEPTH) ** 0.25
LN_EPS = 1e-5
RMS_EPS = 1e-6
LN_EPS_2 = 1e-6
NEG = -1e30
BIG = 3e38
KROWS = 96
TAPS = 31
HALO = TAPS // 2
EXPERTS = 16
CAP = 2 * SEQ // EXPERTS
CAP_C = 2 * CTX // EXPERTS
RING = 12
UC = 4
N_MOD = 6

O_FQ, O_FK, O_FV, O_FL = 0, 256, 512, 768
O_SQ, O_SK, O_SV = 772, 1028, 1284
O_CQ, O_CKV, O_KR, O_MQ, O_GATE = 1540, 1796, 1924, 1956, 2212
O_AQ, O_AK, O_AV, O_BQ, O_BK, O_BV, O_C = 0, 512, 640, 768, 1024, 1280, 1536

C_IDENT, C_CAUSAL, C_BEFORE, C_TRI, C_NEG1, C_STRICT, C_BIG, C_ONE, C_ROTM, C_ROTA = range(0, 1280, 128)
C_COS, C_SIN = 1280, 1280 + SEQ
C_COLMASK = 1280 + 2 * SEQ
C_END = C_COLMASK + 64

V_BMOD = 0
V_CONVW = V_BMOD + DEPTH * 48
V_CONVB = V_CONVW + DEPTH * 2 * TAPS
V_CLNG = V_CONVB + DEPTH * 2
V_CLNB = V_CLNG + DEPTH * 2
V_MQG = V_CLNB + DEPTH * 2
V_MKVG = V_MQG + DEPTH * 2
V_BF = V_MKVG + DEPTH
V_SINK = V_BF + DEPTH
V_COND = V_SINK + DEPTH * 8
V_END = V_COND + 2 * KD


def tiles_of(l):
    return NT + NC if l < DEPTH - 1 else NT


def shape_constants():
    i = np.arange(P)
    c = np.zeros((P, C_END), np.float32)
    c[:, C_IDENT:C_IDENT + P] = np.eye(P)
    c[:, C_CAUSAL:C_CAUSAL + P] = np.where(i[None, :] <= i[:, None], 0.0, NEG)
    c[:, C_BEFORE:C_BEFORE + P] = np.where(i[None, :] >= i[:, None], 0.0, NEG)
    c[:, C_TRI:C_TRI + P] = np.where(i[:, None] >= i[None, :], -1.0, 0.0)
    c[:, C_NEG1:C_NEG1 + P] = -1.0
    c[:, C_STRICT:C_STRICT + P] = np.where(i[:, None] < i[None, :], 1.0, 0.0)
    c[:, C_BIG:C_BIG + P] = np.where(i[:, None] < i[None, :], BIG, 0.0)
    c[:, C_ONE:C_ONE + P] = 1.0
    rot = np.zeros((P, P), np.float32)
    for j in range(ROPE // 2):
        rot[HD + ROPE // 2 + j, HD + j] = -1.0
        rot[HD + j, HD + ROPE // 2 + j] = 1.0
    c[:, C_ROTM:C_ROTM + P] = rot
    rot = np.zeros((P, P), np.float32)
    for o in range(0, P, 32):
        for j in range(16):
            rot[o + 16 + j, o + j] = -1.0
            rot[o + j, o + 16 + j] = 1.0
    c[:, C_ROTA:C_ROTA + P] = rot
    half = ROPE // 2
    pos = np.arange(SEQ, dtype=np.float32)
    inv = np.float32(10000.0) ** (-np.arange(half, dtype=np.float32) / np.float32(half))
    ang = (pos[:, None] * inv[None, :]).astype(np.float32).T
    for o in (HD, HD + half):
        c[o:o + half, C_COS:C_COS + SEQ] = np.cos(ang)
        c[o:o + half, C_SIN:C_SIN + SEQ] = np.sin(ang)
    q = np.arange(64)
    start = np.clip(q - 8, 0, 48)
    seen = (q[None, :] >= start[:, None]) & (q[None, :] < start[:, None] + 16)
    c[:, C_COLMASK:C_COLMASK + 64] = np.tile(np.where(seen, 0.0, NEG), (2, 1))
    axial = np.zeros((P, 2 * SEQ), np.float32)
    tok = np.arange(SEQ)
    for o in range(0, P, 16):
        place = (tok // 64 if (o // 32) % 2 == 0 else tok % 64).astype(np.float32)
        a = (place[:, None] * inv[None, :]).astype(np.float32).T
        axial[o:o + 16, 0:SEQ] = np.cos(a)
        axial[o:o + 16, SEQ:] = np.sin(a)
    return c, axial


def build_program(nc, a, known, banks, sem_names, stop=99):
    counts, marks, places, sems = {}, {}, {}, {}
    frozen = [False]

    with ExitStack() as ctx:
        def sb(name, shape, dt=F32):
            return ctx.enter_context(nc.sbuf_tensor(name, shape, dt))

        def sem(name):
            if name not in sems:
                sems[name] = ctx.enter_context(nc.semaphore(name))
            return sems[name]

        def done(name, event=None, by=1):
            if not frozen[0]:
                counts[name] = counts.get(name, 0) + by
                marks[(name, event)] = counts[name]
            return sem(name), by

        def at(name, event=None):
            return sem(name), known.get((name, event), 1)

        def emptied(job):
            for name in ("evac_act", "evac_dve"):
                if (name, job) in known:
                    return at(name, job)
            return at("evac_act", job)

        ring = sb("ring", [P, RING, KD * P])
        h = sb("h", [P, NT, D])
        hc = sb("hc", [P, NC, D])
        hT = sb("hT", [P, KD, SEQ])
        hcT = sb("hcT", [P, KD, CTX])
        mixT = sb("mixT", [P, KD, SEQ])
        mixcT = sb("mixcT", [P, KD, CTX])
        qz = sb("qz", [P, HEADS, SEQ])
        kz = sb("kz", [P, HEADS, SEQ])
        v = sb("v", [P, NT, 256])
        const = sb("const", [P, C_END])
        vec = sb("vec", [P, V_END])
        probs = sb("probs", [P, 3 * 768])
        probsT = sb("probsT", [P, 2, 6, P])
        work = sb("work", [P, 8448])
        wkvup = sb("wkvup", [P, HEADS * 2 * HD])
        cond = sb("cond", [P, KD, 32])
        modrow = sb("modrow", [P, P])
        modc = sb("modc", [P, DEPTH, 48, 2])
        col = sb("col", [P, 80])
        aff = sb("aff", [P, NT + NC, EXPERTS])
        wr = sb("wr", [P, KD, EXPERTS])
        gates = sb("gates", [P, EXPERTS + 1])
        idxf = sb("idxf", [P, EXPERTS + 1])
        idx = sb("idx", [P, EXPERTS + 2], I32)
        idx_at = [sb(f"idx_at{b}", [P, 1], I32) for b in range(2)]
        idx_to = [sb(f"idx_to{b}", [P, 1], I32) for b in range(2)]

        xt = kz[:, :, :].rearrange("p a b -> p (a b)").rearrange("p (r d) -> p r d", r=2)
        h2t = qz[:, :, :].rearrange("p a b -> p (a b)").rearrange("p (r k t) -> p r k t", r=2, k=KD)
        lnrow = work[:, 0:2 * D].rearrange("p (r d) -> p r d", r=2)
        grow = work[:, 2 * D:4 * D].rearrange("p (r d) -> p r d", r=2)
        sp_off = [0, 512, 896, 1152]
        SPW = 1280
        sp = work[:, 0:2 * SPW].rearrange("p (r n) -> p r n", r=2)
        sbw = work[:, 2 * SPW:4 * SPW].rearrange("p (r n) -> p r n", r=2)
        sbt = work[:, 4 * SPW:4 * SPW + 1024].rearrange("p (r n) -> p r n", r=2)
        cqT = work[:, 0:1024].rearrange("p (c n) -> p c n", c=2)
        ckvT = work[:, 1024:1536]
        sqT = work[:, 1536:3072].rearrange("p (c n) -> p c n", c=3)
        rms = work[:, 3072:4096].rearrange("p (c n) -> p c n", c=2)
        rope_t = work[:, 4096:4608]
        kr = work[:, 6144:6656]
        flog = work[:, 6656:7168]
        fls = work[:, 7168:8192].rearrange("p (r n) -> p r n", r=2)
        hcf = hc[:, :, :].rearrange("p a b -> p (a b)")
        wmisc = hcf[:, 0:1024].rearrange("p (k n) -> p k n", k=KD)
        wqup = hcf[:, 1024:1024 + 2 * HEADS * MLA_QK].rearrange("p (k n) -> p k n", k=2)
        hp = work[:, 0:2 * (SEQ + 2 * HALO)].rearrange("p (c n) -> p c n", c=2)
        acc = work[:, 1088:2112].rearrange("p (c n) -> p c n", c=2)
        csq = work[:, 2112:3136].rearrange("p (c n) -> p c n", c=2)
        csd = work[:, 3136:3648]
        glu = work[:, 3648:4160]
        rt1 = work[:, 4160:4672]
        rt2 = csq[:, 0, :]
        QC = work[:, 5120:6144].rearrange("p (a n) -> p a n", a=HEADS)
        KC = work[:, 6144:7680].rearrange("p (a n) -> p a n", a=6)
        VC = work[:, 7680:8448].rearrange("p (t n) -> p t n", t=NC)

        def bias_of(hh):
            return work[:, hh * D:(hh + 1) * D]

        affT = probs[0:EXPERTS, 0:SEQ + CTX]
        topv = probs[0:EXPERTS, 768:864]
        topf = probs[0:EXPERTS, 864:960]
        topi = sb("topi", [EXPERTS, 96], U32)
        hTf = hT[:, :, :].rearrange("p a b -> p (a b)")
        xs = hTf[:, 0:2 * D].rearrange("p (r d) -> p r d", r=2)
        xsT = hTf[:, 2 * D:2 * D + 2 * KD * 96].rearrange("p (r k t) -> p r k t", r=2, k=KD)
        sig = work[:, 4096:4608]
        sigc = work[:, 4608:4864]
        hid = work[:, 4864:5376]
        hidc = work[:, 5376:5632]
        hidT = work[:, 5632:5632 + 768].rearrange("p (k t) -> p k t", k=KD)
        ye = hcT[:, :, :].rearrange("p a b -> p (a b)").rearrange("p (r d) -> p r d", r=2)
        ysb = mixT[:, :, :].rearrange("p a b -> p (a b)").rearrange("p (t d) -> p t d", t=NT)
        ysbc = mixcT[:, :, :].rearrange("p a b -> p (a b)").rearrange("p (t d) -> p t d", t=NC)

        ps = ctx.enter_context(nc.psum_tensor("ps", [P, 8, 512], F32))
        psflat = ps[:, :, :].rearrange("p b n -> p (b n)")

        def cst(o, n=P, rows=slice(0, P)):
            return const[rows, o:o + n]

        ident = cst(C_IDENT)

        def ctile(t):
            return t >= NT

        def res(t):
            return hc[:, t - NT, :] if ctile(t) else h[:, t, :]

        def bank_of(job):
            return banks.get(("job", job), 6)

        job_ring = [6, 7]
        bank_user = {}

        def open_job(pe, job):
            b = job_ring.pop(0)
            job_ring.append(b)
            if b in bank_user:
                pe.wait_ge(*emptied(bank_user[b]))
            bank_user[b] = job
            places[("job", job)] = b
            return b

        slot_keys = []
        slot_uses = [0] * RING

        def load_slot(eng, key, src):
            n = len(slot_keys)
            s = n % RING
            if n >= RING and slot_keys[n - RING][0] == "moe_end":
                ml = slot_keys[n - RING][1]
                eng.wait_ge(sem("moe_k"), known.get(("moe_k", (ml, 0, 0, 0)), 1) + 48 * ROUNDS - RING + s)
            elif n >= RING:
                eng.wait_ge(*at(*banks.get(("last", slot_keys[n - RING]), ("job_done", None))))
            slot_keys.append(key)
            slot_uses[s] += 1
            places[("slot", key)] = (s, 16 * slot_uses[s])
            eng.dma_start(ring[:, s, :].rearrange("p (k n) -> p k n", k=KD), src).then_inc(sem(f"slot{s}"), 16)

        def slot(pe, key):
            s, n = banks.get(("slot", key), (0, 16))
            pe.wait_ge(sem(f"slot{s}"), n)
            return ring[:, s, :].rearrange("p (k n) -> p k n", k=KD)

        def last_use(key, job):
            places[("last", key)] = ("job_done", job)

        def last_in_slot(s):
            return [key for n, key in enumerate(slot_keys) if n % RING == s and key is not None][-1]

        mod_order = [(l, j) for l in range(DEPTH) for j in range(12)]

        def w_cols(w, l, c0, n=P):
            return w[l, :, c0:c0 + n].rearrange("(k p) c -> p k c", p=P)

        def units_of(ph):
            kind, l, part = ph
            n = NC if kind in ("ca", "cb") else NT
            return [(ph, t, hh) for t in range(n) for hh in range(HEADS)]

        def keys_of(u):
            (kind, l, part), t, hh = u
            if kind in ("fox", "mla"):
                return t + 1
            if kind in ("mem", "ca", "cb"):
                return NC
            if kind == "wa":
                return (2 if t in (0, NT - 1) else 3) + NC
            return NT + NC

        seq = {}

        def all_phases():
            out = []
            for l in range(DEPTH):
                out += [("fox", l, 0), ("mla", l, 0), ("mem", l, 0)]
            for l in range(DEPTH):
                for part in range(2):
                    out += [("wa", l, part)] + ([("ca", l, part)] if l == 0 else [])
                out += [("nb", l, 0)] + ([("cb", l, 0)] if l == 0 else [])
            return out

        n_units = 0
        for ph in all_phases():
            for u in units_of(ph):
                seq[u] = n_units
                n_units += 1
        by_seq = {n: u for u, n in seq.items()}

        def has_sink(u):
            return u[0][0] in ("wa", "ca")

        def sink_col(u):
            (kind, l, part), t, hh = u
            c = V_SINK + 8 * l + 4 * part + hh
            return vec[:, c:c + 1]

        def chunks_of(u):
            n = keys_of(u)
            return [range(c, min(c + 4, n)) for c in range(0, n, 4)]

        turn_seq = []
        for n in range(n_units):
            turn_seq += [(by_seq[n], c) for c in range(len(chunks_of(by_seq[n])))]
        turn_at = {x: n for n, x in enumerate(turn_seq)}

        def ring_col(first):
            return lambda u: col[:, first + seq[u] % UC:first + 1 + seq[u] % UC]

        nmax, rsum, rinv, esink, rmax = (ring_col(60 + UC * k) for k in range(5))

        def wide(ph):
            return ph[0] in ("wa", "nb")

        def lag_of(ph):
            return 2 if wide(ph) else 3

        def score_span(u):
            o = (seq[u] % 2) * 1024 if wide(u[0]) else (seq[u] % 4) * 512
            return o, o + keys_of(u) * P

        def probs_span(u):
            o = (seq[u] % 3) * 768 if wide(u[0]) else (seq[u] % 4) * 512
            return o, o + keys_of(u) * P

        def before(u, span):
            a0, a1 = span(u)
            for n in range(seq[u] - 1, max(seq[u] - 9, -1), -1):
                b0, b1 = span(by_seq[n])
                if a0 < b1 and b0 < a1:
                    return by_seq[n]
            return None

        def s_psum(u):
            return psflat[:, slice(*score_span(u))]

        def p_sbuf(u):
            return probs[:, slice(*probs_span(u))]

        def pair_job(u):
            return ("pv", u[0], u[1], u[2] // 2)

        def mix_out(u):
            (kind, l, part), t, hh = u
            chunk = {"fox": 0, "mla": 4, "mem": 6, "wa": 2 * part, "ca": 2 * part, "nb": 4, "cb": 4}[kind] + hh // 2
            dst = mixcT if kind in ("ca", "cb") else mixT
            return dst[:, chunk, t * P:(t + 1) * P]

        def pe_t_job(pe, job, slot_key, rhs, n, last=True):
            w = slot(pe, slot_key)
            b = open_job(pe, job)
            for k in range(KD):
                mm = nc.tensor.matmul(ps[:, b, 0:n], w[:, k, :], rhs[:, k, 0:n], start=(k == 0), stop=(k == KD - 1))
            mm.then_inc(*done("job_done", job))
            if last:
                last_use(slot_key, job)

        def pe_n_job(pe, job, slot_key, lhs, tiles, last=True):
            w = slot(pe, slot_key)
            b = open_job(pe, job)
            for t in range(tiles):
                for k in range(KD):
                    mm = nc.tensor.matmul(ps[:, b, t * P:(t + 1) * P], lhs[:, k, t * P:(t + 1) * P], w[:, k, :],
                                          start=(k == 0), stop=(k == KD - 1))
            mm.then_inc(*done("job_done", job))
            if last:
                last_use(slot_key, job)

        def pe_scores(pe, u):
            (kind, l, part), t, hh = u
            w = before(u, score_span)
            if w is not None:
                pe.wait_ge(*at("probs", w))
            S = s_psum(u)
            q = (QC if kind in ("ca", "cb") else qz)[0:KROWS, hh, t * P:(t + 1) * P]
            parts = []
            if kind in ("fox", "mla"):
                parts = [(q, kz[0:KROWS, hh, 0:(t + 1) * P], 0), (ident, cst(C_CAUSAL), t * P)]
            elif kind == "mem":
                parts = [(q, kz[0:KROWS, hh, 0:CTX], 0)]
            elif kind in ("ca", "cb"):
                parts = [(q, KC[0:KROWS, part if kind == "ca" else 2 + hh, :], 0)]
            elif kind == "nb":
                o = (7 - 2 * t) * 64
                parts = [(q, kz[0:KROWS, hh, :], 0), (ident, bias_of(hh)[:, o:o + SEQ], 0),
                         (q, KC[0:KROWS, 2 + hh, :], SEQ)]
                pe.wait_ge(*at("bias_ready", (l, hh)))
            else:
                j0, j1 = max(t - 1, 0), min(t + 1, NT - 1)
                w = (j1 - j0 + 1) * P
                parts = [(q, kz[0:KROWS, part, j0 * P:(j1 + 1) * P], 0)]
                if t > 0:
                    parts.append((ident, cst(C_BEFORE), 0))
                if t < NT - 1:
                    parts.append((ident, cst(C_CAUSAL), w - P))
                parts += [(q, KC[0:KROWS, part, c * P:(c + 1) * P], w + c * P) for c in range(NC)]
            for lhs, rhs, o in parts:
                mm = nc.tensor.matmul(S[:, o:o + rhs.shape[-1]], lhs, rhs, start=lhs is not ident, stop=True,
                                      skip_group_check=True)
            mm.then_inc(*done("scores", u))

        def v_block(u, j):
            (kind, l, part), t, hh = u
            if kind in ("fox", "mla", "mem"):
                return v[:, j, hh * HD:(hh + 1) * HD]
            if kind == "ca":
                return VC[:, j, part * HD:(part + 1) * HD]
            if kind == "cb":
                return VC[:, j, P + hh * HD:P + (hh + 1) * HD]
            if kind == "nb":
                return v[:, j, hh * HD:(hh + 1) * HD] if j < NT else VC[:, j - NT, P + hh * HD:P + (hh + 1) * HD]
            j0, j1 = max(t - 1, 0), min(t + 1, NT - 1)
            w = j1 - j0 + 1
            return v[:, j0 + j, part * HD:(part + 1) * HD] if j < w else VC[:, j - w, part * HD:(part + 1) * HD]

        def pe_turn(pe, u):
            pe.wait_ge(*at("probs_normed", u))
            for c, blocks in enumerate(chunks_of(u)):
                n = turn_at[(u, c)]
                if n >= 2:
                    pe.wait_ge(*at("probsT_ready", turn_seq[n - 2]))
                for i, j in enumerate(blocks):
                    mm = nc.tensor.transpose(ps[:, 4 + n % 2, i * P:(i + 1) * P],
                                             p_sbuf(u)[:, j * P:(j + 1) * P], ident)
                mm.then_inc(*done("turned", (u, c)))

        def pe_pv(pe, u):
            pair = [(u[0], u[1], u[2] - 1), u]
            job = pair_job(u)
            b = open_job(pe, job)
            for w in pair:
                pe.wait_ge(*at("probsT_ready", (w, len(chunks_of(w)) - 1)))
            n = keys_of(u)
            for j in range(n):
                for e, w in enumerate(pair):
                    mm = nc.tensor.matmul(ps[e * HD:(e + 1) * HD, b, 0:P], v_block(w, j),
                                          probsT[:, seq[w] % 2, j, :], start=(j == 0), stop=(j == n - 1))
            mm.then_inc(*done("job_done", job))

        def pe_softmax(pe, ph):
            us = units_of(ph)
            lag = lag_of(ph)
            for i in range(len(us) + lag + 1):
                if i < len(us):
                    pe_scores(pe, us[i])
                if lag <= i < len(us) + lag:
                    pe_turn(pe, us[i - lag])
                if i > lag and us[i - lag - 1][2] % 2:
                    pe_pv(pe, us[i - lag - 1])

        def sb_unit(n):
            return n // 4, 3 - n % 4

        def pe_stick(pe, l):
            for n in range(4 * HEADS + 2):
                if n < 4 * HEADS:
                    hh, i = sb_unit(n)
                    w = SEQ - i * P
                    if n >= 2:
                        pe.wait_ge(*at("softplus_raw", (l, n - 2)))
                    nc.tensor.matmul(ps[:, n % 2, 0:w], kz[0:KROWS, hh, i * P:(i + 1) * P], qz[0:KROWS, hh, i * P:SEQ],
                                     start=True, stop=True).then_inc(*done("sb_logits", (l, n)))
                if n >= 2:
                    m = n - 2
                    hh, i = sb_unit(m)
                    w = SEQ - i * P
                    if m >= 2:
                        pe.wait_ge(*at("sb_weights", (l, m - 2)))
                    nc.tensor.matmul(ps[:, 2 + m % 2, 0:w], kz[0:KROWS, hh, i * P:(i + 1) * P],
                                     qz[0:KROWS, hh, i * P:SEQ], start=True, stop=False, skip_group_check=True)
                    for j in range(i, 4):
                        if j == i:
                            pe.wait_ge(*at("softplus", (l, m)))
                        mm = nc.tensor.matmul(ps[:, 2 + m % 2, (j - i) * P:w], cst(C_TRI if j == i else C_NEG1),
                                              sp[:, hh % 2, sp_off[j]:sp_off[j] + SEQ - j * P], start=False,
                                              stop=(j == 3), skip_group_check=True)
                    mm.then_inc(*done("sb_logw", (l, m)))
                    if i == 0 and hh % 2:
                        job = ("sbpv", l, hh // 2)
                        b = open_job(pe, job)
                        pe.wait_ge(*at("sb_weights", (l, m)))
                        for j in range(4):
                            for e in range(2):
                                mm = nc.tensor.matmul(ps[e * HD:(e + 1) * HD, b, j * P:SEQ],
                                                      v[:, j, (hh - 1 + e) * HD:(hh + e) * HD],
                                                      sbw[:, e, sp_off[j]:sp_off[j] + SEQ - j * P],
                                                      start=(j == 0), stop=(j == 3), skip_group_check=True)
                        mm.then_inc(*done("job_done", job))

        mod_pe = iter(mod_order)

        def pe_modulation(pe, n):
            for _ in range(n):
                l, j = next(mod_pe)
                w = [slot(pe, ("mod", l, 4 * j + q)) for q in range(4)]
                job = ("mod", l, j)
                b = open_job(pe, job)
                for k in range(KD):
                    for q in range(4):
                        mm = nc.tensor.matmul(ps[32 * q:32 * q + 32, b, 0:P], cond[:, k, :], w[q][:, k, :],
                                              start=(k == 0), stop=(k == KD - 1), skip_group_check=True)
                mm.then_inc(*done("job_done", job))
                for q in range(4):
                    last_use(("mod", l, 4 * j + q), job)
                job = ("modT", l, j)
                b = open_job(pe, job)
                pe.wait_ge(*emptied(("mod", l, j)))
                nc.tensor.transpose(ps[:, b, 0:P], modrow[:, :], ident).then_inc(*done("job_done", job))

        def pe_head(pe, st, t):
            kind = st[0]
            pe.wait_ge(*at("tile_ready", (st, t)))
            src = res(t) if kind == "plain" else xt[:, t % 2, :]
            for half in range(2):
                job = ("turn", st, t, half)
                b = open_job(pe, job)
                for c in range(4):
                    o = (4 * half + c) * P
                    mm = nc.tensor.transpose(ps[:, b, c * P:(c + 1) * P], src[:, o:o + P], ident)
                mm.then_inc(*done("job_done", job))

        def pe_route(pe, st, t):
            job = ("route", st, t)
            b = open_job(pe, job)
            pe.wait_ge(*emptied(("turn", st, t, 1)))
            pe.wait_ge(sem("router_landed"), 16 * (st[1] + 1))
            for k in range(KD):
                mm = nc.tensor.matmul(ps[:, b, 0:EXPERTS], h2t[:, t % 2, k, :], wr[:, k, :], start=(k == 0),
                                      stop=(k == KD - 1))
            mm.then_inc(*done("job_done", job))

        def pe_affinities(pe, st, t):
            job = ("affT", st, t)
            b = open_job(pe, job)
            pe.wait_ge(*at("aff", (st, t)))
            nc.tensor.transpose(ps[0:EXPERTS, b, 0:P], aff[:, t, :], ident).then_inc(*done("job_done", job))

        def mixer_tiles(l):
            return [NT + t for t in range(NC)] * (l == 0) + list(range(NT))

        def staggered(tiles, steps):
            for i in range(len(tiles) + max(lag for _, lag in steps)):
                for step, lag in steps:
                    if 0 <= i - lag < len(tiles):
                        step(tiles[i - lag])

        def pe_out(pe, st, lhs, t, slots, first, last):
            for half in range(2):
                job = ("out", st, t, half)
                ws = [slot(pe, s) for s in slots[4 * half:4 * half + 4]] if first else [
                    ring[:, banks.get(("slot", s), (0, 16))[0], :].rearrange("p (k n) -> p k n", k=KD)
                    for s in slots[4 * half:4 * half + 4]]
                b = open_job(pe, job)
                tl = t - NT if ctile(t) else t
                for c in range(4):
                    for k in range(KD):
                        mm = nc.tensor.matmul(ps[:, b, c * P:(c + 1) * P], lhs[:, k, tl * P:(tl + 1) * P],
                                              ws[c][:, k, :], start=(k == 0), stop=(k == KD - 1))
                mm.then_inc(*done("job_done", job))
                if last:
                    for s in slots[4 * half:4 * half + 4]:
                        last_use(s, job)

        def pe_gate_rows(pe, l, which):
            for r in range(2 if l == 0 else 1):
                for half in range(2):
                    job = ("grow", l, which, r, half)
                    b = open_job(pe, job)
                    for c in range(4):
                        pe.wait_ge(*at(f"diag{which}", (l, which, r, 4 * half + c)))
                        mm = nc.tensor.matmul(ps[:, b, c * P:(c + 1) * P], cst(C_ONE),
                                              modrow_diag(4 * half + c), start=True, stop=True)
                        if c < 3:
                            mm.then_inc(*done("diag_used", (l, which, r, 4 * half + c)))
                    mm.then_inc(*done("job_done", job))

        diag = sb("diag", [P, 2, P])

        def modrow_diag(c):
            return diag[:, c % 2, :]

        def diag_free(l, which, r, c):
            if c % 4 < 3:
                return at("diag_used", (l, which, r, c))
            return at("job_done", ("grow", l, which, r, c // 4))

        def w1(l, name, c):
            return ("w1", l, name, c)

        def first_block_slots(l):
            out = [(w1(l, "gate", c), w_cols(a["w_in"], l, O_GATE + c * P)) for c in range(8)]
            for name, o in (("fq", O_FQ), ("fk", O_FK), ("fv", O_FV)):
                out += [(w1(l, name, c), w_cols(a["w_in"], l, o + c * P)) for c in range(2)]
            out.append("mod")
            for name, o in (("sq", O_SQ), ("sk", O_SK), ("sv", O_SV)):
                out += [(w1(l, name, c), w_cols(a["w_in"], l, o + c * P)) for c in range(2)]
            out.append("mod")
            out += [(w1(l, "ckv", 0), w_cols(a["w_in"], l, O_CKV))]
            out += [(w1(l, "cq", c), w_cols(a["w_in"], l, O_CQ + c * P)) for c in range(2)]
            out.append("mod")
            out += [(w1(l, "mq", c), w_cols(a["w_in"], l, O_MQ + c * P)) for c in range(2)]
            out += [(w1(l, "mk", c), w_cols(a["w_mem_kv"], l, c * P)) for c in range(2)]
            out += [(w1(l, "mv", c), w_cols(a["w_mem_kv"], l, 256 + c * P)) for c in range(2)]
            out.append("mod")
            out += [(w1(l, "wo", c), w_cols(a["w_out"], l, c * P)) for c in range(8)]
            return out

        def second_block_slots(l):
            def s(name, o, n):
                return [(w1(2 + l, name, c), w_cols(a["w_in_2"], l, o + c * P)) for c in range(n)]
            aq = s("aq", O_AQ, 4)
            return (s("ak", O_AK, 1) + aq[0:2] + s("a", O_C, 2) + s("g", O_C + 256, 2) + s("av", O_AV, 1)
                    + s("bk", O_BK, 2) + s("bv", O_BV, 2) + aq[2:4] + s("bq", O_BQ, 2)
                    + [(w1(2 + l, "wo", c), w_cols(a["w_out_2"], l, c * P)) for c in range(8)])

        def pe_first_block(pe, l):
            pe.wait_ge(*emptied(("turn", ("plain", l), NT - 1, 1)))
            for c in range(8):
                pe_t_job(pe, ("gate", l, c), w1(l, "gate", c), hT, SEQ)
            pe.wait_ge(sem("misc_landed"), 64 * (l + 1))
            job = ("misc", l)
            b = open_job(pe, job)
            for k in range(KD):
                mm = nc.tensor.matmul(ps[:, b, :], wmisc[:, k, :], hT[:, k, :], start=(k == 0), stop=(k == KD - 1))
            mm.then_inc(*done("job_done", job))
            for name in ("fq", "fk"):
                for c in range(2):
                    pe_t_job(pe, (name, l, c), w1(l, name, c), hT, SEQ)
            for c in range(2):
                pe_n_job(pe, ("fv", l, c), w1(l, "fv", c), hT, NT)
            pe.wait_ge(*emptied(("fk", l, 1)))
            pe.wait_ge(*emptied(("fv", l, 1)))
            pe.wait_ge(sem("fcum_landed"), 64 * (l + 1))
            pe.wait_ge(*at("fox_rows", l))
            pe_softmax(pe, ("fox", l, 0))
            pe_modulation(pe, 3)
            for name in ("sq", "sk"):
                for c in range(2):
                    pe_t_job(pe, (name, l, c), w1(l, name, c), hT, SEQ)
            for c in range(2):
                pe_n_job(pe, ("sv", l, c), w1(l, "sv", c), hT, NT)
            pe.wait_ge(*emptied(("sk", l, 1)))
            pe.wait_ge(*emptied(("sv", l, 1)))
            pe.wait_ge(*at("zero_rows", ("sb", l)))
            pe_stick(pe, l)
            pe_modulation(pe, 3)
            pe_t_job(pe, ("ckv", l, 0), w1(l, "ckv", 0), hT, SEQ)
            for c in range(2):
                pe_t_job(pe, ("cq", l, c), w1(l, "cq", c), hT, SEQ)
            job = ("kvsum", l)
            b = open_job(pe, job)
            pe.wait_ge(*at("squares", (l, 2)))
            nc.tensor.matmul(ps[:, b, :], cst(C_ONE), sqT[:, 2, :], start=True, stop=True).then_inc(*done("job_done", job))
            job = ("qsum", l)
            b = open_job(pe, job)
            pe.wait_ge(*at("squares", (l, 1)))
            for c in range(2):
                mm = nc.tensor.matmul(ps[:, b, :], cst(C_ONE), sqT[:, c, :], start=(c == 0), stop=(c == 1))
            mm.then_inc(*done("job_done", job))
            job = ("krr", l)
            b = open_job(pe, job)
            pe.wait_ge(*emptied(("misc", l)))
            nc.tensor.matmul(ps[0:KROWS, b, :], const[0:KROWS, C_ROTM:C_ROTM + KROWS], kr[0:KROWS, :], start=True,
                             stop=True).then_inc(*done("job_done", job))
            pe.wait_ge(*at("rms_ready", (l, "kv")))
            pe.wait_ge(sem("mla_landed"), 32 * (l + 1))
            for hh in range(HEADS):
                job = ("mk", l, hh)
                b = open_job(pe, job)
                nc.tensor.matmul(ps[0:HD, b, :], wkvup[:, hh * P:hh * P + HD], ckvT, start=True,
                                 stop=True).then_inc(*done("job_done", job))
            for half in range(2):
                job = ("mv", l, half)
                b = open_job(pe, job)
                for t in range(2):
                    o = (2 * half + t) * P
                    mm = nc.tensor.matmul(ps[:, b, t * 256:(t + 1) * 256], ckvT[:, o:o + P],
                                          wkvup[:, :].rearrange("p (h x) -> p h x", h=HEADS)[:, :, HD:2 * HD],
                                          start=True, stop=True)
                mm.then_inc(*done("job_done", job))
            pe.wait_ge(*at("rms_ready", (l, "q")))
            for hh in range(HEADS):
                job = ("mqu", l, hh)
                b = open_job(pe, job)
                for c in range(2):
                    mm = nc.tensor.matmul(ps[0:MLA_QK, b, :], wqup[:, c, hh * MLA_QK:(hh + 1) * MLA_QK], cqT[:, c, :],
                                          start=(c == 0), stop=(c == 1))
                mm.then_inc(*done("job_done", job))
            for hh in range(HEADS):
                job = ("mqr", l, hh)
                b = open_job(pe, job)
                pe.wait_ge(*emptied(("mqu", l, hh)))
                nc.tensor.matmul(ps[0:KROWS, b, :], const[0:KROWS, C_ROTM:C_ROTM + KROWS], qz[0:KROWS, hh, :],
                                 start=True, stop=True).then_inc(*done("job_done", job))
            pe.wait_ge(*at("kr_spread", l))
            pe.wait_ge(*at("mla_q", (l, HEADS - 1)))
            pe.wait_ge(*emptied(("mv", l, 1)))
            pe_softmax(pe, ("mla", l, 0))
            pe_modulation(pe, 3)
            for c in range(2):
                pe_t_job(pe, ("mq", l, c), w1(l, "mq", c), hT, SEQ)
            for c in range(2):
                pe_t_job(pe, ("memk", l, c), w1(l, "mk", c), hcT, CTX)
            for c in range(2):
                pe_n_job(pe, ("memv", l, c), w1(l, "mv", c), hcT, NC)
            pe.wait_ge(*emptied(("memk", l, 1)))
            pe.wait_ge(*emptied(("memv", l, 1)))
            pe.wait_ge(*at("zero_rows", ("mem", l)))
            pe_softmax(pe, ("mem", l, 0))
            pe_modulation(pe, 3)
            pe.wait_ge(*emptied(("pv", ("mem", l, 0), NT - 1, 1)))
            st = ("first", l)
            nxt = ("plain", l + 1) if l + 1 < DEPTH else ("pre", 0)
            for t in range(NT):
                pe_out(pe, st, mixT, t, [w1(l, "wo", c) for c in range(8)], t == 0, t == NT - 1)
                if t > 0:
                    pe_head(pe, nxt, t - 1)
            pe_head(pe, nxt, NT - 1)

        def pe_rope2(pe, l, name, c):
            job = ("rot", l, name, c)
            b = open_job(pe, job)
            pe.wait_ge(*emptied((name, l, c, 0)))
            nc.tensor.matmul(ps[:, b, :], cst(C_ROTA), rt1, start=True, stop=True).then_inc(*done("job_done", job))

        def streams(l, name):
            return (0, 1) if l == 0 or name in ("ak", "av", "bk", "bv") else (0,)

        def pe_conv_stats(pe, l, r):
            n = (SEQ, CTX)[r]
            for job, ready, src in ((("cmean", l, r), ("conv_done", (l, r)), acc), (("cvar", l, r), ("conv_sq", (l, r)), csq)):
                b = open_job(pe, job)
                pe.wait_ge(*at(*ready))
                for c in range(2):
                    mm = nc.tensor.matmul(ps[:, b, 0:n], cst(C_ONE), src[:, c, 0:n], start=(c == 0), stop=(c == 1))
                mm.then_inc(*done("job_done", job))

        def pe_second_block(pe, l):
            pe.wait_ge(*emptied(("turn", ("pre", l), NT + NC - 1, 1)))
            ht = (hT, hcT)
            def q_job(c):
                pe_t_job(pe, ("aq", l, c, 0), w1(2 + l, "aq", c), hT, SEQ, last=l > 0)
                pe_rope2(pe, l, "aq", c)
                if l == 0:
                    pe_t_job(pe, ("aq", l, c, 1), w1(2 + l, "aq", c), hcT, CTX)

            pe_t_job(pe, ("ak", l, 0, 0), w1(2 + l, "ak", 0), hT, SEQ, last=False)
            pe_rope2(pe, l, "ak", 0)
            pe_t_job(pe, ("ak", l, 0, 1), w1(2 + l, "ak", 0), hcT, CTX)
            for c in range(2):
                q_job(c)
            for r in streams(l, "a"):
                for name in ("a", "g"):
                    for c in range(2):
                        pe_t_job(pe, (name, l, c, r), w1(2 + l, name, c), ht[r], (SEQ, CTX)[r],
                                 last=r == streams(l, "a")[-1])
            for r in (0, 1):
                pe_n_job(pe, ("av", l, 0, r), w1(2 + l, "av", 0), ht[r], (NT, NC)[r], last=r == 1)
            for c in range(2):
                pe_t_job(pe, ("bk", l, c, 1), w1(2 + l, "bk", c), hcT, CTX, last=False)
            for c in range(2):
                pe_n_job(pe, ("bv", l, c, 1), w1(2 + l, "bv", c), hcT, NC, last=False)
            for part in range(2):
                if part == 1:
                    q_job(2)
                    q_job(3)
                if part == 0:
                    pe_conv_stats(pe, l, 0)
                    if l == 0:
                        pe_conv_stats(pe, l, 1)
                pe.wait_ge(*at("roped", (l, "aq", 2 * part + 1)))
                pe.wait_ge(*at("zero_rows", ("second", l)))
                if l == 0:
                    pe.wait_ge(*emptied(("aq", l, 2 * part + 1, 1)))
                pe.wait_ge(*emptied(("bv", l, 1, 1)))
                pe_softmax(pe, ("wa", l, part))
                if l == 0:
                    pe_softmax(pe, ("ca", l, part))
            for c in range(2):
                pe_t_job(pe, ("bk", l, c, 0), w1(2 + l, "bk", c), hT, SEQ)
            for c in range(2):
                pe_n_job(pe, ("bv", l, c, 0), w1(2 + l, "bv", c), hT, NT)
            for c in range(2):
                for r in streams(l, "bq"):
                    pe_t_job(pe, ("bq", l, c, r), w1(2 + l, "bq", c), ht[r], (SEQ, CTX)[r], last=r == streams(l, "bq")[-1])
            pe.wait_ge(*emptied(("bq", l, 1, streams(l, "bq")[-1])))
            pe_softmax_by_head(pe, l)
            if l == 0:
                pe_softmax(pe, ("cb", l, 0))
            pe_gate_rows(pe, l, 0)
            pe.wait_ge(*at("conv_out", (l, streams(l, "a")[-1])))
            lastu = ("cb", l, 0) if l == 0 else ("nb", l, 0)
            pe.wait_ge(*emptied(("pv", lastu, (NC if l == 0 else NT) - 1, 1)))
            st = ("mixer", l)
            tiles = list(range(NT + NC)) if l == 0 else list(range(NT))
            job_ring.extend(range(6))
            tiles = mixer_tiles(l)
            rt = ("route", l)
            staggered(tiles, [
                (lambda t: pe_out(pe, st, mixcT if ctile(t) else mixT, t, [w1(2 + l, "wo", c) for c in range(8)],
                                  t == tiles[0], t == tiles[-1]), 0),
                (lambda t: pe_head(pe, rt, t), 1),
                (lambda t: pe_route(pe, rt, t), 2),
                (lambda t: pe_affinities(pe, rt, t), 3)])
            pe_gate_rows(pe, l, 1)
            job = ("topT", l)
            b = open_job(pe, job)
            job_ring[:] = [6, 7]
            rows = CAP + (CAP_C if l == 0 else 0)
            pe.wait_ge(*at("topk", l))
            nc.tensor.transpose(ps[0:rows, b, 0:EXPERTS], topv[:, 0:rows], ident[0:EXPERTS, 0:EXPERTS])
            nc.tensor.transpose(ps[0:rows, b, EXPERTS:2 * EXPERTS], topf[:, 0:rows],
                                ident[0:EXPERTS, 0:EXPERTS]).then_inc(*done("job_done", job))
            pe_experts(pe, l)

        def pe_softmax_by_head(pe, l):
            pe_softmax(pe, ("nb", l, 0))

        ROUNDS = EXPERTS // 2

        def at_round(name, event, i, back=0):
            per = known.get(("per_round", event[0], name), 1)
            return sem(name), i * per + max(known.get((name, event), 1) - back * per, -back * per + 1)

        def slot_count(s, l, n, i):
            return i * 64 + (banks.get(("moe_slot", l, s), 0) + 16 * (n + 1))

        def rounds(eng, l, body):
            before = dict(counts)
            body(0)
            per = {k: counts[k] - before.get(k, 0) for k in counts if counts[k] != before.get(k, 0)}
            frozen[0] = True
            with eng.Fori(1, ROUNDS) as i:
                body(i)
            frozen[0] = False
            for k, n in per.items():
                marks[("per_round", l, k)] = n
                counts[k] = before.get(k, 0) + ROUNDS * n

        def settled(eng, count):
            return count if first_round(count) else eng.compute_val(count)

        def first_round(i):
            return isinstance(i, int)

        def pe_experts(pe, l):
            rows = CAP + (CAP_C if l == 0 else 0)
            G, U, GC, UC, Y, YC = 2, 3, 4, 5, 6, 7

            def turn_xs(i, u, event):
                for hb in range(2):
                    for c in range(4):
                        mm = nc.tensor.transpose(ps[:, hb, c * 96:c * 96 + rows],
                                                 xs[0:rows, (u + 1) % 2, (4 * hb + c) * P:(4 * hb + c + 1) * P],
                                                 ident[0:rows, 0:rows])
                    mm.then_inc(*done("xs_turned", (l, event, hb)))

            def product(i, u, m, lhs, dst, dstc, last_event):
                for k in range(KD):
                    pos = (24 * u + 8 * m + k)
                    s = pos % RING
                    pe.wait_ge(sem(f"slot{s}"), slot_count(s, l, pos // RING, i))
                    w = ring[:, s, :]
                    for half in range(2):
                        mm = nc.tensor.matmul(ps[64 * half:64 * half + 64, dst, :], lhs[:, k, 0:CAP],
                                              w[:, half * 512:(half + 1) * 512], start=(k == 0), stop=(k == KD - 1),
                                              skip_group_check=True)
                    if l == 0:
                        for q in range(4):
                            mm = nc.tensor.matmul(ps[32 * q:32 * q + 32, dstc, 0:256], lhs[:, k, CAP:CAP + CAP_C],
                                                  w[:, q * 256:(q + 1) * 256], start=(k == 0), stop=(k == KD - 1),
                                                  skip_group_check=True)
                    mm.then_inc(*done("moe_k", (l, u, m, k)))

            pe.wait_ge(*emptied(("topT", l)))
            pe.wait_ge(*emptied(("grow", l, 1, 1 if l == 0 else 0, 1)))
            pe.wait_ge(sem("gathered0"), known.get(("gather", l, 0), 16))
            turn_xs(0, -1, "first")

            def body(i):
                for u in range(2):
                    b = u
                    if u == 0:
                        if first_round(i):
                            pe.wait_ge(*at("xsT_act", (l, "first")))
                            pe.wait_ge(*at("xsT_dve", (l, "first")))
                        else:
                            pe.wait_ge(*at_round("xsT_act", (l, 1), i, 1))
                            pe.wait_ge(*at_round("xsT_dve", (l, 1), i, 1))
                    else:
                        pe.wait_ge(*at_round("xsT_act", (l, 0), i))
                        pe.wait_ge(*at_round("xsT_dve", (l, 0), i))
                    product(i, u, 0, xsT[:, b, :, :], G, GC, None)
                    product(i, u, 1, xsT[:, b, :, :], U, UC, None)
                    count = settled(pe, gather_count(l, u, i))
                    pe.wait_ge(*emptied(("topT", l)))
                    pe.wait_ge(sem(f"gathered{(u + 1) % 2}"), count)
                    turn_xs(i, u, u)
                    pe.wait_ge(*at_round("hid", (l, u, 0), i))
                    for c in range(4):
                        mm = nc.tensor.transpose(ps[:, G, c * P:(c + 1) * P], hid[:, c * P:(c + 1) * P], ident)
                    mm.then_inc(*done("hid_turned", (l, u, 0)))
                    if l == 0:
                        pe.wait_ge(*at_round("hid", (l, u, 1), i))
                        for c in range(2):
                            mm = nc.tensor.transpose(ps[:, GC, c * P:(c + 1) * P], hidc[:, c * P:(c + 1) * P], ident)
                        mm.then_inc(*done("hid_turned", (l, u, 1)))
                    pe.wait_ge(*at_round("hidT", (l, u), i))
                    if not (first_round(i) and u == 0):
                        pe.wait_ge(*at_round("ye_copied", (l, 1 - u), i, 1 - u))
                    product(i, u, 2, hidT, Y, YC, None)

            rounds(pe, l, body)

        def gather_count(l, u, i):
            return i * 16 + (known.get(("gather", l, 1 - u), 16) + 16 * u)

        def experts_act(act, l):
            rows = CAP + (CAP_C if l == 0 else 0)
            G, U, GC, UC, Y, YC = 2, 3, 4, 5, 6, 7

            def mod_cols(c, r):
                return (modc[:, l, 32 + c, r:r + 1], modc[:, l, 24 + c, r:r + 1])

            def modulate(i, u, event):
                for c in range(4):
                    for r in range(2 if l == 0 else 1):
                        o, n = ((0, CAP), (CAP, CAP_C))[r]
                        sc, sh = mod_cols(c, r)
                        ins = nc.scalar.activation(xsT[:, (u + 1) % 2, c, o:o + n], ps[:, 0, c * 96 + o:c * 96 + o + n],
                                                   ACT.Identity, bias=sh, scale=sc)
                ins.then_inc(*done("xsT_act", (l, event)))

            act.wait_ge(*at("xs_turned", (l, "first", 0)))
            modulate(0, -1, "first")

            def body(i):
                for u in range(2):
                    act.wait_ge(*at_round("moe_k", (l, u, 0, KD - 1), i))
                    if not (first_round(i) and u == 0):
                        act.wait_ge(*at_round("hid", (l, 1 - u, 1 if l == 0 else 0), i, 1 - u))
                    nc.scalar.activation(sig, ps[:, G, :], ACT.Silu).then_inc(*done("gated", (l, u, 0)))
                    if l == 0:
                        nc.scalar.activation(sigc, ps[:, GC, 0:256], ACT.Silu).then_inc(*done("gated", (l, u, 1)))
                    act.wait_ge(*at_round("xs_turned", (l, u, 0), i))
                    modulate(i, u, u)
                    act.wait_ge(*at_round("moe_k", (l, u, 2, KD - 1), i))
                    if not first_round(i):
                        act.wait_ge(sem("scattered"), scatter_count(l, u, i, 1))
                    elif l > 0:
                        act.wait_ge(sem("scattered"), known.get(("scatter_base", l), 0))
                    for half in range(2):
                        ins = nc.scalar.activation(ye[0:CAP, u, half * 512:(half + 1) * 512],
                                                   ps[64 * half:64 * half + 64, Y, :], ACT.Copy)
                    if l == 0:
                        for q in range(4):
                            ins = nc.scalar.activation(ye[CAP:rows, u, q * 256:(q + 1) * 256],
                                                       ps[32 * q:32 * q + 32, YC, 0:256], ACT.Copy)
                    ins.then_inc(*done("ye_copied", (l, u)))

            rounds(act, l, body)

        def scatter_count(l, u, i, back=0):
            return i * 32 + (known.get(("scatter_base", l), 0) + 16 * (u + 1) - 32 * back)

        def experts_dve(dve, l):
            rows = CAP + (CAP_C if l == 0 else 0)
            G, U, GC, UC, Y, YC = 2, 3, 4, 5, 6, 7

            def modulate(i, u, event):
                for c in range(4, 8):
                    for r in range(2 if l == 0 else 1):
                        o, n = ((0, CAP), (CAP, CAP_C))[r]
                        ins = nc.vector.tensor_scalar(xsT[:, (u + 1) % 2, c, o:o + n],
                                                      ps[:, 1, (c - 4) * 96 + o:(c - 4) * 96 + o + n],
                                                      modc[:, l, 32 + c, r:r + 1], modc[:, l, 24 + c, r:r + 1],
                                                      ALU.mult, ALU.add)
                ins.then_inc(*done("xsT_dve", (l, event)))

            dve.wait_ge(*at("xs_turned", (l, "first", 1)))
            modulate(0, -1, "first")

            def body(i):
                for u in range(2):
                    dve.wait_ge(*at_round("moe_k", (l, u, 1, KD - 1), i))
                    dve.wait_ge(*at_round("gated", (l, u, 0), i))
                    nc.vector.tensor_tensor(hid, sig, ps[:, U, :], ALU.mult).then_inc(*done("hid", (l, u, 0)))
                    if l == 0:
                        dve.wait_ge(*at_round("gated", (l, u, 1), i))
                        nc.vector.tensor_tensor(hidc, sigc, ps[:, UC, 0:256], ALU.mult).then_inc(*done("hid", (l, u, 1)))
                    dve.wait_ge(*at_round("hid_turned", (l, u, 0), i))
                    dst = hidT.rearrange("p (a j) t -> p j a t", a=2)[:, :, :, 0:CAP]
                    src = ps[:, G, :].rearrange("p (j a t) -> p j a t", j=4, a=2)
                    ins = nc.vector.tensor_copy(dst, src)
                    if l == 0:
                        dve.wait_ge(*at_round("hid_turned", (l, u, 1), i))
                        dst = hidT.rearrange("p (a j) t -> p j a t", a=4)[:, :, :, CAP:CAP + CAP_C]
                        src = ps[:, GC, 0:256].rearrange("p (j a t) -> p j a t", j=2, a=4)
                        ins = nc.vector.tensor_copy(dst, src)
                    ins.then_inc(*done("hidT", (l, u)))
                    dve.wait_ge(*at_round("xs_turned", (l, u, 1), i))
                    modulate(i, u, u)
                    dve.wait_ge(*at_round("ye_copied", (l, u), i))
                    e = 2 * i + u
                    g = gates[0:rows, e:e + 1] if first_round(i) else gates[0:rows, bass.ds(e, 1)]
                    nc.vector.tensor_scalar(ye[0:rows, u, :], ye[0:rows, u, :], g, None,
                                            ALU.mult).then_inc(*done("ye", (l, u)))

            rounds(dve, l, body)

        def experts_pool(pool, l):
            rows = CAP + (CAP_C if l == 0 else 0)
            src = a["x_norm"][l]
            dst = a["y_moe"][l]

            def gather(event, e, b):
                col_e = idx[0:rows, e:e + 1] if first_round(e) else idx[0:rows, bass.ds(e, 1)]
                nc.gpsimd.tensor_copy(idx_at[b][0:rows, :], col_e).then_inc(*done("idx_at", (l, event)))

            def start(b, w):
                count = settled(pool, w[1])
                pool.wait_ge(*at("idx", l))
                pool.wait_ge(w[0], count)
                nc.gpsimd.indirect_dma_start(
                    out=xs[0:rows, b, :], out_offset=None, in_=src,
                    in_offset=bass.IndirectOffsetOnAxis(ap=idx_at[b][0:rows, 0:1], axis=0)).then_inc(sem(f"gathered{b}"), 16)

            pool.wait_ge(*at("idx", l))
            pool.wait_ge(*at_last_store(l))
            for b in range(2):
                gather(("first", b), b, b)
                start(b, at("idx_at", (l, ("first", b))))
                base = counts.get(f"gathers{b}", 0)
                marks[("gather", l, b)] = base + 16
                counts[f"gathers{b}"] = base + 16 + 16 * ROUNDS
            marks[("scatter_base", l)] = l * 16 * EXPERTS

            def body(i):
                for u in range(2):
                    e = 2 * i + u
                    if u == 1:
                        pool.wait_ge(*at_round("xs_turned", (l, 0, 1), i))
                    elif first_round(i):
                        pool.wait_ge(*at("xs_turned", (l, "first", 1)))
                    else:
                        pool.wait_ge(*at_round("xs_turned", (l, 1, 1), i, 1))
                    gather(u, e + 2, u)
                    start(u, at_round("idx_at", (l, u), i))
                    if not (first_round(i) and u == 0):
                        pool.wait_ge(sem("scattered"), scatter_count(l, 1 - u, i, 1 - u))
                    col_e = idx[0:rows, e:e + 1] if first_round(e) else idx[0:rows, bass.ds(e, 1)]
                    nc.gpsimd.tensor_copy(idx_to[u][0:rows, :], col_e).then_inc(*done("idx_to", (l, u)))
                    scaled, count = at_round("ye", (l, u), i)
                    count = settled(pool, count)
                    copied, count_to = at_round("idx_to", (l, u), i)
                    count_to = settled(pool, count_to)
                    pool.wait_ge(sem("y_zeroed"), 16 * sum(map(tiles_of, range(DEPTH))))
                    pool.wait_ge(copied, count_to)
                    pool.wait_ge(scaled, count)
                    nc.gpsimd.indirect_dma_start(
                        out=dst, out_offset=bass.IndirectOffsetOnAxis(ap=idx_to[u][0:rows, 0:1], axis=0),
                        in_=ye[0:rows, u, :], in_offset=None, compute_op=ALU.add).then_inc(sem("scattered"), 16)

            rounds(pool, l, body)

        def at_last_store(l):
            return sem("x_norm_stored"), known.get(("x_norm_stored_all", l), 16)

        def dve_norm(dve, event, src, dst, rows=None, final=None):
            k = ln_count[0] % 2
            ln_count[0] += 1
            st = col[:, 16 + 12 * k:28 + 12 * k].rearrange("p (c s) -> p c s", c=2)
            mv = col[:, 40 + 2 * k:42 + 2 * k]
            rstd = col[:, 46 + k:47 + k]
            for c in range(2):
                ins = nc.vector.bn_stats(st[:, c, :], src[:, c * 512:(c + 1) * 512])
            ins.then_inc(*done("dve_step", ("st", event)))
            dve.wait_ge(*at("dve_step", ("st", event)))
            nc.vector.bn_aggr(mv, col[:, 16 + 12 * k:28 + 12 * k]).then_inc(*done("variance", event))
            if rows is not None:
                dve.wait_ge(*at("variance", event))
                nc.vector.scalar_tensor_tensor(dst, src, mv[:, 0:1], rows[0], ALU.subtract, ALU.mult)
            dve.wait_ge(*at("deviation", event))
            nc.vector.reciprocal(rstd, col[:, 44 + k:45 + k]).then_inc(*done("dve_step", ("ri", event)))
            dve.wait_ge(*at("dve_step", ("ri", event)))
            if rows is not None:
                ins = nc.vector.scalar_tensor_tensor(dst, dst, rstd, rows[1], ALU.mult, ALU.add)
            else:
                ins = nc.vector.tensor_scalar(dst, src, mv[:, 0:1], rstd, ALU.subtract, ALU.mult)
            ins.then_inc(*done(*(final or ("dve_step", ("b", event)))))

        ln_count = [0]
        ln_count_act = [0]

        def act_root(act, event, eps):
            k = ln_count_act[0] % 2
            ln_count_act[0] += 1
            act.wait_ge(*at("variance", event))
            nc.scalar.activation(col[:, 44 + k:45 + k], col[:, 41 + 2 * k:42 + 2 * k], ACT.Sqrt,
                                 bias=epsc(eps)).then_inc(*done("deviation", event))

        def epsc(eps):
            return {LN_EPS: col[:, 50:51], LN_EPS_2: col[:, 51:52]}[eps]

        def rows_of(stage):
            return lnrow[:, 0, :], lnrow[:, 1, :]

        def dve_out(dve, st, t):
            kind, l = st
            for half in range(2):
                o = slice(half * 512, half * 512 + 512)
                job = ("out", st, t, half)
                dve.wait_ge(*at("job_done", job))
                src = ps[:, bank_of(job), :]
                if kind == "first":
                    nc.vector.scalar_tensor_tensor(res(t)[:, o], res(t)[:, o], ALPHA, src, ALU.mult,
                                                   ALU.add).then_inc(*done("evac_dve", job))
                else:
                    dve_gated(dve, job, t, o, src, l)
            if t == (0 if kind == "first" else mixer_tiles(l)[0]):
                dve.wait_ge(sem("rows_landed"), rows_landed(st))
            if kind == "first":
                dve.wait_ge(*at("evac_dve", ("out", st, t, 1)))
            else:
                dve.wait_ge(*at("dve_step", ("res", st, t, 1)))

        def dve_gated(dve, job, t, o, src, l):
            if job[3] == 1:
                dve.wait_ge(*at("dve_step", ("res", job[1], t, 0)))
            elif t != mixer_tiles(l)[0]:
                dve.wait_ge(*at("dve_step", ("res", job[1], mixer_tiles(l)[mixer_tiles(l).index(t) - 1], 1)))
            r = 1 if ctile(t) else 0
            if t == mixer_tiles(l)[0] and job[3] == 0:
                rr = 1 if l == 0 else 0
                dve.wait_ge(*emptied(("grow", l, 0, rr, 1)))
            nc.vector.tensor_tensor(rot_t[:, :], grow[:, r, o], src, ALU.mult).then_inc(*done("evac_dve", job))
            dve.wait_ge(*at("evac_dve", job))
            nc.vector.scalar_tensor_tensor(res(t)[:, o], res(t)[:, o], ALPHA, rot_t[:, :], ALU.mult,
                                           ALU.add).then_inc(*done("dve_step", ("res", job[1], t, job[3])))

        row_loads = []

        def rows_landed(st):
            return known.get(("rows_landed", st), 32)

        def dve_head(dve, st, t):
            kind, l = st
            if kind == "plain":
                return
            seen = xt_users[0]
            if len(seen) >= 2:
                pst, pt = seen[-2]
                dve.wait_ge(*at("job_done", ("turn", pst, pt, 1)))
                if pst[0] == "route":
                    dve.wait_ge(sem("x_norm_stored"), known.get(("x_norm_stored", pst, pt), 16))
            seen.append((st, t))
            dve_norm(dve, (st, t), res(t), xt[:, t % 2, :], final=("tile_ready", (st, t)))

        xt_users = [[]]

        def act_head(act, st, t, root=True):
            kind, l = st
            if kind != "plain" and root:
                act_root(act, (st, t), LN_EPS_2)
            for half in range(2):
                job = ("turn", st, t, half)
                act.wait_ge(*at("job_done", job))
                src = ps[:, bank_of(job), :].rearrange("p (c t) -> p c t", c=4)
                tl = t - NT if ctile(t) else t
                ts = slice(tl * P, (tl + 1) * P)
                if kind == "plain" or kind == "memory":
                    dst = hcT if ctile(t) else hT
                    ins = nc.scalar.activation(dst[:, 4 * half:4 * half + 4, ts], src, ACT.Copy)
                else:
                    if half == 0 and (t == 0 or kind == "route" and t == mixer_tiles(l)[0]):
                        act.wait_ge(*at("modulation", (l, 9)))
                        act.wait_ge(*at("evac_dve", ("modT", l, 11)))
                    r = 1 if ctile(t) else 0
                    o = 0 if kind == "pre" else 24
                    for c in range(4):
                        cc = 4 * half + c
                        if kind == "pre":
                            dst = (hcT if ctile(t) else hT)[:, cc, ts]
                        else:
                            dst = h2t[:, t % 2, cc, :]
                        ins = nc.scalar.activation(dst, src[:, c, :], ACT.Identity, bias=modc[:, l, o + cc, r:r + 1],
                                                   scale=modc[:, l, o + 8 + cc, r:r + 1])
                ins.then_inc(*done("evac_act", job))

        def act_route(act, st, t):
            job = ("route", st, t)
            act.wait_ge(*at("job_done", job))
            act.wait_ge(*at("route_max", (st, t)))
            nc.scalar.activation(aff[:, t, :], ps[:, bank_of(job), 0:EXPERTS], ACT.Exp, bias=col[:, 10 + t % 2:11 + t % 2],
                                 accum_out=col[:, 12 + t % 2:13 + t % 2]).then_inc(*done("evac_act", job))

        def act_affinities(act, st, t):
            job = ("affT", st, t)
            act.wait_ge(*at("job_done", job))
            nc.scalar.activation(affT[:, t * P:(t + 1) * P], ps[0:EXPERTS, bank_of(job), 0:P],
                                 ACT.Copy).then_inc(*done("evac_act", job))

        def dve_route(dve, st, t):
            job = ("route", st, t)
            dve.wait_ge(*at("job_done", job))
            nc.vector.tensor_reduce(col[:, 10 + t % 2:11 + t % 2], ps[:, bank_of(job), 0:EXPERTS], AX, ALU.max,
                                    negate=True).then_inc(*done("route_max", (st, t)))
            dve.wait_ge(*at("evac_act", job))
            nc.vector.reciprocal(col[:, 14 + t % 2:15 + t % 2],
                                 col[:, 12 + t % 2:13 + t % 2]).then_inc(*done("dve_step", ("rr", st, t)))
            dve.wait_ge(*at("dve_step", ("rr", st, t)))
            nc.vector.tensor_scalar(aff[:, t, :], aff[:, t, :], col[:, 14 + t % 2:15 + t % 2], None,
                                    ALU.mult).then_inc(*done("aff", (st, t)))

        def dve_topk(dve, l, r):
            o, n, s0, cap = ((0, SEQ, 0, CAP), (SEQ, CTX, CAP, CAP_C))[r]
            dve.wait_ge(*at("evac_act", ("affT", ("route", l), (NT, NT + NC)[r] - 1)))
            cur = affT[:, o:o + n]
            for g in range(cap // 8):
                s = slice(s0 + 8 * g, s0 + 8 * g + 8)
                nc.vector.max(topv[:, s], cur).then_inc(*done("dve_step", ("mx", l, r, g)))
                dve.wait_ge(*at("dve_step", ("mx", l, r, g)))
                nc.vector.max_index(topi[:, s], topv[:, s], cur).then_inc(*done("dve_step", ("mi", l, r, g)))
                if g + 1 < cap // 8:
                    dve.wait_ge(*at("dve_step", ("mi", l, r, g)))
                    nc.vector.match_replace(cur, topv[:, s], cur, -1.0).then_inc(*done("dve_step", ("mr", l, r, g)))
                    dve.wait_ge(*at("dve_step", ("mr", l, r, g)))

        def dve_slots(dve, l):
            for r in streams(l, "a"):
                dve.wait_ge(*at("dve_step", ("mi", l, r, (CAP, CAP_C)[r] // 8 - 1)))
            ins = nc.vector.tensor_copy(topf[:, 0:CAP], topi[:, 0:CAP])
            if l == 0:
                ins = nc.vector.tensor_scalar(topf[:, CAP:CAP + CAP_C], topi[:, CAP:CAP + CAP_C], float(SEQ), None, ALU.add)
            ins.then_inc(*done("topk", l))
            job = ("topT", l)
            rows = CAP + (CAP_C if l == 0 else 0)
            b = bank_of(job)
            dve.wait_ge(*at("job_done", job))
            nc.vector.tensor_copy(gates[0:rows, 0:EXPERTS], ps[0:rows, b, 0:EXPERTS])
            nc.vector.tensor_copy(idxf[0:rows, 0:EXPERTS],
                                  ps[0:rows, b, EXPERTS:2 * EXPERTS]).then_inc(*done("evac_dve", job))
            dve.wait_ge(*at("evac_dve", job))
            nc.vector.tensor_copy(idx[0:rows, 0:EXPERTS], idxf[0:rows, 0:EXPERTS])
            nc.vector.tensor_copy(idx[0:rows, EXPERTS:EXPERTS + 2], idxf[0:rows, 0:2]).then_inc(*done("idx", l))

        def dve_moe_out(dve, l):
            st = ("experts", l)
            tiles = list(range(NT + NC)) if l == 0 else list(range(NT))
            for t in tiles:
                r = 1 if ctile(t) else 0
                y = ysbc[:, t - NT, :] if ctile(t) else ysb[:, t, :]
                dve.wait_ge(sem("y_landed"), known.get(("y_landed", l, t), 16))
                if t == 0:
                    dve.wait_ge(*emptied(("grow", l, 1, 1 if l == 0 else 0, 1)))
                    dve.wait_ge(sem("rows_landed"), rows_landed(st))
                nc.vector.tensor_tensor(y, y, grow[:, r, :], ALU.mult).then_inc(*done("dve_step", ("gy", l, t)))
                dve.wait_ge(*at("dve_step", ("gy", l, t)))
                nc.vector.scalar_tensor_tensor(res(t), res(t), ALPHA, y, ALU.mult,
                                               ALU.add).then_inc(*done("dve_step", ("ry", l, t)))
                dve.wait_ge(*at("dve_step", ("ry", l, t)))
                last = l == DEPTH - 1
                dve_norm(dve, (st, t), res(t), res(t), rows_of(st),
                         final=("out_ready", t) if last else ("dve_step", ("b", (st, t))))
                if not last:
                    dve.wait_ge(*at("dve_step", ("b", (st, t))))
                    dve_head(dve, ("pre", l + 1), t)

        def act_moe_out(act, l):
            st = ("experts", l)
            tiles = list(range(NT + NC)) if l == 0 else list(range(NT))
            for t in tiles:
                act_root(act, (st, t), LN_EPS_2)
                if l < DEPTH - 1:
                    act_head(act, ("pre", l + 1), t)

        def dve_softmax(dve, ph, scale_mix):
            us = units_of(ph)

            def top(u):
                dve.wait_ge(*at("scores", u))
                if seq[u] >= UC:
                    dve.wait_ge(*at("probs", by_seq[seq[u] - UC]))
                if not has_sink(u):
                    nc.vector.tensor_reduce(nmax(u), s_psum(u), AX, ALU.max, negate=True).then_inc(*done("nmax", u))
                else:
                    nc.vector.tensor_reduce(rmax(u), s_psum(u), AX, ALU.max).then_inc(*done("dve_step", ("mx", u)))
                    dve.wait_ge(*at("dve_step", ("mx", u)))
                    nc.vector.tensor_scalar(nmax(u), rmax(u), sink_col(u), -1.0, ALU.max,
                                            ALU.mult).then_inc(*done("nmax", u))

            def norm(u):
                dve.wait_ge(*at("probs", u))
                total = rsum(u)
                if has_sink(u):
                    dve.wait_ge(*at("sink_exp", u))
                    nc.vector.tensor_tensor(rmax(u), rsum(u), esink(u), ALU.add).then_inc(*done("dve_step", ("su", u)))
                    dve.wait_ge(*at("dve_step", ("su", u)))
                    total = rmax(u)
                nc.vector.reciprocal(rinv(u), total).then_inc(*done("dve_step", ("ri", u)))
                dve.wait_ge(*at("dve_step", ("ri", u)))
                p = p_sbuf(u)
                nc.vector.tensor_scalar(p, p, rinv(u), None, ALU.mult).then_inc(*done("probs_normed", u))

            def leave(u):
                job = pair_job(u)
                dve.wait_ge(*at("job_done", job))
                src = ps[:, bank_of(job), 0:P]
                dst = mix_out(u)
                if scale_mix:
                    ins = nc.vector.tensor_tensor(dst, dst, src, ALU.mult)
                else:
                    ins = nc.vector.tensor_copy(dst, src)
                ins.then_inc(*done("evac_dve", job))

            lag = lag_of(ph)
            for i in range(len(us) + lag + 2):
                if i < len(us):
                    top(us[i])
                if 1 <= i <= len(us):
                    norm(us[i - 1])
                if i >= lag + 2 and us[i - lag - 2][2] % 2:
                    leave(us[i - lag - 2])

        def act_softmax(act, ph):
            us = units_of(ph)

            def expo(u):
                n = seq[u]
                act.wait_ge(*at("nmax", u))
                w = before(u, probs_span)
                if w is not None:
                    act.wait_ge(*at("turned", (w, len(chunks_of(w)) - 1)))
                nc.scalar.activation(p_sbuf(u), s_psum(u), ACT.Exp, bias=nmax(u),
                                     accum_out=rsum(u)).then_inc(*done("probs", u))
                if has_sink(u):
                    nc.scalar.activation(esink(u), sink_col(u), ACT.Exp, bias=nmax(u)).then_inc(*done("sink_exp", u))

            def copy(u):
                n = seq[u]
                for c, blocks in enumerate(chunks_of(u)):
                    act.wait_ge(*at("turned", (u, c)))
                    if c == 0 and n >= 2:
                        w = by_seq[n - 2]
                        act.wait_ge(*at("job_done", pair_job(w if w[2] % 2 else (w[0], w[1], w[2] + 1))))
                    m = turn_at[(u, c)]
                    nc.scalar.activation(probsT[:, n % 2, blocks[0]:blocks[-1] + 1, :],
                                         ps[:, 4 + m % 2, 0:len(blocks) * P].rearrange("p (b q) -> p b q", q=P),
                                         ACT.Copy).then_inc(*done("probsT_ready", (u, c)))

            lag = lag_of(ph)
            for i in range(len(us) + lag):
                if i >= lag:
                    copy(us[i - lag])
                if i < len(us):
                    expo(us[i])

        def act_heads(act, name, l, c, r, dst, scale=1.0, heads=True):
            job = (name, l, c, r) if r is not None else (name, l, c)
            n = CTX if r == 1 or name == "memk" else SEQ
            act.wait_ge(*at("job_done", job))
            for e in range(2):
                ins = nc.scalar.activation(dst[0:HD, 2 * (c % 2) + e, 0:n], ps[e * HD:(e + 1) * HD, bank_of(job), 0:n],
                                           ACT.Copy, scale=scale)
            ins.then_inc(*done("evac_act", job))

        def act_values(act, job, dst, tiles):
            act.wait_ge(*at("job_done", job))
            nc.scalar.activation(dst, ps[:, bank_of(job), 0:tiles * P].rearrange("p (t n) -> p t n", t=tiles),
                                 ACT.Copy).then_inc(*done("evac_act", job))

        mod_act = iter(mod_order)
        mod_dve = iter(mod_order)

        def act_modulation(act, n):
            for _ in range(n):
                l, j = next(mod_act)
                job = ("mod", l, j)
                act.wait_ge(*at("job_done", job))
                nc.scalar.activation(modrow[:, :], ps[:, bank_of(job), 0:P], ACT.Copy).then_inc(*done("evac_act", job))

        def dve_modulation(dve, n):
            for _ in range(n):
                l, j = next(mod_dve)
                job = ("modT", l, j)
                dve.wait_ge(*at("job_done", job))
                src = ps[:, bank_of(job), 0:P].rearrange("p (q x) -> p q x", q=4)
                for r in range(2):
                    o = V_BMOD + 48 * l + 4 * j
                    dst = modc[:, l, 4 * j:4 * j + 4, r]
                    ins = nc.vector.tensor_tensor(dst, src[:, :, r], vec[:, o:o + 4], ALU.add)
                ins.then_inc(*done("evac_dve", job))
                dve.wait_ge(*at("evac_dve", job))
                if j // 2 in (1, 4):
                    nc.vector.tensor_scalar(modc[:, l, 4 * j:4 * j + 4, :], modc[:, l, 4 * j:4 * j + 4, :], 1.0, None,
                                            ALU.add).then_inc(*done("modulation", (l, j)))

        def gate_diagonals(eng, engine, l, which):
            for r in range(2 if l == 0 else 1):
                for c in range(8):
                    if c >= 2:
                        eng.wait_ge(*diag_free(l, which, r, c - 2))
                    elif r > 0:
                        eng.wait_ge(*diag_free(l, which, r - 1, 6 + c))
                    g = modc[:, l, (16, 40)[which] + c, r:r + 1]
                    engine.tensor_scalar(modrow_diag(c), ident, g, None, ALU.mult).then_inc(*done(f"diag{which}", (l, which, r, c)))

        def act_gate_rows(act, l, which):
            for r in range(2 if l == 0 else 1):
                for half in range(2):
                    job = ("grow", l, which, r, half)
                    act.wait_ge(*at("job_done", job))
                    nc.scalar.activation(grow[:, r, half * 512:(half + 1) * 512], ps[:, bank_of(job), :],
                                         ACT.Copy).then_inc(*done("evac_act", job))

        def act_first_block(act, l):
            for c in range(8):
                job = ("gate", l, c)
                act.wait_ge(*at("job_done", job))
                nc.scalar.activation(mixT[:, c, :], ps[:, bank_of(job), :], ACT.Silu).then_inc(*done("evac_act", job))
            nc.scalar.preload_act_table_set("natural_log_exp_and_others")
            job = ("misc", l)
            b = bank_of(job)
            act.wait_ge(*at("job_done", job))
            nc.scalar.activation(flog[0:HEADS, :], ps[0:HEADS, b, :], ACT.Identity,
                                 bias=vec[0:HEADS, V_BF + l:V_BF + l + 1]).then_inc(*done("f_logit", l))
            nc.scalar.activation(kr[HD:KROWS, :], ps[HD:KROWS, b, :], ACT.Copy).then_inc(*done("evac_act", job))
            act.wait_ge(*at("f_logit", l))
            nc.scalar.activation(fls[0:HEADS, 0, :], flog[0:HEADS, :], ACT.Abs).then_inc(*done("act_step", ("f0", l)))
            act.wait_ge(*at("act_step", ("f0", l)))
            nc.scalar.activation(fls[0:HEADS, 0, :], fls[0:HEADS, 0, :], ACT.Exp, scale=-1.0).then_inc(*done("act_step", ("f1", l)))
            act.wait_ge(*at("act_step", ("f1", l)))
            nc.scalar.activation(fls[0:HEADS, 0, :], fls[0:HEADS, 0, :], ACT.Ln, bias=one_col[0:HEADS]).then_inc(*done("f_log", l))
            for c in range(2):
                act_heads(act, "fq", l, c, None, qz, HD ** -0.5)
            for c in range(2):
                act_heads(act, "fk", l, c, None, kz)
            for c in range(2):
                act_values(act, ("fv", l, c), v[:, :, c * P:(c + 1) * P], NT)
            act_softmax(act, ("fox", l, 0))
            act_modulation(act, 3)
            for c in range(2):
                act_heads(act, "sq", l, c, None, qz, HD ** -0.5)
            for c in range(2):
                act_heads(act, "sk", l, c, None, kz)
            for c in range(2):
                act_values(act, ("sv", l, c), v[:, :, c * P:(c + 1) * P], NT)
            act_stick(act, l)
            act_modulation(act, 3)
            job = ("ckv", l, 0)
            act.wait_ge(*at("job_done", job))
            nc.scalar.activation(ckvT, ps[:, bank_of(job), :], ACT.Copy).then_inc(*done("evac_act", job))
            for c in range(2):
                job = ("cq", l, c)
                act.wait_ge(*at("job_done", job))
                nc.scalar.activation(cqT[:, c, :], ps[:, bank_of(job), :], ACT.Copy).then_inc(*done("evac_act", job))
            for i, (job, r) in enumerate(((("kvsum", l), KVR), (("qsum", l), QR))):
                act.wait_ge(*at("job_done", job))
                nc.scalar.activation(rms[:, i, :], ps[:, bank_of(job), :], ACT.Sqrt, scale=1.0 / r,
                                     bias=col[:, 51:52]).then_inc(*done("evac_act", job))
            for hh in range(HEADS):
                job = ("mk", l, hh)
                act.wait_ge(*at("job_done", job))
                nc.scalar.activation(kz[0:HD, hh, :], ps[0:HD, bank_of(job), :], ACT.Copy).then_inc(*done("evac_act", job))
            for half in range(2):
                job = ("mv", l, half)
                act.wait_ge(*at("job_done", job))
                nc.scalar.activation(v[:, 2 * half:2 * half + 2, :], ps[:, bank_of(job), :].rearrange("p (t n) -> p t n", t=2),
                                     ACT.Copy).then_inc(*done("evac_act", job))
            for hh in range(HEADS):
                job = ("mqu", l, hh)
                act.wait_ge(*at("job_done", job))
                nc.scalar.activation(qz[0:MLA_QK, hh, :], ps[0:MLA_QK, bank_of(job), :], ACT.Copy,
                                     scale=MLA_QK ** -0.5).then_inc(*done("evac_act", job))
            act_softmax(act, ("mla", l, 0))
            act_modulation(act, 3)
            for c in range(2):
                act_heads(act, "mq", l, c, None, qz, HD ** -0.5)
            for c in range(2):
                act_heads(act, "memk", l, c, None, kz)
            for c in range(2):
                act_values(act, ("memv", l, c), v[:, 0:NC, c * P:(c + 1) * P], NC)
            act_softmax(act, ("mem", l, 0))
            act_modulation(act, 3)
            st = ("first", l)
            nxt = ("plain", l + 1) if l + 1 < DEPTH else ("pre", 0)
            for t in range(NT):
                act_root(act, (st, t), LN_EPS)
                act_head(act, nxt, t)

        one_col = col[:, 52:53]

        def act_stick(act, l):
            def softplus(n):
                hh, i = sb_unit(n)
                w = SEQ - i * P
                act.wait_ge(*at("sb_logits", (l, n)))
                if n >= 2:
                    act.wait_ge(*at("softplus_raw", (l, n - 2)))
                t = sbt[:, n % 2, 0:w]
                nc.scalar.activation(t, ps[:, n % 2, 0:w], ACT.Abs).then_inc(*done("act_step", ("s0", l, n)))
                act.wait_ge(*at("act_step", ("s0", l, n)))
                nc.scalar.activation(t, t, ACT.Exp, scale=-1.0).then_inc(*done("act_step", ("s1", l, n)))
                act.wait_ge(*at("act_step", ("s1", l, n)))
                nc.scalar.activation(t, t, ACT.Ln, bias=one_col).then_inc(*done("sb_log", (l, n)))

            def weights(n):
                hh, i = sb_unit(n)
                w = SEQ - i * P
                act.wait_ge(*at("sb_logw", (l, n)))
                if hh >= 2 and i == 3:
                    act.wait_ge(*at("job_done", ("sbpv", l, hh // 2 - 1)))
                nc.scalar.activation(sbw[:, hh % 2, sp_off[i]:sp_off[i] + w], ps[:, 2 + n % 2, 0:w],
                                     ACT.Exp).then_inc(*done("sb_exp", (l, n)))

            for n in range(4 * HEADS + 2):
                if n < 4 * HEADS:
                    softplus(n)
                if n >= 2:
                    weights(n - 2)

        def dve_stick(dve, l):
            def softplus(n):
                hh, i = sb_unit(n)
                w = SEQ - i * P
                dve.wait_ge(*at("sb_log", (l, n)))
                if hh >= 2:
                    dve.wait_ge(*at("sb_logw", (l, 4 * (hh - 1) - 1)))
                o = sp_off[i]
                nc.vector.scalar_tensor_tensor(sp[:, hh % 2, o:o + w], ps[:, n % 2, 0:w], 0.0, sbt[:, n % 2, 0:w],
                                               ALU.max, ALU.add).then_inc(*done("softplus_raw", (l, n)))
                dve.wait_ge(*at("softplus_raw", (l, n)))
                nc.vector.tensor_tensor(sp[:, hh % 2, o:o + P], sp[:, hh % 2, o:o + P], cst(C_STRICT),
                                        ALU.mult).then_inc(*done("softplus", (l, n)))

            def weights(n):
                hh, i = sb_unit(n)
                o = sp_off[i]
                dve.wait_ge(*at("sb_exp", (l, n)))
                nc.vector.tensor_tensor(sbw[:, hh % 2, o:o + P], sbw[:, hh % 2, o:o + P], cst(C_BIG),
                                        ALU.min).then_inc(*done("sb_weights", (l, n)))

            def leave(p):
                job = ("sbpv", l, p)
                dve.wait_ge(*at("job_done", job))
                nc.vector.tensor_tensor(mixT[:, 2 + p, :], mixT[:, 2 + p, :], ps[:, bank_of(job), :],
                                        ALU.mult).then_inc(*done("evac_dve", job))

            for n in range(4 * HEADS + 3):
                if n < 4 * HEADS:
                    softplus(n)
                if 2 <= n < 4 * HEADS + 2:
                    weights(n - 2)
                if n >= 3 and sb_unit(n - 3) in ((1, 0), (3, 0)):
                    leave(sb_unit(n - 3)[0] // 2)

        def dve_first_block(dve, l):
            dve.wait_ge(*at("f_log", l))
            nc.vector.scalar_tensor_tensor(fls[0:HEADS, 0, :], flog[0:HEADS, :], 0.0, fls[0:HEADS, 0, :], ALU.min,
                                           ALU.subtract).then_inc(*done("dve_step", ("lf", l)))
            dve.wait_ge(*at("dve_step", ("lf", l)))
            nc.vector.tensor_tensor_scan(fls[0:HEADS, 1, :], const[0:HEADS, C_ONE:C_ONE + 1].broadcast_to([HEADS, SEQ]), fls[0:HEADS, 0, :], 0.0, ALU.mult,
                                         ALU.subtract).then_inc(*done("fcum", l))
            dve.wait_ge(*at("evac_act", ("gate", l, 7)))
            dve_softmax(dve, ("fox", l, 0), True)
            dve_modulation(dve, 3)
            dve_stick(dve, l)
            dve_modulation(dve, 3)
            for i, (name, job) in enumerate((("kv", ("kvsum", l)), ("q", ("qsum", l)))):
                dve.wait_ge(*at("evac_act", job))
                nc.vector.reciprocal(rms[:, i, :], rms[:, i, :]).then_inc(*done("dve_step", ("rm", l, i)))
                dve.wait_ge(*at("dve_step", ("rm", l, i)))
                if name == "kv":
                    g = vec[:, V_MKVG + l:V_MKVG + l + 1]
                    dve.wait_ge(*at("squares", (l, 2)))
                    ins = nc.vector.scalar_tensor_tensor(ckvT, ckvT, g, rms[:, i, :], ALU.mult, ALU.mult)
                else:
                    dve.wait_ge(*at("squares", (l, 1)))
                    for c in range(2):
                        g = vec[:, V_MQG + 2 * l + c:V_MQG + 2 * l + c + 1]
                        ins = nc.vector.scalar_tensor_tensor(cqT[:, c, :], cqT[:, c, :], g, rms[:, i, :], ALU.mult, ALU.mult)
                ins.then_inc(*done("rms_ready", (l, name)))
            R = slice(HD, KROWS)
            cos, sin = cst(C_COS, SEQ, R), cst(C_SIN, SEQ, R)
            for name, job, dst in [("k", ("krr", l), kr[R, :])] + [(hh, ("mqr", l, hh), qz[R, hh, :]) for hh in range(HEADS)]:
                dve.wait_ge(*at("job_done", job))
                nc.vector.tensor_tensor(rope_t[R, :], sin, ps[R, bank_of(job), :], ALU.mult).then_inc(*done("evac_dve", job))
                nc.vector.tensor_tensor(dst, dst, cos, ALU.mult).then_inc(*done("dve_step", ("rc", l, name)))
                dve.wait_ge(*at("evac_dve", job))
                dve.wait_ge(*at("dve_step", ("rc", l, name)))
                nc.vector.tensor_tensor(dst, dst, rope_t[R, :], ALU.add).then_inc(
                    *(done("kr_roped", l) if name == "k" else done("mla_q", (l, name))))
                dve.wait_ge(*(at("kr_roped", l) if name == "k" else at("mla_q", (l, name))))
            dve_softmax(dve, ("mla", l, 0), True)
            dve_modulation(dve, 3)
            dve_softmax(dve, ("mem", l, 0), True)
            dve_modulation(dve, 3)
            st = ("first", l)
            nxt = ("plain", l + 1) if l + 1 < DEPTH else ("pre", 0)
            for t in range(NT):
                dve_out(dve, st, t)
                dve_norm(dve, (st, t), res(t), res(t), rows_of(st),
                         final=("tile_ready", (nxt, t)) if nxt[0] == "plain" else None)
                if nxt[0] != "plain":
                    dve.wait_ge(*at("dve_step", ("b", (st, t))))
                dve_head(dve, nxt, t)

        def act_conv_in(act, l):
            act.wait_ge(*at("roped", (l, "ak", 0)))
            for c in range(2):
                job = ("a", l, c, 0)
                act.wait_ge(*at("job_done", job))
                nc.scalar.activation(hp[:, c, HALO:HALO + SEQ], ps[:, bank_of(job), :], ACT.Copy).then_inc(*done("evac_act", job))
            for c in range(2):
                job = ("g", l, c, 0)
                act.wait_ge(*at("job_done", job))
                if c == 1:
                    act.wait_ge(*at("glu", (l, 0, 0)))
                nc.scalar.activation(glu, ps[:, bank_of(job), :], ACT.Sigmoid).then_inc(*done("evac_act", job))

        def dve_taps(dve, l, r, n, src, gate_of):
            dve.wait_ge(*at("halo", (l, r)))
            for c in range(2):
                dve.wait_ge(*at("evac_act", ("g", l, c, r)))
                x = src[:, c, HALO:HALO + n]
                nc.vector.tensor_tensor(x, x, gate_of(c), ALU.mult).then_inc(*done("glu", (l, r, c)))
            for j in range(TAPS):
                for c in range(2):
                    o = V_CONVW + (2 * l + c) * TAPS + j
                    wj = vec[:, o:o + 1]
                    x = src[:, c, j:j + n]
                    if j == 0:
                        dve.wait_ge(*at("glu", (l, r, c)))
                        bo = V_CONVB + 2 * l + c
                        ins = nc.vector.tensor_scalar(acc[:, c, 0:n], x, wj, vec[:, bo:bo + 1], ALU.mult, ALU.add)
                    else:
                        dve.wait_ge(*at("dve_step", ("cv", l, r, j - 1, c)))
                        ins = nc.vector.scalar_tensor_tensor(acc[:, c, 0:n], x, wj, acc[:, c, 0:n], ALU.mult, ALU.add)
                    if j == TAPS - 1 and c == 1:
                        ins.then_inc(*done("conv_done", (l, r)))
                    else:
                        ins.then_inc(*done("dve_step", ("cv", l, r, j, c)))

        def dve_conv(dve, l):
            dve_taps(dve, l, 0, SEQ, hp, lambda c: glu)

        def dve_conv_norm(dve, l, r):
            n = (SEQ, CTX)[r]
            job = ("cmean", l, r)
            dve.wait_ge(*at("job_done", job))
            for c in range(2):
                ins = nc.vector.scalar_tensor_tensor(acc[:, c, 0:n], ps[:, bank_of(job), 0:n], -1.0 / 256, acc[:, c, 0:n],
                                                     ALU.mult, ALU.add)
            ins.then_inc(*done("evac_dve", job))
            dve.wait_ge(*at("evac_dve", job))
            nc.vector.tensor_tensor(csq[:, :, 0:n], acc[:, :, 0:n], acc[:, :, 0:n], ALU.mult).then_inc(*done("conv_sq", (l, r)))
            dve.wait_ge(*at("evac_act", ("cvar", l, r)))
            nc.vector.reciprocal(csd[:, 0:n], csd[:, 0:n]).then_inc(*done("dve_step", ("cr", l, r)))
            dve.wait_ge(*at("dve_step", ("cr", l, r)))
            for c in range(2):
                ins = nc.vector.tensor_tensor(acc[:, c, 0:n], acc[:, c, 0:n], csd[:, 0:n], ALU.mult)
            ins.then_inc(*done("conv_normed", (l, r)))

        def act_conv_out(act, l, r):
            n = (SEQ, CTX)[r]
            job = ("cvar", l, r)
            act.wait_ge(*at("job_done", job))
            nc.scalar.activation(csd[:, 0:n], ps[:, bank_of(job), 0:n], ACT.Sqrt, scale=1.0 / 256,
                                 bias=col[:, 51:52]).then_inc(*done("evac_act", job))
            act.wait_ge(*at("conv_normed", (l, r)))
            dst = (mixT, mixcT)[r]
            for c in range(2):
                ins = nc.scalar.activation(dst[:, 6 + c, 0:n], acc[:, c, 0:n], ACT.Silu,
                                           scale=vec[:, V_CLNG + 2 * l + c:V_CLNG + 2 * l + c + 1],
                                           bias=vec[:, V_CLNB + 2 * l + c:V_CLNB + 2 * l + c + 1])
            ins.then_inc(*done("conv_out", (l, r)))

        def act_rope_in(act, l, name, c):
            job = (name, l, c, 0)
            act.wait_ge(*at("job_done", job))
            prev = {("aq", 0): ("ak", 0)}.get((name, c), (name, c - 1))
            if name == "aq":
                act.wait_ge(*at("roped", (l,) + prev))
            nc.scalar.activation(rt1, ps[:, bank_of(job), :], ACT.Copy,
                                 scale=HD ** -0.5 if name == "aq" else 1.0).then_inc(*done("evac_act", job))

        def dve_rope(dve, l, name, c):
            job = ("rot", l, name, c)
            dve.wait_ge(*at("job_done", job))
            nc.vector.tensor_tensor(rot_t[:, :], axial[:, SEQ:2 * SEQ], ps[:, bank_of(job), :],
                                    ALU.mult).then_inc(*done("evac_dve", job))
            nc.vector.tensor_tensor(rt1, rt1, axial[:, 0:SEQ], ALU.mult).then_inc(*done("dve_step", ("ro", l, name, c)))
            dve.wait_ge(*at("evac_dve", job))
            dve.wait_ge(*at("dve_step", ("ro", l, name, c)))
            dst = qz if name == "aq" else kz
            for e in range(2):
                R = slice(e * HD, (e + 1) * HD)
                ins = nc.vector.tensor_tensor(dst[0:HD, 2 * (c % 2) + e, :], rt1[R, :], rot_t[R, :], ALU.add)
            ins.then_inc(*done("roped", (l, name, c)))
            dve.wait_ge(*at("roped", (l, name, c)))

        rot_t = sb("rot_t", [P, SEQ])
        axial = const[:, C_COS:C_COS + 2 * SEQ]

        def act_second_block(act, l):
            def q_job(c):
                act_rope_in(act, l, "aq", c)
                if l == 0:
                    act_heads(act, "aq", l, c, 1, QC, HD ** -0.5)

            act_rope_in(act, l, "ak", 0)
            act_ctx_keys(act, l, ("ak", l, 0, 1), 0)
            for c in range(2):
                q_job(c)
            act_conv_in(act, l)
            if l == 0:
                act_conv_in_ctx(act, l)
            act_values(act, ("av", l, 0, 0), v[:, :, 0:P], NT)
            act_values(act, ("av", l, 0, 1), VC[:, :, 0:P], NC)
            for c in range(2):
                act_ctx_keys(act, l, ("bk", l, c, 1), 2 + 2 * c)
            for c in range(2):
                act_values(act, ("bv", l, c, 1), VC[:, :, P + c * P:P + (c + 1) * P], NC)
            for part in range(2):
                if part == 1:
                    q_job(2)
                    q_job(3)
                if part == 0:
                    for r in streams(l, "a"):
                        act_conv_out(act, l, r)
                act_softmax(act, ("wa", l, part))
                if l == 0:
                    act_softmax(act, ("ca", l, part))
            for c in range(2):
                act_heads(act, "bk", l, c, 0, kz)
            for c in range(2):
                act_values(act, ("bv", l, c, 0), v[:, :, c * P:(c + 1) * P], NT)
            for c in range(2):
                for r in streams(l, "bq"):
                    act_heads(act, "bq", l, c, r, (qz, QC)[r], HD ** -0.5)
            act_softmax(act, ("nb", l, 0))
            if l == 0:
                act_softmax(act, ("cb", l, 0))
            act_gate_rows(act, l, 0)
            st = ("mixer", l)
            tiles = list(range(NT + NC)) if l == 0 else list(range(NT))
            rt = ("route", l)

            def roots(t):
                act_root(act, (st, t), LN_EPS_2)
                act_root(act, (rt, t), LN_EPS_2)

            staggered(mixer_tiles(l), [
                (lambda t: act_head(act, rt, t, root=False), 1),
                (roots, 0),
                (lambda t: act_route(act, rt, t), 2),
                (lambda t: act_affinities(act, rt, t), 3)])
            act_gate_rows(act, l, 1)
            experts_act(act, l)
            act_moe_out(act, l)

        def act_conv_in_ctx(act, l):
            for c in range(2):
                job = ("a", l, c, 1)
                act.wait_ge(*at("job_done", job))
                nc.scalar.activation(hpc[:, c, HALO:HALO + CTX], ps[:, bank_of(job), 0:CTX], ACT.Copy).then_inc(*done("evac_act", job))
            for c in range(2):
                job = ("g", l, c, 1)
                act.wait_ge(*at("job_done", job))
                nc.scalar.activation(gluc[:, c, :], ps[:, bank_of(job), 0:CTX], ACT.Sigmoid).then_inc(*done("evac_act", job))

        mixcf = mixcT[:, :, :].rearrange("p a b -> p (a b)")
        hpc = mixcf[:, 0:2 * (CTX + 2 * HALO)].rearrange("p (c n) -> p c n", c=2)
        gluc = mixcf[:, 576:1088].rearrange("p (c n) -> p c n", c=2)

        def act_ctx_keys(act, l, job, first):
            act.wait_ge(*at("job_done", job))
            for e in range(2):
                ins = nc.scalar.activation(KC[0:HD, first + e, :], ps[e * HD:(e + 1) * HD, bank_of(job), 0:CTX], ACT.Copy)
            ins.then_inc(*done("evac_act", job))

        def dve_conv_ctx(dve, l):
            dve.wait_ge(*at("conv_out", (l, 0)))
            dve_taps(dve, l, 1, CTX, hpc, lambda c: gluc[:, c, :])

        def dve_second_block(dve, l):
            if l == 0:
                dve.wait_ge(sem("axial_landed"), 16)
            dve_rope(dve, l, "ak", 0)
            dve_rope(dve, l, "aq", 0)
            dve_rope(dve, l, "aq", 1)
            dve_conv(dve, l)
            dve_conv_norm(dve, l, 0)
            if l == 0:
                dve_conv_ctx(dve, l)
                dve_conv_norm(dve, l, 1)
            for part in range(2):
                if part == 1:
                    dve_rope(dve, l, "aq", 2)
                    dve_rope(dve, l, "aq", 3)
                dve_softmax(dve, ("wa", l, part), False)
                if l == 0:
                    dve_softmax(dve, ("ca", l, part), False)
            dve_softmax(dve, ("nb", l, 0), False)
            if l == 0:
                dve_softmax(dve, ("cb", l, 0), False)
            gate_diagonals(dve, nc.vector, l, 0)
            st = ("mixer", l)
            tiles = list(range(NT + NC)) if l == 0 else list(range(NT))
            def residual(t):
                dve_out(dve, st, t)
                dve_norm(dve, (st, t), res(t), res(t), rows_of(st))
                dve.wait_ge(*at("dve_step", ("b", (st, t))))
                dve_head(dve, ("route", l), t)

            staggered(mixer_tiles(l), [(residual, 0), (lambda t: dve_route(dve, ("route", l), t), 2),
                                       (lambda t: t == NT + NC - 1 and dve_topk(dve, l, 1), 4)])
            dve_topk(dve, l, 0)
            dve_slots(dve, l)
            experts_dve(dve, l)
            dve_moe_out(dve, l)

        for name in sem_names:
            sem(name)
        for s in range(RING):
            sem(f"slot{s}")
        block = ctx.enter_context(nc.Block())

        @block.tensor
        def _(pe):
            pe.wait_ge(sem("const_landed"), 32)
            pe.wait_ge(*at("cond", 0))
            for t in (NT, NT + 1):
                pe_head(pe, ("plain", -1), t)
            for t in range(NT):
                pe_head(pe, ("plain", 0), t)
            for l in range(DEPTH):
                if stop > l:
                    pe_first_block(pe, l)
            for l in range(DEPTH):
                if stop > 2 + l:
                    for t in (range(NT, NT + NC) if l == 0 else []):
                        pe_head(pe, ("pre", 0), t)
                    if l > 0:
                        for t in range(NT + NC):
                            pe_head(pe, ("pre", l), t)
                    pe_second_block(pe, l)

        @block.scalar
        def _(act):
            act.dma_start(vec[:, :], a["vec"]).then_inc(sem("vec_landed"), 16)
            act.wait_ge(sem("vec_landed"), 16)
            act.wait_ge(*at("cond_zero", 0))
            nc.scalar.activation(cond[:, :, 0:2], vec[:, V_COND:V_COND + 2 * KD].rearrange("p (k r) -> p k r", r=2),
                                 ACT.Silu).then_inc(*done("cond", 0))
            act.wait_ge(*at("columns", 0))
            for t in (NT, NT + 1):
                act_root(act, (("mem_ln", 0), t), LN_EPS)
                act_head(act, ("plain", -1), t)
            for t in range(NT):
                act_root(act, (("ln_in", 0), t), LN_EPS)
                act_head(act, ("plain", 0), t)
            act.wait_ge(sem("y_zeroed"), 16 * sum(map(tiles_of, range(DEPTH))))
            for l in range(DEPTH):
                if stop > l:
                    act_first_block(act, l)
            for l in range(DEPTH):
                if stop > 2 + l:
                    for t in (range(NT, NT + NC) if l == 0 else []):
                        act_head(act, ("pre", 0), t)
                    act_second_block(act, l)

        @block.vector
        def _(dve):
            nc.vector.memset(col[:, 50:51], LN_EPS)
            nc.vector.memset(col[:, 51:52], LN_EPS_2)
            nc.vector.memset(col[:, 52:53], 1.0).then_inc(*done("columns", 0))
            dve.wait_ge(*at("columns", 0))
            dve.wait_ge(sem("vec_landed"), 16)
            dve.wait_ge(sem("const_landed"), 32)
            for st, nxt, tiles, rows in ((("mem_ln", 0), ("plain", -1), (NT, NT + 1), grow), (("ln_in", 0), ("plain", 0), range(NT), lnrow)):
                for t in tiles:
                    dve.wait_ge(sem(f"x_landed{t}"), 16)
                    if t in (0, NT):
                        dve.wait_ge(sem("in_rows_landed" if t == 0 else "mem_rows_landed"), 32)
                    dve_norm(dve, (st, t), res(t), res(t), (rows[:, 0, :], rows[:, 1, :]), final=("tile_ready", (nxt, t)))
            for l in range(DEPTH):
                if stop > l:
                    dve_first_block(dve, l)
            for l in range(DEPTH):
                if stop > 2 + l:
                    if l == 0:
                        for t in (NT, NT + 1):
                            dve.wait_ge(sem("ctx_landed"), 16 * NC)
                            dve_head(dve, ("pre", 0), t)
                    dve_second_block(dve, l)

        @block.gpsimd
        def _(pool):
            nc.gpsimd.memset(cond[:, :, :], 0.0).then_inc(*done("cond_zero", 0))
            nc.gpsimd.memset(kr[:, :], 0.0)
            nc.gpsimd.memset(probs[:, 0:D], 0.0).then_inc(*done("zeros", 0))
            pool.wait_ge(*at("zeros", 0))
            zeros = probs[:, 0:D]
            for l in range(DEPTH):
                for t in range(tiles_of(l)):
                    pool.dma_start(a["y_moe"][l][t * P:(t + 1) * P, :], zeros).then_inc(sem("y_zeroed"), 16)
            rows_n = [0]

            def load_rows(st, g, b):
                pool.dma_start(lnrow[:, 0, :], g.partition_broadcast(P)).then_inc(sem("rows_landed"), 16)
                pool.dma_start(lnrow[:, 1, :], b.partition_broadcast(P)).then_inc(sem("rows_landed"), 16)
                rows_n[0] += 32
                marks[("rows_landed", st)] = rows_n[0]

            n_stored = [0]
            n_y = [0]
            HR = slice(HD, KROWS)
            for l in range(DEPTH):
                if stop <= l:
                    break
                if l > 0:
                    pool.wait_ge(*at("job_done", ("mv", l - 1, 1)))
                    pool.wait_ge(*at("job_done", ("mqu", l - 1, HEADS - 1)))
                if l == 0:
                    pool.wait_ge(*at("job_done", ("turn", ("plain", -1), NT + NC - 1, 1)))
                    nc.gpsimd.memset(wmisc, 0.0).then_inc(*done("misc_zero", 0))
                    pool.wait_ge(*at("misc_zero", 0))
                cols = w_cols(a["w_in"], l, O_FL, HEADS)
                for k in range(2):
                    kk = slice(4 * k, 4 * k + 4)
                    pool.dma_start(wmisc[:, kk, 0:HEADS], cols[:, kk, :]).then_inc(sem("misc_landed"), 16)
                    pool.dma_start(wmisc[:, kk, HD:KROWS], w_cols(a["w_in"], l, O_KR, ROPE)[:, kk, :]).then_inc(sem("misc_landed"), 16)
                pool.dma_start(wqup, a["w_mla_q_up"][l].rearrange("(k p) c -> p k c", p=P)).then_inc(sem("mla_landed"), 16)
                pool.dma_start(wkvup[:, :], a["w_mla_kv_up"][l]).then_inc(sem("mla_landed"), 16)
                if l > 0:
                    pool.wait_ge(*at("scores", (("mem", l - 1, 0), NT - 1, HEADS - 1)))
                nc.gpsimd.memset(qz[HR, :, :], 0.0).then_inc(*done("rows_zeroed", (l, 0)))
                nc.gpsimd.memset(kz[HR, :, :], 0.0).then_inc(*done("rows_zeroed", (l, 1)))
                pool.wait_ge(*at("rows_zeroed", (l, 1)))
                nc.gpsimd.memset(qz[HD:HD + 1, :, :], 1.0).then_inc(*done("fox_rows", l))
                pool.wait_ge(*at("fcum", l))
                for hh in range(HEADS):
                    pool.dma_start(kz[HD:HD + 1, hh, :], fls[hh:hh + 1, 1, :]).then_inc(sem("fcum_landed"), 16)
                pool.wait_ge(*at("scores", (("fox", l, 0), NT - 1, HEADS - 1)))
                pool.wait_ge(sem("fcum_landed"), 64 * (l + 1))
                nc.gpsimd.memset(qz[HR, :, :], 0.0)
                nc.gpsimd.memset(kz[HR, :, :], 0.0).then_inc(*done("zero_rows", ("sb", l)))
                pool.wait_ge(*at("evac_act", ("ckv", l, 0)))
                nc.gpsimd.tensor_tensor(sqT[:, 2, :], ckvT, ckvT, ALU.mult).then_inc(*done("squares", (l, 2)))
                for c in range(2):
                    pool.wait_ge(*at("evac_act", ("cq", l, c)))
                    nc.gpsimd.tensor_tensor(sqT[:, c, :], cqT[:, c, :], cqT[:, c, :], ALU.mult).then_inc(*done("squares", (l, c)))
                pool.wait_ge(*at("kr_roped", l))
                for hh in range(HEADS):
                    ins = nc.gpsimd.tensor_copy(kz[HR, hh, :], kr[HR, :])
                ins.then_inc(*done("kr_spread", l))
                pool.wait_ge(*at("scores", (("mla", l, 0), NT - 1, HEADS - 1)))
                nc.gpsimd.memset(qz[HR, :, :], 0.0)
                nc.gpsimd.memset(kz[HR, :, :], 0.0).then_inc(*done("zero_rows", ("mem", l)))
                load_rows(("first", l), a["ln_g"][l], a["ln_b"][l])
            for l in range(DEPTH):
                if stop <= 2 + l:
                    break
                if l == 0:
                    pool.wait_ge(*at("mla_q", (DEPTH - 1, HEADS - 1)))
                    pool.dma_start(axial, a["axial"]).then_inc(sem("axial_landed"), 16)
                    pool.wait_ge(*at("job_done", ("memv", DEPTH - 1, 1)))
                    for t in range(NC):
                        pool.dma_start(hc[:, t, :], a["ctx_2"][t * P:(t + 1) * P, :]).then_inc(sem("ctx_landed"), 16)
                pool.dma_start(wr[:, :, :], a["w_router_2"][l].rearrange("(k p) e -> p k e", p=P)).then_inc(sem("router_landed"), 16)
                pool.wait_ge(*at("job_done", ("turn", ("pre", l), NT + NC - 1, 1)))
                nc.gpsimd.memset(hp[:, :, 0:HALO], 0.0)
                nc.gpsimd.memset(hp[:, :, HALO + SEQ:SEQ + 2 * HALO], 0.0).then_inc(*done("halo", (l, 0)))
                if l == 0:
                    nc.gpsimd.memset(hpc[:, :, 0:HALO], 0.0)
                    nc.gpsimd.memset(hpc[:, :, HALO + CTX:CTX + 2 * HALO], 0.0).then_inc(*done("halo", (l, 1)))
                pool.wait_ge(*at("halo", (l, streams(l, "a")[-1])))
                nc.gpsimd.memset(QC[HR, :, :], 0.0)
                nc.gpsimd.memset(KC[HR, :, :], 0.0)
                nc.gpsimd.memset(qz[HR, :, :], 0.0)
                nc.gpsimd.memset(kz[HR, :, :], 0.0).then_inc(*done("zero_rows", ("second", l)))
                for hh in range(HEADS):
                    if hh == 0:
                        pool.wait_ge(*at("conv_out", (l, streams(l, "a")[-1])))
                    b = bias_of(hh)
                    pool.dma_start(b[0:64, 0:960], a["nat_bias_2"][l, hh]).then_inc(sem("bias_landed"), 16)
                    pool.dma_start(b[64:P, 64:1024], a["nat_bias_2"][l, hh]).then_inc(sem("bias_landed"), 16)
                    pool.wait_ge(sem("bias_landed"), 32 * (HEADS * l + hh + 1))
                    pool.wait_ge(*at("zero_rows", ("second", l)))
                    rows14 = b[:, 64:960].rearrange("p (s k) -> p s k", k=64)
                    nc.gpsimd.tensor_tensor(rows14, rows14, cst(C_COLMASK, 64).unsqueeze(1).broadcast_to([P, 14, 64]),
                                            ALU.add).then_inc(*done("bias_ready", (l, hh)))
                pool.wait_ge(*at("scores", (("nb", l, 0), NT - 1, HEADS - 1)))
                load_rows(("mixer", l), a["ln1_g_2"][l], a["ln1_b_2"][l])
                tiles = list(range(NT + NC)) if l == 0 else list(range(NT))
                for t in mixer_tiles(l):
                    st = ("route", l)
                    pool.wait_ge(*at("tile_ready", (st, t)))
                    pool.dma_start(a["x_norm"][l][t * P:(t + 1) * P, :], xt[:, t % 2, :]).then_inc(sem("x_norm_stored"), 16)
                    n_stored[0] += 16
                    marks[("x_norm_stored", st, t)] = n_stored[0]
                    pool.wait_ge(sem("x_norm_stored"), n_stored[0])
                marks[("x_norm_stored_all", l)] = n_stored[0]
                gate_diagonals(pool, nc.gpsimd, l, 1)
                load_rows(("experts", l), a["ln2_g_2"][l], a["ln2_b_2"][l])
                experts_pool(pool, l)
                pool.wait_ge(sem("scattered"), known.get(("scatter_base", l), 0) + 16 * EXPERTS)
                for t in tiles:
                    dst = ysbc[:, t - NT, :] if ctile(t) else ysb[:, t, :]
                    pool.dma_start(dst, a["y_moe"][l][t * P:(t + 1) * P, :]).then_inc(sem("y_landed"), 16)
                    n_y[0] += 16
                for t in tiles:
                    marks[("y_landed", l, t)] = n_y[0]
            if stop > 3:
                for t in range(NT):
                    pool.wait_ge(*at("out_ready", t))
                    pool.dma_start(a["out"][t * P:(t + 1) * P, :], h[:, t, :]).then_inc(sem("out_stored"), 16)
                pool.wait_ge(sem("out_stored"), 16 * NT)
            else:
                for t in range(NT):
                    pool.wait_ge(*at("tile_ready", ({0: ("plain", 0), 1: ("plain", 1), 2: ("pre", 0), 3: ("pre", 1)}[stop], t)))
                for t in range(NT):
                    pool.dma_start(a["out"][t * P:(t + 1) * P, :], h[:, t, :]).then_inc(sem("out_stored"), 16)
                pool.wait_ge(sem("out_stored"), 16 * NT)

        @block.sync
        def _(sp_):
            sp_.dma_start(const[:, 0:C_COS], a["const"][:, 0:C_COS]).then_inc(sem("const_landed"), 16)
            sp_.dma_start(const[:, C_COS:C_END], a["const"][:, C_COS:C_END]).then_inc(sem("const_landed"), 16)
            sp_.dma_start(grow[:, 0, :], a["mem_ln_g"].partition_broadcast(P)).then_inc(sem("mem_rows_landed"), 16)
            sp_.dma_start(grow[:, 1, :], a["mem_ln_b"].partition_broadcast(P)).then_inc(sem("mem_rows_landed"), 16)
            for t in (NT, NT + 1):
                sp_.dma_start(hc[:, t - NT, :], a["mem"][(t - NT) * P:(t - NT + 1) * P, :]).then_inc(sem(f"x_landed{t}"), 16)
            sp_.dma_start(lnrow[:, 0, :], a["ln_in_g"].partition_broadcast(P)).then_inc(sem("in_rows_landed"), 16)
            sp_.dma_start(lnrow[:, 1, :], a["ln_in_b"].partition_broadcast(P)).then_inc(sem("in_rows_landed"), 16)
            for t in range(NT):
                sp_.dma_start(h[:, t, :], a["x"][t * P:(t + 1) * P, :]).then_inc(sem(f"x_landed{t}"), 16)
            mods = iter(mod_order)
            for l in range(DEPTH):
                if stop <= l:
                    break
                for item in first_block_slots(l):
                    if item == "mod":
                        for _ in range(3):
                            ml, j = next(mods)
                            for q in range(4):
                                load_slot(sp_, ("mod", ml, 4 * j + q), w_cols(a["w_mod_2"], ml, (4 * j + q) * P))
                    else:
                        load_slot(sp_, *item)
            for l in range(DEPTH):
                if stop <= 2 + l:
                    break
                for item in second_block_slots(l):
                    load_slot(sp_, *item)
                while len(slot_keys) % RING:
                    slot_keys.append(None)
                old_keys = [last_in_slot(s) for s in range(RING)]
                for s in range(RING):
                    places[("moe_slot", l, s)] = 16 * slot_uses[s]
                base = known.get(("moe_k", (l, 0, 0, 0)), 1) - 1

                def body(i):
                    for u in range(2):
                        e = 2 * i + u
                        for m, w in enumerate((a["w_gate_2"], a["w_up_2"], a["w_down_2"])):
                            for k in range(KD):
                                pos = 24 * u + 8 * m + k
                                s = pos % RING
                                if first_round(i) and pos < RING:
                                    sp_.wait_ge(*at(*banks.get(("last", old_keys[s]), ("job_done", None))))
                                else:
                                    sp_.wait_ge(sem("moe_k"), i * 48 + (base + pos - RING + 1))
                                if first_round(i):
                                    src = w[l, e, k * P:(k + 1) * P, :]
                                else:
                                    src = w[l, bass.ds(e, 1), k * P:(k + 1) * P, :].rearrange("o p n -> (o p) n")
                                sp_.dma_start(ring[:, s, :], src).then_inc(sem(f"slot{s}"), 16)

                body(0)
                with sp_.Fori(1, ROUNDS) as i:
                    body(i)
                for s in range(RING):
                    slot_uses[s] += 4 * ROUNDS
                slot_keys.extend(("moe_end", l, s) for s in range(RING))

    return marks, places, list(sems)


def program_inputs(inputs):
    f = {k: np.ascontiguousarray(np.asarray(x)) for k, x in inputs.items()}
    const, axial = shape_constants()
    out = {"const": const, "axial": axial}
    for k in ("ln_in_g", "ln_in_b", "mem_ln_g", "mem_ln_b", "w_in", "w_mla_q_up", "w_mla_kv_up", "w_mem_kv", "w_out",
              "ln_g", "ln_b", "w_mod_2", "w_in_2", "w_out_2", "ln1_g_2", "ln1_b_2", "w_router_2", "w_gate_2", "w_up_2",
              "w_down_2", "ln2_g_2", "ln2_b_2"):
        out[k] = f[k]
    out["x"], out["mem"], out["ctx_2"] = f["x"][0], f["mem"][0], f["ctx_2"][0]
    vec = np.zeros((P, V_END), np.float32)
    vec[:, V_BMOD:V_CONVW] = f["b_mod_2"].reshape(DEPTH * 48, P).T
    vec[:, V_CONVW:V_CONVB] = f["conv_w_2"].reshape(DEPTH, TAPS, 2, P).transpose(3, 0, 2, 1).reshape(P, -1)
    vec[:, V_CONVB:V_CLNG] = f["conv_b_2"].reshape(DEPTH * 2, P).T
    vec[:, V_CLNG:V_CLNB] = f["conv_ln_g_2"].reshape(DEPTH * 2, P).T
    vec[:, V_CLNB:V_MQG] = f["conv_ln_b_2"].reshape(DEPTH * 2, P).T
    vec[:, V_MQG:V_MKVG] = f["mla_q_norm_g"].reshape(DEPTH * 2, P).T
    vec[:, V_MKVG:V_BF] = f["mla_kv_norm_g"].T
    vec[0:HEADS, V_BF:V_SINK] = f["b_forget"].T
    vec[:, V_SINK:V_COND] = f["a_sink_2"].reshape(1, -1)
    both = np.stack([f["c_2"][0], f["c_ctx_2"]])
    vec[:, V_COND:V_END] = both.reshape(2, KD, P).transpose(2, 1, 0).reshape(P, -1)
    out["vec"] = vec
    q = np.arange(64)
    dc = np.clip(q[None, :] - q[:, None], -15, 15) + 15
    nb = f["nat_bias_2"][:, :, :, dc]
    out["nat_bias_2"] = np.ascontiguousarray(nb.transpose(0, 1, 3, 2, 4)).reshape(DEPTH, HEADS, 64, 15 * 64)
    return out


def declare(nc, arrays):
    a = {k: nc.dram_tensor(f"in_{k}", x.shape, mybir.dt.from_np(x.dtype), kind="ExternalInput").ap()
         for k, x in arrays.items()}
    a["out"] = nc.dram_tensor("out_0", (SEQ, D), F32, kind="ExternalOutput").ap()
    for name in ("x_norm", "y_moe"):
        a[name] = [nc.dram_tensor(f"{name}{l}", (P * tiles_of(l), D), F32, kind="Internal").ap() for l in range(DEPTH)]
    return a


def kernel(**inputs):
    import concourse.bacc as bacc
    from concourse.bass_utils import run_bass_kernel_spmd

    arrays = program_inputs(inputs)
    noted = ({}, {}, [])
    for _ in range(2):
        nc = bacc.Bacc("TRN2", target_bir_lowering=False, num_devices=1)
        noted = build_program(nc, declare(nc, arrays), *noted)
    r = run_bass_kernel_spmd(nc, [{f"in_{k}": x for k, x in arrays.items()}], core_ids=[0])
    return np.asarray(r.results[0]["out_0"]).reshape(1, SEQ, D)
```

```python
from contextlib import ExitStack

import numpy as np

import concourse.bass as bass
from concourse import mybir

F32 = mybir.dt.float32
I32 = mybir.dt.int32
U32 = mybir.dt.uint32
ALU = mybir.AluOpType
ACT = mybir.ActivationFunctionType
AX = mybir.AxisListType.X

P = 128
D = 1024
KD = D // P
SEQ = 512
NT = SEQ // P
CTX = 256
NC = CTX // P
DEPTH = 2
HEADS = 4
HD = 64
ROPE = 32
MLA_QK = HD + ROPE
QR = 256
KVR = 128
ALPHA = (2 * DEPTH) ** 0.25
LN_EPS = 1e-5
RMS_EPS = 1e-6
LN_EPS_2 = 1e-6
NEG = -1e30
BIG = 3e38
KROWS = 96
TAPS = 31
HALO = TAPS // 2
EXPERTS = 16
CAP = 2 * SEQ // EXPERTS
CAP_C = 2 * CTX // EXPERTS
RING = 12
UC = 4

O_FQ, O_FK, O_FV, O_FL = 0, 256, 512, 768
O_SQ, O_SK, O_SV = 772, 1028, 1284
O_CQ, O_CKV, O_KR, O_MQ, O_GATE = 1540, 1796, 1924, 1956, 2212
O_AQ, O_AK, O_AV, O_BQ, O_BK, O_BV, O_C = 0, 512, 640, 768, 1024, 1280, 1536

C_IDENT, C_CAUSAL, C_BEFORE, C_TRI, C_NEG1, C_STRICT, C_BIG, C_ONE, C_ROTM, C_ROTA = range(0, 1280, 128)
C_COS, C_SIN = 1280, 1280 + SEQ
C_COLMASK = 1280 + 2 * SEQ
C_END = C_COLMASK + 64

V_BMOD = 0
V_CONVW = V_BMOD + DEPTH * 48
V_CONVB = V_CONVW + DEPTH * 2 * TAPS
V_CLNG = V_CONVB + DEPTH * 2
V_CLNB = V_CLNG + DEPTH * 2
V_MQG = V_CLNB + DEPTH * 2
V_MKVG = V_MQG + DEPTH * 2
V_BF = V_MKVG + DEPTH
V_SINK = V_BF + DEPTH
V_COND = V_SINK + DEPTH * 8
V_END = V_COND + 2 * KD


def tiles_of(l):
    return NT + NC if l < DEPTH - 1 else NT


def shape_constants():
    i = np.arange(P)
    c = np.zeros((P, C_END), np.float32)
    c[:, C_IDENT:C_IDENT + P] = np.eye(P)
    c[:, C_CAUSAL:C_CAUSAL + P] = np.where(i[None, :] <= i[:, None], 0.0, NEG)
    c[:, C_BEFORE:C_BEFORE + P] = np.where(i[None, :] >= i[:, None], 0.0, NEG)
    c[:, C_TRI:C_TRI + P] = np.where(i[:, None] >= i[None, :], -1.0, 0.0)
    c[:, C_NEG1:C_NEG1 + P] = -1.0
    c[:, C_STRICT:C_STRICT + P] = np.where(i[:, None] < i[None, :], 1.0, 0.0)
    c[:, C_BIG:C_BIG + P] = np.where(i[:, None] < i[None, :], BIG, 0.0)
    c[:, C_ONE:C_ONE + P] = 1.0
    rot = np.zeros((P, P), np.float32)
    for j in range(ROPE // 2):
        rot[HD + ROPE // 2 + j, HD + j] = -1.0
        rot[HD + j, HD + ROPE // 2 + j] = 1.0
    c[:, C_ROTM:C_ROTM + P] = rot
    rot = np.zeros((P, P), np.float32)
    for o in range(0, P, 32):
        for j in range(16):
            rot[o + 16 + j, o + j] = -1.0
            rot[o + j, o + 16 + j] = 1.0
    c[:, C_ROTA:C_ROTA + P] = rot
    half = ROPE // 2
    pos = np.arange(SEQ, dtype=np.float32)
    inv = np.float32(10000.0) ** (-np.arange(half, dtype=np.float32) / np.float32(half))
    ang = (pos[:, None] * inv[None, :]).astype(np.float32).T
    for o in (HD, HD + half):
        c[o:o + half, C_COS:C_COS + SEQ] = np.cos(ang)
        c[o:o + half, C_SIN:C_SIN + SEQ] = np.sin(ang)
    q = np.arange(64)
    start = np.clip(q - 8, 0, 48)
    seen = (q[None, :] >= start[:, None]) & (q[None, :] < start[:, None] + 16)
    c[:, C_COLMASK:C_COLMASK + 64] = np.tile(np.where(seen, 0.0, NEG), (2, 1))
    axial = np.zeros((P, 2 * SEQ), np.float32)
    tok = np.arange(SEQ)
    for o in range(0, P, 16):
        place = (tok // 64 if (o // 32) % 2 == 0 else tok % 64).astype(np.float32)
        a = (place[:, None] * inv[None, :]).astype(np.float32).T
        axial[o:o + 16, 0:SEQ] = np.cos(a)
        axial[o:o + 16, SEQ:] = np.sin(a)
    return c, axial


def build_program(nc, a, known, banks, sem_names):
    counts, marks, places, sems = {}, {}, {}, {}
    frozen = [False]

    with ExitStack() as ctx:
        def sb(name, shape, dt=F32):
            return ctx.enter_context(nc.sbuf_tensor(name, shape, dt))

        def sem(name):
            if name not in sems:
                sems[name] = ctx.enter_context(nc.semaphore(name))
            return sems[name]

        def done(name, event=None, by=1):
            if not frozen[0]:
                counts[name] = counts.get(name, 0) + by
                marks[(name, event)] = counts[name]
            return sem(name), by

        def at(name, event=None):
            return sem(name), known.get((name, event), 1)

        def emptied(job):
            for name in ("evac_act", "evac_dve"):
                if (name, job) in known:
                    return at(name, job)
            return at("evac_act", job)

        ring = sb("ring", [P, RING, KD * P])
        h = sb("h", [P, NT, D])
        hc = sb("hc", [P, NC, D])
        hT = sb("hT", [P, KD, SEQ])
        hcT = sb("hcT", [P, KD, CTX])
        mixT = sb("mixT", [P, KD, SEQ])
        mixcT = sb("mixcT", [P, KD, CTX])
        qz = sb("qz", [P, HEADS, SEQ])
        kz = sb("kz", [P, HEADS, SEQ])
        v = sb("v", [P, NT, 256])
        const = sb("const", [P, C_END])
        vec = sb("vec", [P, V_END])
        probs = sb("probs", [P, 4 * 640])
        probsT = sb("probsT", [P, 2, 6, P])
        work = sb("work", [P, 8512])
        wkvup = sb("wkvup", [P, HEADS * 2 * HD])
        cond = sb("cond", [P, KD, 32])
        modrow = sb("modrow", [P, P])
        modc = sb("modc", [P, DEPTH, 48, 2])
        col = sb("col", [P, 80])
        aff = sb("aff", [P, NT + NC, EXPERTS])
        wr = sb("wr", [P, KD, EXPERTS])
        gates = sb("gates", [P, EXPERTS + 1])
        idxf = sb("idxf", [P, EXPERTS + 1])
        idx = sb("idx", [P, EXPERTS + 2], I32)
        idx_at = [sb(f"idx_at{b}", [P, 1], I32) for b in range(2)]
        idx_to = [sb(f"idx_to{b}", [P, 1], I32) for b in range(2)]

        xt = kz[:, :, :].rearrange("p a b -> p (a b)").rearrange("p (r d) -> p r d", r=2)
        h2t = qz[:, :, :].rearrange("p a b -> p (a b)").rearrange("p (r k t) -> p r k t", r=2, k=KD)
        lnrow = work[:, 0:2 * D].rearrange("p (r d) -> p r d", r=2)
        grow = work[:, 2 * D:4 * D].rearrange("p (r d) -> p r d", r=2)
        sp_off = [0, 512, 896, 1152]
        SPW = 1280
        sp = work[:, 0:2 * SPW].rearrange("p (r n) -> p r n", r=2)
        sbw = work[:, 2 * SPW:4 * SPW].rearrange("p (r n) -> p r n", r=2)
        sbt = work[:, 4 * SPW:4 * SPW + 1024].rearrange("p (r n) -> p r n", r=2)
        cqT = work[:, 0:1024].rearrange("p (c n) -> p c n", c=2)
        ckvT = work[:, 1024:1536]
        sqT = work[:, 1536:3072].rearrange("p (c n) -> p c n", c=3)
        rms = work[:, 3072:4096].rearrange("p (c n) -> p c n", c=2)
        rope_t = work[:, 4096:4608]
        kr = work[:, 6144:6656]
        flog = work[:, 6656:7168]
        fls = work[:, 7168:8192].rearrange("p (r n) -> p r n", r=2)
        hcf = hc[:, :, :].rearrange("p a b -> p (a b)")
        wmisc = hcf[:, 0:1024].rearrange("p (k n) -> p k n", k=KD)
        wqup = hcf[:, 1024:1024 + 2 * HEADS * MLA_QK].rearrange("p (k n) -> p k n", k=2)
        hp = work[:, 0:2 * (SEQ + 2 * HALO)].rearrange("p (c n) -> p c n", c=2)
        acc = work[:, 1088:2112].rearrange("p (c n) -> p c n", c=2)
        csq = work[:, 2112:3136].rearrange("p (c n) -> p c n", c=2)
        csd = work[:, 3136:3648]
        glu = work[:, 3648:4160]
        rt1 = work[:, 4160:4672]
        rot_t = work[:, 4672:5184]
        QC = work[:, 5184:6208].rearrange("p (a n) -> p a n", a=HEADS)
        KC = work[:, 6208:7744].rearrange("p (a n) -> p a n", a=6)
        VC = work[:, 7744:8512].rearrange("p (t n) -> p t n", t=NC)

        def bias_of(hh):
            return work[:, hh * D:(hh + 1) * D]

        affT = probs[0:EXPERTS, 0:SEQ + CTX]
        topv = probs[0:EXPERTS, 768:864]
        topf = probs[0:EXPERTS, 864:960]
        topi = sb("topi", [EXPERTS, 96], U32)
        hTf = hT[:, :, :].rearrange("p a b -> p (a b)")
        xs = hTf[:, 0:2 * D].rearrange("p (r d) -> p r d", r=2)
        xsT = hTf[:, 2 * D:2 * D + 2 * KD * 96].rearrange("p (r k t) -> p r k t", r=2, k=KD)
        sig = work[:, 4096:4608]
        sigc = work[:, 4608:4864]
        hid = work[:, 4864:5376]
        hidc = work[:, 5376:5632]
        hidT = work[:, 5632:5632 + 768].rearrange("p (k t) -> p k t", k=KD)
        ye = hcT[:, :, :].rearrange("p a b -> p (a b)").rearrange("p (r d) -> p r d", r=2)

        ps = ctx.enter_context(nc.psum_tensor("ps", [P, 8, 512], F32))
        psflat = ps[:, :, :].rearrange("p b n -> p (b n)")

        def cst(o, n=P, rows=slice(0, P)):
            return const[rows, o:o + n]

        ident = cst(C_IDENT)

        def ctile(t):
            return t >= NT

        def res(t):
            return hc[:, t - NT, :] if ctile(t) else h[:, t, :]

        def bank_of(job):
            return banks.get(("job", job), 6)

        job_ring = [6, 7]
        bank_user = {}

        def open_job(pe, job):
            b = job_ring.pop(0)
            job_ring.append(b)
            if b in bank_user:
                pe.wait_ge(*emptied(bank_user[b]))
            bank_user[b] = job
            places[("job", job)] = b
            return b

        def wide_jobs():
            job_ring[:] = list(range(8))

        def narrow_jobs(pe):
            job_ring[:] = [6, 7]
            for b in range(6):
                if b in bank_user:
                    pe.wait_ge(*emptied(bank_user.pop(b)))

        slot_keys = []
        slot_uses = [0] * RING

        def load_slot(eng, key, src):
            n = len(slot_keys)
            s = n % RING
            if n >= RING and slot_keys[n - RING][0] == "moe_end":
                ml = slot_keys[n - RING][1]
                eng.wait_ge(sem("moe_k"), known.get(("moe_k", (ml, 0, 0, 0)), 1) + EXPERT_SLOTS * (EXPERTS - 1) + s)
            elif n >= RING:
                eng.wait_ge(*at(*banks.get(("last", slot_keys[n - RING]), ("job_done", None))))
            slot_keys.append(key)
            slot_uses[s] += 1
            places[("slot", key)] = (s, 16 * slot_uses[s])
            eng.dma_start(ring[:, s, :].rearrange("p (k n) -> p k n", k=KD), src).then_inc(sem(f"slot{s}"), 16)

        def slot(pe, key):
            s, n = banks.get(("slot", key), (0, 16))
            pe.wait_ge(sem(f"slot{s}"), n)
            return ring[:, s, :].rearrange("p (k n) -> p k n", k=KD)

        def last_use(key, job):
            places[("last", key)] = ("job_done", job)

        def last_in_slot(s):
            return [key for n, key in enumerate(slot_keys) if n % RING == s and key is not None][-1]

        mod_order = [(l, j) for l in range(DEPTH) for j in range(12)]

        def w_cols(w, l, c0, n=P):
            return w[l, :, c0:c0 + n].rearrange("(k p) c -> p k c", p=P)

        def units_of(ph):
            kind, l, part = ph
            n = NC if kind in ("ca", "cb") else NT
            return [(ph, t, hh) for t in range(n) for hh in range(HEADS)]

        def keys_of(u):
            (kind, l, part), t, hh = u
            if kind in ("fox", "mla"):
                return t + 1
            if kind in ("mem", "ca", "cb"):
                return NC
            if kind == "wa":
                return (2 if t in (0, NT - 1) else 3) + NC
            return NT + NC

        seq = {}

        def all_phases():
            out = []
            for l in range(DEPTH):
                out += [("fox", l, 0), ("mla", l, 0), ("mem", l, 0)]
            for l in range(DEPTH):
                for part in range(2):
                    out += [("wa", l, part)] + ([("ca", l, part)] if l == 0 else [])
                out += [("nb", l, 0)] + ([("cb", l, 0)] if l == 0 else [])
            return out

        n_units = 0
        for ph in all_phases():
            for u in units_of(ph):
                seq[u] = n_units
                n_units += 1
        by_seq = {n: u for u, n in seq.items()}

        def has_sink(u):
            return u[0][0] in ("wa", "ca")

        def sink_col(u):
            (kind, l, part), t, hh = u
            c = V_SINK + 8 * l + 4 * part + hh
            return vec[:, c:c + 1]

        def chunks_of(u):
            n = keys_of(u)
            return [range(c, min(c + 4, n)) for c in range(0, n, 4)]

        turn_seq = []
        for n in range(n_units):
            turn_seq += [(by_seq[n], c) for c in range(len(chunks_of(by_seq[n])))]
        turn_at = {x: n for n, x in enumerate(turn_seq)}

        def ring_col(first):
            return lambda u: col[:, first + seq[u] % UC:first + 1 + seq[u] % UC]

        nmax, rsum, rinv, esink, rmax = (ring_col(60 + UC * k) for k in range(5))

        def wide(ph):
            return ph[0] in ("wa", "nb")

        def joined(ph):
            kind, l, part = ph
            after = {"wa": "ca", "nb": "cb"}.get(kind) if l == 0 else None
            return units_of(ph) + (units_of((after, l, part)) if after else [])

        def lag_of(ph):
            return 2 if ph[0] == "nb" else 3

        def score_span(u):
            o = (seq[u] % 2) * 1024 if wide(u[0]) else (seq[u] % 4) * 512
            return o, o + keys_of(u) * P

        def probs_span(u):
            n, w = {"nb": (3, 768), "wa": (4, 640)}.get(u[0][0], (4, 512))
            o = (seq[u] % n) * w
            return o, o + keys_of(u) * P

        def before(u, span):
            a0, a1 = span(u)
            for n in range(seq[u] - 1, max(seq[u] - 9, -1), -1):
                b0, b1 = span(by_seq[n])
                if a0 < b1 and b0 < a1:
                    return by_seq[n]
            return None

        def s_psum(u):
            return psflat[:, slice(*score_span(u))]

        def p_sbuf(u):
            return probs[:, slice(*probs_span(u))]

        def pair_job(u):
            return ("pv", u[0], u[1], u[2] // 2)

        def mix_out(u):
            (kind, l, part), t, hh = u
            chunk = {"fox": 0, "mla": 4, "mem": 6, "wa": 2 * part, "ca": 2 * part, "nb": 4, "cb": 4}[kind] + hh // 2
            dst = mixcT if kind in ("ca", "cb") else mixT
            return dst[:, chunk, t * P:(t + 1) * P]

        def pe_t_job(pe, job, slot_key, rhs, n, last=True):
            w = slot(pe, slot_key)
            b = open_job(pe, job)
            for k in range(KD):
                mm = nc.tensor.matmul(ps[:, b, 0:n], w[:, k, :], rhs[:, k, 0:n], start=(k == 0), stop=(k == KD - 1))
            mm.then_inc(*done("job_done", job))
            if last:
                last_use(slot_key, job)

        def pe_n_job(pe, job, slot_key, lhs, tiles, last=True):
            w = slot(pe, slot_key)
            b = open_job(pe, job)
            for t in range(tiles):
                for k in range(KD):
                    mm = nc.tensor.matmul(ps[:, b, t * P:(t + 1) * P], lhs[:, k, t * P:(t + 1) * P], w[:, k, :],
                                          start=(k == 0), stop=(k == KD - 1))
            mm.then_inc(*done("job_done", job))
            if last:
                last_use(slot_key, job)

        def pe_scores(pe, u):
            (kind, l, part), t, hh = u
            w = before(u, score_span)
            if w is not None:
                pe.wait_ge(*at("probs", w))
            S = s_psum(u)
            q = (QC if kind in ("ca", "cb") else qz)[0:KROWS, hh, t * P:(t + 1) * P]
            parts = []
            if kind in ("fox", "mla"):
                parts = [(q, kz[0:KROWS, hh, 0:(t + 1) * P], 0), (ident, cst(C_CAUSAL), t * P)]
            elif kind == "mem":
                parts = [(q, kz[0:KROWS, hh, 0:CTX], 0)]
            elif kind in ("ca", "cb"):
                parts = [(q, KC[0:KROWS, part if kind == "ca" else 2 + hh, :], 0)]
            elif kind == "nb":
                parts = [(q, kz[0:KROWS, hh, :], 0), (q, KC[0:KROWS, 2 + hh, :], SEQ)]
            else:
                j0, j1 = max(t - 1, 0), min(t + 1, NT - 1)
                w = (j1 - j0 + 1) * P
                parts = [(q, kz[0:KROWS, part, j0 * P:(j1 + 1) * P], 0)]
                if t > 0:
                    parts.append((ident, cst(C_BEFORE), 0))
                if t < NT - 1:
                    parts.append((ident, cst(C_CAUSAL), w - P))
                parts += [(q, KC[0:KROWS, part, c * P:(c + 1) * P], w + c * P) for c in range(NC)]
            for lhs, rhs, o in parts:
                mm = nc.tensor.matmul(S[:, o:o + rhs.shape[-1]], lhs, rhs, start=lhs is not ident, stop=True,
                                      skip_group_check=True)
            mm.then_inc(*done("scores", u))

        def v_block(u, j):
            (kind, l, part), t, hh = u
            if kind in ("fox", "mla", "mem"):
                return v[:, j, hh * HD:(hh + 1) * HD]
            if kind == "ca":
                return VC[:, j, part * HD:(part + 1) * HD]
            if kind == "cb":
                return VC[:, j, P + hh * HD:P + (hh + 1) * HD]
            if kind == "nb":
                return v[:, j, hh * HD:(hh + 1) * HD] if j < NT else VC[:, j - NT, P + hh * HD:P + (hh + 1) * HD]
            j0, j1 = max(t - 1, 0), min(t + 1, NT - 1)
            w = j1 - j0 + 1
            return v[:, j0 + j, part * HD:(part + 1) * HD] if j < w else VC[:, j - w, part * HD:(part + 1) * HD]

        def pe_turn(pe, u):
            pe.wait_ge(*at("probs_normed", u))
            for c, blocks in enumerate(chunks_of(u)):
                n = turn_at[(u, c)]
                if n >= 2:
                    pe.wait_ge(*at("probsT_ready", turn_seq[n - 2]))
                for i, j in enumerate(blocks):
                    mm = nc.tensor.transpose(ps[:, 4 + n % 2, i * P:(i + 1) * P],
                                             p_sbuf(u)[:, j * P:(j + 1) * P], ident)
                mm.then_inc(*done("turned", (u, c)))

        def pe_pv(pe, u):
            pair = [(u[0], u[1], u[2] - 1), u]
            job = pair_job(u)
            b = open_job(pe, job)
            for w in pair:
                pe.wait_ge(*at("probsT_ready", (w, len(chunks_of(w)) - 1)))
            n = keys_of(u)
            for j in range(n):
                for e, w in enumerate(pair):
                    mm = nc.tensor.matmul(ps[e * HD:(e + 1) * HD, b, 0:P], v_block(w, j),
                                          probsT[:, seq[w] % 2, j, :], start=(j == 0), stop=(j == n - 1))
            mm.then_inc(*done("job_done", job))

        def pe_softmax(pe, ph):
            us = joined(ph)
            lag = lag_of(ph)
            for i in range(len(us) + lag + 1):
                if i < len(us):
                    pe_scores(pe, us[i])
                if lag <= i < len(us) + lag:
                    pe_turn(pe, us[i - lag])
                if i > lag and us[i - lag - 1][2] % 2:
                    pe_pv(pe, us[i - lag - 1])
                if mods_at(ph, i, 0):
                    pe_mod(pe, mods_at(ph, i, 0))
                if mods_at(ph, i, 2):
                    pe_mod_turn(pe, mods_at(ph, i, 2))

        def sb_unit(n):
            return n // 4, 3 - n % 4

        def pe_stick(pe, l):
            for n in range(4 * HEADS + 2):
                if n < 4 * HEADS:
                    hh, i = sb_unit(n)
                    w = SEQ - i * P
                    if n >= 4:
                        pe.wait_ge(*at("sb_weights", (l, n - 4)))
                    nc.tensor.matmul(ps[:, n % 4, 0:w], kz[0:KROWS, hh, i * P:(i + 1) * P], qz[0:KROWS, hh, i * P:SEQ],
                                     start=True, stop=True).then_inc(*done("sb_logits", (l, n)))
                if n >= 2:
                    m = n - 2
                    hh, i = sb_unit(m)
                    w = SEQ - i * P
                    for j in range(i, 4):
                        if j == i:
                            pe.wait_ge(*at("softplus", (l, m)))
                        mm = nc.tensor.matmul(ps[:, m % 4, (j - i) * P:w], cst(C_TRI if j == i else C_NEG1),
                                              sp[:, hh % 2, sp_off[j]:sp_off[j] + SEQ - j * P], start=False,
                                              stop=True, skip_group_check=True)
                    mm.then_inc(*done("sb_logw", (l, m)))
                    if i == 0 and hh % 2:
                        job = ("sbpv", l, hh // 2)
                        b = open_job(pe, job)
                        pe.wait_ge(*at("sb_weights", (l, m)))
                        for j in range(4):
                            for e in range(2):
                                mm = nc.tensor.matmul(ps[e * HD:(e + 1) * HD, b, j * P:SEQ],
                                                      v[:, j, (hh - 1 + e) * HD:(hh + e) * HD],
                                                      sbw[:, e, sp_off[j]:sp_off[j] + SEQ - j * P],
                                                      start=(j == 0), stop=(j == 3), skip_group_check=True)
                        mm.then_inc(*done("job_done", job))
                if mods_at(("sb", l), n, 0):
                    pe_mod(pe, mods_at(("sb", l), n, 0))
                if mods_at(("sb", l), n, 2):
                    pe_mod_turn(pe, mods_at(("sb", l), n, 2))

        def pe_mod(pe, lj):
            l, j = lj
            w = [slot(pe, ("mod", l, 4 * j + q)) for q in range(4)]
            job = ("mod", l, j)
            b = open_job(pe, job)
            for k in range(KD):
                for q in range(4):
                    mm = nc.tensor.matmul(ps[32 * q:32 * q + 32, b, 0:P], cond[:, k, :], w[q][:, k, :],
                                          start=(k == 0), stop=(k == KD - 1), skip_group_check=True)
            mm.then_inc(*done("job_done", job))
            for q in range(4):
                last_use(("mod", l, 4 * j + q), job)

        def pe_mod_turn(pe, lj):
            l, j = lj
            job = ("modT", l, j)
            b = open_job(pe, job)
            pe.wait_ge(*emptied(("mod", l, j)))
            nc.tensor.transpose(ps[:, b, 0:P], modrow[:, :], ident).then_inc(*done("job_done", job))

        MODS = 3

        def mods_at(ph, i, delay):
            kind, l = ph[0], ph[1]
            if kind not in MOD_STEPS:
                return None
            group = MODS * (4 * l + ("fox", "sb", "mla", "mem").index(kind))
            for n, step in enumerate(MOD_STEPS[kind]):
                if i - delay == step:
                    return mod_order[group + n]
            return None

        MOD_STEPS = {"fox": (0, 2, 17), "sb": (0, 2, 15), "mem": (0, 4)}

        def mod_of_tail(l):
            return mod_order[MODS * 4 * (l + 1) - 1]

        def mods_of_mla(l):
            return mod_order[MODS * (4 * l + 2):MODS * (4 * l + 3)]

        def pe_head(pe, st, t):
            kind = st[0]
            pe.wait_ge(*at("tile_ready", (st, t)))
            src = res(t) if kind == "plain" else xt[:, t % 2, :]
            for half in range(2):
                job = ("turn", st, t, half)
                b = open_job(pe, job)
                for c in range(4):
                    o = (4 * half + c) * P
                    mm = nc.tensor.transpose(ps[:, b, c * P:(c + 1) * P], src[:, o:o + P], ident)
                mm.then_inc(*done("job_done", job))

        def pe_route(pe, st, t):
            job = ("route", st, t)
            b = open_job(pe, job)
            pe.wait_ge(*emptied(("turn", st, t, 1)))
            pe.wait_ge(sem("router_landed"), 16 * (st[1] + 1))
            for k in range(KD):
                mm = nc.tensor.matmul(ps[:, b, 0:EXPERTS], h2t[:, t % 2, k, :], wr[:, k, :], start=(k == 0),
                                      stop=(k == KD - 1))
            mm.then_inc(*done("job_done", job))

        def pe_affinities(pe, st, t):
            job = ("affT", st, t)
            b = open_job(pe, job)
            pe.wait_ge(*at("aff", (st, t)))
            nc.tensor.transpose(ps[0:EXPERTS, b, 0:P], aff[:, t, :], ident).then_inc(*done("job_done", job))

        def mixer_tiles(l):
            return [NT + t for t in range(NC)] * (l == 0) + list(range(NT))

        def staggered(tiles, steps):
            for i in range(len(tiles) + max(lag for _, lag in steps)):
                for step, lag in steps:
                    if 0 <= i - lag < len(tiles):
                        step(tiles[i - lag])

        def pe_out(pe, st, lhs, t, slots, first, last):
            for half in range(2):
                job = ("out", st, t, half)
                ws = [slot(pe, s) for s in slots[4 * half:4 * half + 4]] if first else [
                    ring[:, banks.get(("slot", s), (0, 16))[0], :].rearrange("p (k n) -> p k n", k=KD)
                    for s in slots[4 * half:4 * half + 4]]
                b = open_job(pe, job)
                tl = t - NT if ctile(t) else t
                for c in range(4):
                    for k in range(KD):
                        mm = nc.tensor.matmul(ps[:, b, c * P:(c + 1) * P], lhs[:, k, tl * P:(tl + 1) * P],
                                              ws[c][:, k, :], start=(k == 0), stop=(k == KD - 1))
                mm.then_inc(*done("job_done", job))
                if last:
                    for s in slots[4 * half:4 * half + 4]:
                        last_use(s, job)

        def pe_gate_rows(pe, l, which):
            for r in range(2 if l == 0 else 1):
                for half in range(2):
                    job = ("grow", l, which, r, half)
                    b = open_job(pe, job)
                    for c in range(4):
                        pe.wait_ge(*at(f"diag{which}", (l, which, r, 4 * half + c)))
                        mm = nc.tensor.matmul(ps[:, b, c * P:(c + 1) * P], cst(C_ONE),
                                              modrow_diag(4 * half + c), start=True, stop=True)
                        if c < 3:
                            mm.then_inc(*done("diag_used", (l, which, r, 4 * half + c)))
                    mm.then_inc(*done("job_done", job))

        diag = sb("diag", [P, 2, P])

        def modrow_diag(c):
            return diag[:, c % 2, :]

        def diag_free(l, which, r, c):
            if c % 4 < 3:
                return at("diag_used", (l, which, r, c))
            return at("job_done", ("grow", l, which, r, c // 4))

        def w1(l, name, c):
            return ("w1", l, name, c)

        def first_block_slots(l):
            out = [(w1(l, "gate", c), w_cols(a["w_in"], l, O_GATE + c * P)) for c in range(8)]
            for name, o in (("fq", O_FQ), ("fk", O_FK), ("fv", O_FV)):
                out += [(w1(l, name, c), w_cols(a["w_in"], l, o + c * P)) for c in range(2)]
            out.append("mod")
            for name, o in (("sq", O_SQ), ("sk", O_SK), ("sv", O_SV)):
                out += [(w1(l, name, c), w_cols(a["w_in"], l, o + c * P)) for c in range(2)]
            out.append("mod")
            out += [(w1(l, "ckv", 0), w_cols(a["w_in"], l, O_CKV))]
            out += [(w1(l, "cq", c), w_cols(a["w_in"], l, O_CQ + c * P)) for c in range(2)]
            out.append("mod")
            out += [(w1(l, "mq", c), w_cols(a["w_in"], l, O_MQ + c * P)) for c in range(2)]
            out += [(w1(l, "mk", c), w_cols(a["w_mem_kv"], l, c * P)) for c in range(2)]
            out += [(w1(l, "mv", c), w_cols(a["w_mem_kv"], l, 256 + c * P)) for c in range(2)]
            out.append("mod")
            out += [(w1(l, "wo", c), w_cols(a["w_out"], l, c * P)) for c in range(8)]
            return out

        def second_block_slots(l):
            def s(name, o, n):
                return [(w1(2 + l, name, c), w_cols(a["w_in_2"], l, o + c * P)) for c in range(n)]
            aq = s("aq", O_AQ, 4)
            return (s("a", O_C, 2) + s("g", O_C + 256, 2) + s("av", O_AV, 1)
                    + s("bk", O_BK, 2) + s("bv", O_BV, 2) + s("ak", O_AK, 1) + aq + s("bq", O_BQ, 2)
                    + [(w1(2 + l, "wo", c), w_cols(a["w_out_2"], l, c * P)) for c in range(8)])

        def pe_first_block(pe, l):
            pe.wait_ge(*emptied(("turn", ("plain", l), NT - 1, 1)))
            for c in range(8):
                pe_t_job(pe, ("gate", l, c), w1(l, "gate", c), hT, SEQ)
                if l == 0 and c == 3:
                    for t in (NT, NT + 1):
                        pe_head(pe, ("plain", -1), t)
            pe.wait_ge(sem("misc_landed"), 64 * (l + 1))
            job = ("misc", l)
            b = open_job(pe, job)
            for k in range(KD):
                mm = nc.tensor.matmul(ps[:, b, :], wmisc[:, k, :], hT[:, k, :], start=(k == 0), stop=(k == KD - 1))
            mm.then_inc(*done("job_done", job))
            for name in ("fq", "fk"):
                for c in range(2):
                    pe_t_job(pe, (name, l, c), w1(l, name, c), hT, SEQ)
            for c in range(2):
                pe_n_job(pe, ("fv", l, c), w1(l, "fv", c), hT, NT)
            pe.wait_ge(*emptied(("fk", l, 1)))
            pe.wait_ge(*emptied(("fv", l, 1)))
            pe.wait_ge(sem("fcum_landed"), 64 * (l + 1))
            pe.wait_ge(*at("fox_rows", l))
            narrow_jobs(pe)
            pe_softmax(pe, ("fox", l, 0))
            wide_jobs()
            for name in ("sq", "sk"):
                for c in range(2):
                    pe_t_job(pe, (name, l, c), w1(l, name, c), hT, SEQ)
            for c in range(2):
                pe_n_job(pe, ("sv", l, c), w1(l, "sv", c), hT, NT)
            pe.wait_ge(*emptied(("sk", l, 1)))
            pe.wait_ge(*emptied(("sv", l, 1)))
            pe.wait_ge(*at("zero_rows", ("sb", l)))
            narrow_jobs(pe)
            pe_stick(pe, l)
            wide_jobs()
            pe_t_job(pe, ("ckv", l, 0), w1(l, "ckv", 0), hT, SEQ)
            for c in range(2):
                pe_t_job(pe, ("cq", l, c), w1(l, "cq", c), hT, SEQ)
            job = ("kvsum", l)
            b = open_job(pe, job)
            pe.wait_ge(*at("squares", (l, 2)))
            nc.tensor.matmul(ps[:, b, :], cst(C_ONE), sqT[:, 2, :], start=True, stop=True).then_inc(*done("job_done", job))
            job = ("qsum", l)
            b = open_job(pe, job)
            pe.wait_ge(*at("squares", (l, 1)))
            for c in range(2):
                mm = nc.tensor.matmul(ps[:, b, :], cst(C_ONE), sqT[:, c, :], start=(c == 0), stop=(c == 1))
            mm.then_inc(*done("job_done", job))
            job = ("krr", l)
            b = open_job(pe, job)
            pe.wait_ge(*emptied(("misc", l)))
            nc.tensor.matmul(ps[0:KROWS, b, :], const[0:KROWS, C_ROTM:C_ROTM + KROWS], kr[0:KROWS, :], start=True,
                             stop=True).then_inc(*done("job_done", job))
            pe.wait_ge(*at("rms_ready", (l, "kv")))
            pe.wait_ge(sem("mla_landed"), 32 * (l + 1))
            for hh in range(HEADS):
                job = ("mk", l, hh)
                b = open_job(pe, job)
                nc.tensor.matmul(ps[0:HD, b, :], wkvup[:, hh * P:hh * P + HD], ckvT, start=True,
                                 stop=True).then_inc(*done("job_done", job))
            for half in range(2):
                job = ("mv", l, half)
                b = open_job(pe, job)
                for t in range(2):
                    o = (2 * half + t) * P
                    mm = nc.tensor.matmul(ps[:, b, t * 256:(t + 1) * 256], ckvT[:, o:o + P],
                                          wkvup[:, :].rearrange("p (h x) -> p h x", h=HEADS)[:, :, HD:2 * HD],
                                          start=True, stop=True)
                mm.then_inc(*done("job_done", job))
            pe.wait_ge(*at("rms_ready", (l, "q")))
            for hh in range(HEADS):
                job = ("mqu", l, hh)
                b = open_job(pe, job)
                for c in range(2):
                    mm = nc.tensor.matmul(ps[0:MLA_QK, b, :], wqup[:, c, hh * MLA_QK:(hh + 1) * MLA_QK], cqT[:, c, :],
                                          start=(c == 0), stop=(c == 1))
                mm.then_inc(*done("job_done", job))
            for hh in range(HEADS):
                job = ("mqr", l, hh)
                b = open_job(pe, job)
                pe.wait_ge(*emptied(("mqu", l, hh)))
                nc.tensor.matmul(ps[0:KROWS, b, :], const[0:KROWS, C_ROTM:C_ROTM + KROWS], qz[0:KROWS, hh, :],
                                 start=True, stop=True).then_inc(*done("job_done", job))
            for lj in mods_of_mla(l):
                pe_mod(pe, lj)
                pe_mod_turn(pe, lj)
            pe.wait_ge(*at("kr_spread", l))
            pe.wait_ge(*at("mla_q", (l, HEADS - 1)))
            pe.wait_ge(*emptied(("mv", l, 1)))
            narrow_jobs(pe)
            pe_softmax(pe, ("mla", l, 0))
            wide_jobs()
            for c in range(2):
                pe_t_job(pe, ("mq", l, c), w1(l, "mq", c), hT, SEQ)
            for c in range(2):
                pe_t_job(pe, ("memk", l, c), w1(l, "mk", c), hcT, CTX)
            for c in range(2):
                pe_n_job(pe, ("memv", l, c), w1(l, "mv", c), hcT, NC)
            pe.wait_ge(*emptied(("memk", l, 1)))
            pe.wait_ge(*emptied(("memv", l, 1)))
            pe.wait_ge(*at("zero_rows", ("mem", l)))
            narrow_jobs(pe)
            pe_softmax(pe, ("mem", l, 0))
            wide_jobs()
            pe.wait_ge(*emptied(("pv", ("mem", l, 0), NT - 1, 1)))
            st = ("first", l)
            nxt = ("plain", l + 1) if l + 1 < DEPTH else ("pre", 0)
            for t in range(NT):
                pe_out(pe, st, mixT, t, [w1(l, "wo", c) for c in range(8)], t == 0, t == NT - 1)
                if t > 0:
                    pe_head(pe, nxt, t - 1)
            pe_mod(pe, mod_of_tail(l))
            pe_mod_turn(pe, mod_of_tail(l))
            pe_head(pe, nxt, NT - 1)

        def pe_rope2(pe, l, name, c):
            job = ("rot", l, name, c)
            b = open_job(pe, job)
            pe.wait_ge(*emptied((name, l, c, 0)))
            nc.tensor.matmul(ps[:, b, :], cst(C_ROTA), rt1, start=True, stop=True).then_inc(*done("job_done", job))

        def streams(l, name):
            return (0, 1) if l == 0 or name in ("ak", "av", "bk", "bv") else (0,)

        def pe_conv_stat(pe, l, r, name):
            n = (SEQ, CTX)[r]
            ready, src = {"cmean": ("conv_done", acc), "cvar": ("conv_sq", csq)}[name]
            job = (name, l, r)
            b = open_job(pe, job)
            pe.wait_ge(*at(ready, (l, r)))
            for c in range(2):
                mm = nc.tensor.matmul(ps[:, b, 0:n], cst(C_ONE), src[:, c, 0:n], start=(c == 0), stop=(c == 1))
            mm.then_inc(*done("job_done", job))

        def pe_second_block(pe, l):
            ht = (hT, hcT)

            def q_job(c):
                pe_t_job(pe, ("aq", l, c, 0), w1(2 + l, "aq", c), hT, SEQ, last=l > 0)
                pe_rope2(pe, l, "aq", c)
                if l == 0:
                    pe_t_job(pe, ("aq", l, c, 1), w1(2 + l, "aq", c), hcT, CTX)

            def conv_in(r):
                for name in ("a", "g"):
                    for c in range(2):
                        pe_t_job(pe, (name, l, c, r), w1(2 + l, name, c), ht[r], (SEQ, CTX)[r],
                                 last=r == streams(l, "a")[-1])

            wide_jobs()
            pe.wait_ge(*emptied(("turn", ("pre", l), NT - 1, 1)))
            conv_in(0)
            for t in range(NT, NT + NC):
                pe_head(pe, ("pre", l), t)
            pe.wait_ge(*emptied(("turn", ("pre", l), NT + NC - 1, 1)))
            if l == 0:
                conv_in(1)
            for r in (0, 1):
                pe_n_job(pe, ("av", l, 0, r), w1(2 + l, "av", 0), ht[r], (NT, NC)[r], last=r == 1)
            for c in range(2):
                pe_t_job(pe, ("bk", l, c, 1), w1(2 + l, "bk", c), hcT, CTX, last=False)
            for c in range(2):
                pe_n_job(pe, ("bv", l, c, 1), w1(2 + l, "bv", c), hcT, NC, last=False)
            if l == 0:
                pe_conv_stat(pe, l, 0, "cmean")
            pe_t_job(pe, ("ak", l, 0, 0), w1(2 + l, "ak", 0), hT, SEQ, last=False)
            pe_rope2(pe, l, "ak", 0)
            if l == 0:
                pe_conv_stat(pe, l, 0, "cvar")
            pe_t_job(pe, ("ak", l, 0, 1), w1(2 + l, "ak", 0), hcT, CTX)
            for r in streams(l, "aq"):
                for c in range(2):
                    pe_t_job(pe, ("aq", l, c, r), w1(2 + l, "aq", c), ht[r], (SEQ, CTX)[r],
                             last=r == streams(l, "aq")[-1])
            if l > 0:
                pe_conv_stat(pe, l, 0, "cmean")
            pe_rope2(pe, l, "aq", 0)
            if l > 0:
                pe_conv_stat(pe, l, 0, "cvar")
            pe_rope2(pe, l, "aq", 1)
            for part in range(2):
                if part == 1:
                    wide_jobs()
                    if l == 0:
                        pe_conv_stat(pe, l, 1, "cmean")
                    q_job(2)
                    if l == 0:
                        pe_conv_stat(pe, l, 1, "cvar")
                    q_job(3)
                pe.wait_ge(*at("roped", (l, "aq", 2 * part + 1)))
                pe.wait_ge(*at("zero_rows", ("second", l)))
                if l == 0:
                    pe.wait_ge(*emptied(("aq", l, 2 * part + 1, 1)))
                pe.wait_ge(*emptied(("bv", l, 1, 1)))
                narrow_jobs(pe)
                pe_softmax(pe, ("wa", l, part))
            wide_jobs()
            for c in range(2):
                pe_t_job(pe, ("bk", l, c, 0), w1(2 + l, "bk", c), hT, SEQ)
            for c in range(2):
                pe_n_job(pe, ("bv", l, c, 0), w1(2 + l, "bv", c), hT, NT)
            for c in range(2):
                for r in streams(l, "bq"):
                    pe_t_job(pe, ("bq", l, c, r), w1(2 + l, "bq", c), ht[r], (SEQ, CTX)[r], last=r == streams(l, "bq")[-1])
            pe.wait_ge(*emptied(("bq", l, 1, streams(l, "bq")[-1])))
            narrow_jobs(pe)
            pe_softmax(pe, ("nb", l, 0))
            wide_jobs()
            pe_gate_rows(pe, l, 0)
            pe.wait_ge(*at("conv_out", (l, streams(l, "a")[-1])))
            lastu = ("cb", l, 0) if l == 0 else ("nb", l, 0)
            pe.wait_ge(*emptied(("pv", lastu, (NC if l == 0 else NT) - 1, 1)))
            st = ("mixer", l)
            tiles = list(range(NT + NC)) if l == 0 else list(range(NT))
            tiles = mixer_tiles(l)
            rt = ("route", l)
            staggered(tiles, [
                (lambda t: pe_out(pe, st, mixcT if ctile(t) else mixT, t, [w1(2 + l, "wo", c) for c in range(8)],
                                  t == tiles[0], t == tiles[-1]), 0),
                (lambda t: pe_head(pe, rt, t), 1),
                (lambda t: pe_route(pe, rt, t), 2),
                (lambda t: pe_affinities(pe, rt, t), 3)])
            pe_gate_rows(pe, l, 1)
            job = ("topT", l)
            b = open_job(pe, job)
            rows = CAP + (CAP_C if l == 0 else 0)
            pe.wait_ge(*at("topk", l))
            nc.tensor.transpose(ps[0:rows, b, 0:EXPERTS], topv[:, 0:rows], ident[0:EXPERTS, 0:EXPERTS])
            nc.tensor.transpose(ps[0:rows, b, EXPERTS:2 * EXPERTS], topf[:, 0:rows],
                                ident[0:EXPERTS, 0:EXPERTS]).then_inc(*done("job_done", job))
            pe_experts(pe, l)

        ROUNDS = EXPERTS // 2

        def at_round(name, event, i, back=0):
            per = known.get(("per_round", event[0], name), 1)
            return sem(name), i * per + max(known.get((name, event), 1) - back * per, -back * per + 1)

        EXPERT_SLOTS = 3 * KD
        spare = ([mixT[:, 2 * c:2 * c + 2, :].rearrange("p a b -> p (a b)") for c in range(4)]
                 + [mixcT[:, 4 * c:4 * c + 4, :].rearrange("p a b -> p (a b)") for c in range(2)]
                 + [v[:, :, :].rearrange("p a b -> p (a b)"), probs[:, D:2 * D]]
                 + [t[:, 2 * c:2 * c + 2, :].rearrange("p a b -> p (a b)") for t in (qz, kz) for c in range(2)])

        def expert_slot(s):
            return ring[:, s, :] if s < RING else spare[s - RING]

        def slot_count(s, l, u, i):
            return i * 32 + (banks.get(("moe_slot", l, s), 0) + 16 * (u + 1))

        def rounds(eng, l, body):
            before = dict(counts)
            body(0)
            per = {k: counts[k] - before.get(k, 0) for k in counts if counts[k] != before.get(k, 0)}
            frozen[0] = True
            with eng.Fori(1, ROUNDS) as i:
                body(i)
            frozen[0] = False
            for k, n in per.items():
                marks[("per_round", l, k)] = n
                counts[k] = before.get(k, 0) + ROUNDS * n

        def settled(eng, count):
            return count if first_round(count) else eng.compute_val(count)

        def first_round(i):
            return isinstance(i, int)

        def pe_experts(pe, l):
            rows = CAP + (CAP_C if l == 0 else 0)
            G, U, GC, UC, Y, YC = 2, 3, 4, 5, 6, 7

            def turn_xs(i, u, event):
                for hb in range(2):
                    for c in range(4):
                        mm = nc.tensor.transpose(ps[:, hb, c * 96:c * 96 + rows],
                                                 xs[0:rows, (u + 1) % 2, (4 * hb + c) * P:(4 * hb + c + 1) * P],
                                                 ident[0:rows, 0:rows])
                    mm.then_inc(*done("xs_turned", (l, event, hb)))

            def product(i, u, m, lhs, dst, dstc, last_event):
                for k in range(KD):
                    s = KD * m + k
                    pe.wait_ge(sem(f"slot{s}"), slot_count(s, l, u, i))
                    w = expert_slot(s)
                    for half in range(2):
                        mm = nc.tensor.matmul(ps[64 * half:64 * half + 64, dst, :], lhs[:, k, 0:CAP],
                                              w[:, half * 512:(half + 1) * 512], start=(k == 0), stop=(k == KD - 1),
                                              skip_group_check=True)
                    if l == 0:
                        for q in range(4):
                            mm = nc.tensor.matmul(ps[32 * q:32 * q + 32, dstc, 0:256], lhs[:, k, CAP:CAP + CAP_C],
                                                  w[:, q * 256:(q + 1) * 256], start=(k == 0), stop=(k == KD - 1),
                                                  skip_group_check=True)
                    mm.then_inc(*done("moe_k", (l, u, m, k)))

            pe.wait_ge(*emptied(("topT", l)))
            pe.wait_ge(*emptied(("grow", l, 1, 1 if l == 0 else 0, 1)))
            pe.wait_ge(sem("gathered0"), known.get(("gather", l, 0), 16))
            turn_xs(0, -1, "first")

            def body(i):
                for u in range(2):
                    b = u
                    if u == 0:
                        if first_round(i):
                            pe.wait_ge(*at("xsT_act", (l, "first")))
                            pe.wait_ge(*at("xsT_dve", (l, "first")))
                        else:
                            pe.wait_ge(*at_round("xsT_act", (l, 1), i, 1))
                            pe.wait_ge(*at_round("xsT_dve", (l, 1), i, 1))
                    else:
                        pe.wait_ge(*at_round("xsT_act", (l, 0), i))
                        pe.wait_ge(*at_round("xsT_dve", (l, 0), i))
                    product(i, u, 0, xsT[:, b, :, :], G, GC, None)
                    product(i, u, 1, xsT[:, b, :, :], U, UC, None)
                    count = settled(pe, gather_count(l, u, i))
                    pe.wait_ge(*emptied(("topT", l)))
                    pe.wait_ge(sem(f"gathered{(u + 1) % 2}"), count)
                    turn_xs(i, u, u)
                    pe.wait_ge(*at_round("hid", (l, u, 0), i))
                    for c in range(4):
                        mm = nc.tensor.transpose(ps[:, G, c * P:(c + 1) * P], hid[:, c * P:(c + 1) * P], ident)
                    mm.then_inc(*done("hid_turned", (l, u, 0)))
                    if l == 0:
                        pe.wait_ge(*at_round("hid", (l, u, 1), i))
                        for c in range(2):
                            mm = nc.tensor.transpose(ps[:, GC, c * P:(c + 1) * P], hidc[:, c * P:(c + 1) * P], ident)
                        mm.then_inc(*done("hid_turned", (l, u, 1)))
                    pe.wait_ge(*at_round("hidT", (l, u), i))
                    if not (first_round(i) and u == 0):
                        pe.wait_ge(*at_round("ye_copied", (l, 1 - u), i, 1 - u))
                    product(i, u, 2, hidT, Y, YC, None)

            rounds(pe, l, body)

        def gather_count(l, u, i):
            return i * 16 + (known.get(("gather", l, 1 - u), 16) + 16 * u)

        def experts_act(act, l):
            rows = CAP + (CAP_C if l == 0 else 0)
            G, U, GC, UC, Y, YC = 2, 3, 4, 5, 6, 7

            def mod_cols(c, r):
                return (modc[:, l, 32 + c, r:r + 1], modc[:, l, 24 + c, r:r + 1])

            def modulate(i, u, event):
                for c in range(4):
                    for r in range(2 if l == 0 else 1):
                        o, n = ((0, CAP), (CAP, CAP_C))[r]
                        sc, sh = mod_cols(c, r)
                        ins = nc.scalar.activation(xsT[:, (u + 1) % 2, c, o:o + n], ps[:, 0, c * 96 + o:c * 96 + o + n],
                                                   ACT.Identity, bias=sh, scale=sc)
                ins.then_inc(*done("xsT_act", (l, event)))

            act.wait_ge(*at("xs_turned", (l, "first", 0)))
            modulate(0, -1, "first")

            def body(i):
                for u in range(2):
                    act.wait_ge(*at_round("moe_k", (l, u, 0, KD - 1), i))
                    if not (first_round(i) and u == 0):
                        act.wait_ge(*at_round("hid", (l, 1 - u, 1 if l == 0 else 0), i, 1 - u))
                    nc.scalar.activation(sig, ps[:, G, :], ACT.Silu).then_inc(*done("gated", (l, u, 0)))
                    if l == 0:
                        nc.scalar.activation(sigc, ps[:, GC, 0:256], ACT.Silu).then_inc(*done("gated", (l, u, 1)))
                    act.wait_ge(*at_round("xs_turned", (l, u, 0), i))
                    modulate(i, u, u)
                    act.wait_ge(*at_round("moe_k", (l, u, 2, KD - 1), i))
                    if not first_round(i):
                        act.wait_ge(sem("scattered"), scatter_count(l, u, i, 1))
                    elif l > 0:
                        act.wait_ge(sem("scattered"), known.get(("scatter_base", l), 0))
                    for half in range(2):
                        ins = nc.scalar.activation(ye[0:CAP, u, half * 512:(half + 1) * 512],
                                                   ps[64 * half:64 * half + 64, Y, :], ACT.Copy)
                    if l == 0:
                        for q in range(4):
                            ins = nc.scalar.activation(ye[CAP:rows, u, q * 256:(q + 1) * 256],
                                                       ps[32 * q:32 * q + 32, YC, 0:256], ACT.Copy)
                    ins.then_inc(*done("ye_copied", (l, u)))

            rounds(act, l, body)

        def scatter_count(l, u, i, back=0):
            return i * 32 + (known.get(("scatter_base", l), 0) + 16 * (u + 1) - 32 * back)

        def experts_dve(dve, l):
            rows = CAP + (CAP_C if l == 0 else 0)
            G, U, GC, UC, Y, YC = 2, 3, 4, 5, 6, 7

            def modulate(i, u, event):
                for c in range(4, 8):
                    for r in range(2 if l == 0 else 1):
                        o, n = ((0, CAP), (CAP, CAP_C))[r]
                        ins = nc.vector.tensor_scalar(xsT[:, (u + 1) % 2, c, o:o + n],
                                                      ps[:, 1, (c - 4) * 96 + o:(c - 4) * 96 + o + n],
                                                      modc[:, l, 32 + c, r:r + 1], modc[:, l, 24 + c, r:r + 1],
                                                      ALU.mult, ALU.add)
                ins.then_inc(*done("xsT_dve", (l, event)))

            dve.wait_ge(*at("xs_turned", (l, "first", 1)))
            modulate(0, -1, "first")
            dve.wait_ge(*emptied(("grow", l, 1, 1 if l == 0 else 0, 1)))

            def body(i):
                for u in range(2):
                    dve.wait_ge(*at_round("moe_k", (l, u, 1, KD - 1), i))
                    dve.wait_ge(*at_round("gated", (l, u, 0), i))
                    nc.vector.tensor_tensor(hid, sig, ps[:, U, :], ALU.mult).then_inc(*done("hid", (l, u, 0)))
                    if l == 0:
                        dve.wait_ge(*at_round("gated", (l, u, 1), i))
                        nc.vector.tensor_tensor(hidc, sigc, ps[:, UC, 0:256], ALU.mult).then_inc(*done("hid", (l, u, 1)))
                    dve.wait_ge(*at_round("hid_turned", (l, u, 0), i))
                    dst = hidT.rearrange("p (a j) t -> p j a t", a=2)[:, :, :, 0:CAP]
                    src = ps[:, G, :].rearrange("p (j a t) -> p j a t", j=4, a=2)
                    ins = nc.vector.tensor_copy(dst, src)
                    if l == 0:
                        dve.wait_ge(*at_round("hid_turned", (l, u, 1), i))
                        dst = hidT.rearrange("p (a j) t -> p j a t", a=4)[:, :, :, CAP:CAP + CAP_C]
                        src = ps[:, GC, 0:256].rearrange("p (j a t) -> p j a t", j=2, a=4)
                        ins = nc.vector.tensor_copy(dst, src)
                    ins.then_inc(*done("hidT", (l, u)))
                    dve.wait_ge(*at_round("xs_turned", (l, u, 1), i))
                    modulate(i, u, u)
                    dve.wait_ge(*at_round("ye_copied", (l, u), i))
                    e = 2 * i + u
                    for r in range(2 if l == 0 else 1):
                        R = (slice(0, CAP), slice(CAP, rows))[r]
                        g = gates[R, e:e + 1] if first_round(i) else gates[R, bass.ds(e, 1)]
                        ins = nc.vector.scalar_tensor_tensor(ye[R, u, :], ye[R, u, :], g, grow[R, r, :], ALU.mult, ALU.mult)
                    ins.then_inc(*done("ye", (l, u)))

            rounds(dve, l, body)

        def experts_pool(pool, l, load_rows):
            rows = CAP + (CAP_C if l == 0 else 0)
            src = a["x_norm"][l]
            dst = a["y_moe"][l]

            def gather(event, e, b):
                col_e = idx[0:rows, e:e + 1] if first_round(e) else idx[0:rows, bass.ds(e, 1)]
                nc.gpsimd.tensor_copy(idx_at[b][0:rows, :], col_e).then_inc(*done("idx_at", (l, event)))

            def start(b, w):
                count = settled(pool, w[1])
                pool.wait_ge(*at("idx", l))
                pool.wait_ge(w[0], count)
                nc.gpsimd.indirect_dma_start(
                    out=xs[0:rows, b, :], out_offset=None, in_=src,
                    in_offset=bass.IndirectOffsetOnAxis(ap=idx_at[b][0:rows, 0:1], axis=0)).then_inc(sem(f"gathered{b}"), 16)

            pool.wait_ge(*at("idx", l))
            pool.wait_ge(*at_last_store(l))
            for b in range(2):
                gather(("first", b), b, b)
                start(b, at("idx_at", (l, ("first", b))))
                base = counts.get(f"gathers{b}", 0)
                marks[("gather", l, b)] = base + 16
                counts[f"gathers{b}"] = base + 16 + 16 * ROUNDS
            marks[("scatter_base", l)] = l * 16 * EXPERTS
            load_rows(("experts", l), a["ln2_g_2"][l], a["ln2_b_2"][l])

            def body(i):
                for u in range(2):
                    e = 2 * i + u
                    if u == 1:
                        pool.wait_ge(*at_round("xs_turned", (l, 0, 1), i))
                    elif first_round(i):
                        pool.wait_ge(*at("xs_turned", (l, "first", 1)))
                    else:
                        pool.wait_ge(*at_round("xs_turned", (l, 1, 1), i, 1))
                    gather(u, e + 2, u)
                    start(u, at_round("idx_at", (l, u), i))
                    if not (first_round(i) and u == 0):
                        pool.wait_ge(sem("scattered"), scatter_count(l, 1 - u, i, 1 - u))
                    col_e = idx[0:rows, e:e + 1] if first_round(e) else idx[0:rows, bass.ds(e, 1)]
                    nc.gpsimd.tensor_copy(idx_to[u][0:rows, :], col_e).then_inc(*done("idx_to", (l, u)))
                    scaled, count = at_round("ye", (l, u), i)
                    count = settled(pool, count)
                    copied, count_to = at_round("idx_to", (l, u), i)
                    count_to = settled(pool, count_to)
                    pool.wait_ge(sem("residual_stored"), 16 * sum(map(tiles_of, range(l + 1))))
                    pool.wait_ge(copied, count_to)
                    pool.wait_ge(scaled, count)
                    nc.gpsimd.indirect_dma_start(
                        out=dst, out_offset=bass.IndirectOffsetOnAxis(ap=idx_to[u][0:rows, 0:1], axis=0),
                        in_=ye[0:rows, u, :], in_offset=None, compute_op=ALU.add).then_inc(sem("scattered"), 16)

            rounds(pool, l, body)

        def at_last_store(l):
            return sem("x_norm_stored"), known.get(("x_norm_stored_all", l), 16)

        def dve_norm(dve, event, src, dst, rows=None, final=None):
            k = ln_count[0] % 2
            ln_count[0] += 1
            st = col[:, 16 + 12 * k:28 + 12 * k].rearrange("p (c s) -> p c s", c=2)
            mv = col[:, 40 + 2 * k:42 + 2 * k]
            rstd = col[:, 46 + k:47 + k]
            for c in range(2):
                ins = nc.vector.bn_stats(st[:, c, :], src[:, c * 512:(c + 1) * 512])
            ins.then_inc(*done("dve_step", ("st", event)))
            dve.wait_ge(*at("dve_step", ("st", event)))
            nc.vector.bn_aggr(mv, col[:, 16 + 12 * k:28 + 12 * k]).then_inc(*done("variance", event))
            if rows is not None:
                dve.wait_ge(*at("variance", event))
                nc.vector.scalar_tensor_tensor(dst, src, mv[:, 0:1], rows[0], ALU.subtract, ALU.mult)
            dve.wait_ge(*at("deviation", event))
            nc.vector.reciprocal(rstd, col[:, 44 + k:45 + k]).then_inc(*done("dve_step", ("ri", event)))
            dve.wait_ge(*at("dve_step", ("ri", event)))
            if rows is not None:
                ins = nc.vector.scalar_tensor_tensor(dst, dst, rstd, rows[1], ALU.mult, ALU.add)
            else:
                ins = nc.vector.tensor_scalar(dst, src, mv[:, 0:1], rstd, ALU.subtract, ALU.mult)
            ins.then_inc(*done(*(final or ("dve_step", ("b", event)))))

        ln_count = [0]
        ln_count_act = [0]

        def act_root(act, event, eps):
            k = ln_count_act[0] % 2
            ln_count_act[0] += 1
            act.wait_ge(*at("variance", event))
            nc.scalar.activation(col[:, 44 + k:45 + k], col[:, 41 + 2 * k:42 + 2 * k], ACT.Sqrt,
                                 bias=epsc(eps)).then_inc(*done("deviation", event))

        def epsc(eps):
            return {LN_EPS: col[:, 50:51], LN_EPS_2: col[:, 51:52]}[eps]

        def rows_of(stage):
            return lnrow[:, 0, :], lnrow[:, 1, :]

        def dve_out(dve, st, t):
            kind, l = st
            for half in range(2):
                o = slice(half * 512, half * 512 + 512)
                job = ("out", st, t, half)
                dve.wait_ge(*at("job_done", job))
                src = ps[:, bank_of(job), :]
                if kind == "first":
                    nc.vector.scalar_tensor_tensor(res(t)[:, o], res(t)[:, o], ALPHA, src, ALU.mult,
                                                   ALU.add).then_inc(*done("evac_dve", job))
                else:
                    dve_gated(dve, job, t, o, src, l)
            if t == (0 if kind == "first" else mixer_tiles(l)[0]):
                dve.wait_ge(sem("rows_landed"), rows_landed(st))
            if kind == "first":
                dve.wait_ge(*at("evac_dve", ("out", st, t, 1)))
            else:
                dve.wait_ge(*at("dve_step", ("res", st, t, 1)))

        def dve_gated(dve, job, t, o, src, l):
            if job[3] == 1:
                dve.wait_ge(*at("dve_step", ("res", job[1], t, 0)))
            elif t != mixer_tiles(l)[0]:
                dve.wait_ge(*at("dve_step", ("res", job[1], mixer_tiles(l)[mixer_tiles(l).index(t) - 1], 1)))
            r = 1 if ctile(t) else 0
            if t == mixer_tiles(l)[0] and job[3] == 0:
                rr = 1 if l == 0 else 0
                dve.wait_ge(*emptied(("grow", l, 0, rr, 1)))
            nc.vector.tensor_tensor(rot_t[:, :], grow[:, r, o], src, ALU.mult).then_inc(*done("evac_dve", job))
            dve.wait_ge(*at("evac_dve", job))
            nc.vector.scalar_tensor_tensor(res(t)[:, o], res(t)[:, o], ALPHA, rot_t[:, :], ALU.mult,
                                           ALU.add).then_inc(*done("dve_step", ("res", job[1], t, job[3])))

        def rows_landed(st):
            return known.get(("rows_landed", st), 32)

        def dve_head(dve, st, t):
            kind, l = st
            if kind == "plain":
                return
            seen = xt_users[0]
            if len(seen) >= 2:
                pst, pt = seen[-2]
                dve.wait_ge(*at("job_done", ("turn", pst, pt, 1)))
                if pst[0] == "route":
                    dve.wait_ge(sem("x_norm_stored"), known.get(("x_norm_stored", pst, pt), 16))
            seen.append((st, t))
            dve_norm(dve, (st, t), res(t), xt[:, t % 2, :], final=("tile_ready", (st, t)))

        xt_users = [[]]

        def act_head(act, st, t, root=True):
            kind, l = st
            if kind != "plain" and root:
                act_root(act, (st, t), LN_EPS_2)
            for half in range(2):
                job = ("turn", st, t, half)
                act.wait_ge(*at("job_done", job))
                src = ps[:, bank_of(job), :].rearrange("p (c t) -> p c t", c=4)
                tl = t - NT if ctile(t) else t
                ts = slice(tl * P, (tl + 1) * P)
                if kind == "plain":
                    dst = hcT if ctile(t) else hT
                    ins = nc.scalar.activation(dst[:, 4 * half:4 * half + 4, ts], src, ACT.Copy)
                else:
                    if half == 0 and (t == 0 or kind == "route" and t == mixer_tiles(l)[0]):
                        act.wait_ge(*at("modulation", (l, 9)))
                        act.wait_ge(*at("evac_dve", ("modT", l, 11)))
                    r = 1 if ctile(t) else 0
                    o = 0 if kind == "pre" else 24
                    for c in range(4):
                        cc = 4 * half + c
                        if kind == "pre":
                            dst = (hcT if ctile(t) else hT)[:, cc, ts]
                        else:
                            dst = h2t[:, t % 2, cc, :]
                        ins = nc.scalar.activation(dst, src[:, c, :], ACT.Identity, bias=modc[:, l, o + cc, r:r + 1],
                                                   scale=modc[:, l, o + 8 + cc, r:r + 1])
                ins.then_inc(*done("evac_act", job))

        def act_route(act, st, t):
            job = ("route", st, t)
            act.wait_ge(*at("job_done", job))
            act.wait_ge(*at("route_max", (st, t)))
            nc.scalar.activation(aff[:, t, :], ps[:, bank_of(job), 0:EXPERTS], ACT.Exp, bias=col[:, 10 + t % 2:11 + t % 2],
                                 accum_out=col[:, 12 + t % 2:13 + t % 2]).then_inc(*done("evac_act", job))

        def act_affinities(act, st, t):
            job = ("affT", st, t)
            act.wait_ge(*at("job_done", job))
            nc.scalar.activation(affT[:, t * P:(t + 1) * P], ps[0:EXPERTS, bank_of(job), 0:P],
                                 ACT.Copy).then_inc(*done("evac_act", job))

        def dve_route(dve, st, t):
            job = ("route", st, t)
            dve.wait_ge(*at("job_done", job))
            nc.vector.tensor_reduce(col[:, 10 + t % 2:11 + t % 2], ps[:, bank_of(job), 0:EXPERTS], AX, ALU.max,
                                    negate=True).then_inc(*done("route_max", (st, t)))
            dve.wait_ge(*at("evac_act", job))
            nc.vector.reciprocal(col[:, 14 + t % 2:15 + t % 2],
                                 col[:, 12 + t % 2:13 + t % 2]).then_inc(*done("dve_step", ("rr", st, t)))
            dve.wait_ge(*at("dve_step", ("rr", st, t)))
            nc.vector.tensor_scalar(aff[:, t, :], aff[:, t, :], col[:, 14 + t % 2:15 + t % 2], None,
                                    ALU.mult).then_inc(*done("aff", (st, t)))

        def dve_topk(dve, l, r):
            o, n, s0, cap = ((0, SEQ, 0, CAP), (SEQ, CTX, CAP, CAP_C))[r]
            dve.wait_ge(*at("evac_act", ("affT", ("route", l), (NT, NT + NC)[r] - 1)))
            cur = affT[:, o:o + n]
            for g in range(cap // 8):
                s = slice(s0 + 8 * g, s0 + 8 * g + 8)
                nc.vector.max(topv[:, s], cur).then_inc(*done("dve_step", ("mx", l, r, g)))
                dve.wait_ge(*at("dve_step", ("mx", l, r, g)))
                nc.vector.max_index(topi[:, s], topv[:, s], cur).then_inc(*done("dve_step", ("mi", l, r, g)))
                if g + 1 < cap // 8:
                    dve.wait_ge(*at("dve_step", ("mi", l, r, g)))
                    nc.vector.match_replace(cur, topv[:, s], cur, -1.0).then_inc(*done("dve_step", ("mr", l, r, g)))
                    dve.wait_ge(*at("dve_step", ("mr", l, r, g)))

        def dve_slots(dve, l):
            for r in streams(l, "a"):
                dve.wait_ge(*at("dve_step", ("mi", l, r, (CAP, CAP_C)[r] // 8 - 1)))
            ins = nc.vector.tensor_copy(topf[:, 0:CAP], topi[:, 0:CAP])
            if l == 0:
                ins = nc.vector.tensor_scalar(topf[:, CAP:CAP + CAP_C], topi[:, CAP:CAP + CAP_C], float(SEQ), None, ALU.add)
            ins.then_inc(*done("topk", l))
            job = ("topT", l)
            rows = CAP + (CAP_C if l == 0 else 0)
            b = bank_of(job)
            dve.wait_ge(*at("job_done", job))
            nc.vector.tensor_copy(gates[0:rows, 0:EXPERTS], ps[0:rows, b, 0:EXPERTS])
            nc.vector.tensor_copy(idxf[0:rows, 0:EXPERTS],
                                  ps[0:rows, b, EXPERTS:2 * EXPERTS]).then_inc(*done("evac_dve", job))
            dve.wait_ge(*at("evac_dve", job))
            nc.vector.tensor_copy(idx[0:rows, 0:EXPERTS], idxf[0:rows, 0:EXPERTS])
            nc.vector.tensor_copy(idx[0:rows, EXPERTS:EXPERTS + 2], idxf[0:rows, 0:2]).then_inc(*done("idx", l))

        def dve_moe_out(dve, l):
            st = ("experts", l)
            tiles = list(range(NT + NC)) if l == 0 else list(range(NT))
            for t in tiles:
                dve.wait_ge(sem(f"y_landed{t}"), 16 * (l + 1))
                if t == 0:
                    dve.wait_ge(sem("rows_landed"), rows_landed(st))
                last = l == DEPTH - 1
                dve_norm(dve, (st, t), res(t), res(t), rows_of(st),
                         final=("out_ready", t) if last else ("dve_step", ("b", (st, t))))
                if not last:
                    dve.wait_ge(*at("dve_step", ("b", (st, t))))
                    dve_head(dve, ("pre", l + 1), t)

        def act_moe_out(act, l):
            st = ("experts", l)
            tiles = list(range(NT + NC)) if l == 0 else list(range(NT))
            for t in tiles:
                act_root(act, (st, t), LN_EPS_2)
                if l < DEPTH - 1 and not ctile(t):
                    act_head(act, ("pre", l + 1), t)
                elif l < DEPTH - 1:
                    act_root(act, (("pre", l + 1), t), LN_EPS_2)

        def dve_softmax(dve, ph, scale_mix, between=None):
            us = joined(ph)

            def top(u):
                dve.wait_ge(*at("scores", u))
                if seq[u] >= UC:
                    dve.wait_ge(*at("probs", by_seq[seq[u] - UC]))
                if u[0][0] == "nb":
                    (_, l, _), t, hh = u
                    dve.wait_ge(*at("bias_ready", (l, hh)))
                    o = (7 - 2 * t) * 64
                    logits = s_psum(u)[:, 0:SEQ]
                    nc.vector.tensor_tensor(logits, logits, bias_of(hh)[:, o:o + SEQ],
                                            ALU.add).then_inc(*done("dve_step", ("nb", u)))
                    dve.wait_ge(*at("dve_step", ("nb", u)))
                if not has_sink(u):
                    nc.vector.tensor_reduce(nmax(u), s_psum(u), AX, ALU.max, negate=True).then_inc(*done("nmax", u))
                else:
                    nc.vector.tensor_reduce(rmax(u), s_psum(u), AX, ALU.max).then_inc(*done("dve_step", ("mx", u)))
                    dve.wait_ge(*at("dve_step", ("mx", u)))
                    nc.vector.tensor_scalar(nmax(u), rmax(u), sink_col(u), -1.0, ALU.max,
                                            ALU.mult).then_inc(*done("nmax", u))

            def norm(u):
                dve.wait_ge(*at("probs", u))
                total = rsum(u)
                if has_sink(u):
                    dve.wait_ge(*at("sink_exp", u))
                    nc.vector.tensor_tensor(rmax(u), rsum(u), esink(u), ALU.add).then_inc(*done("dve_step", ("su", u)))
                    dve.wait_ge(*at("dve_step", ("su", u)))
                    total = rmax(u)
                nc.vector.reciprocal(rinv(u), total).then_inc(*done("dve_step", ("ri", u)))
                dve.wait_ge(*at("dve_step", ("ri", u)))
                p = p_sbuf(u)
                nc.vector.tensor_scalar(p, p, rinv(u), None, ALU.mult).then_inc(*done("probs_normed", u))

            def leave(u):
                job = pair_job(u)
                dve.wait_ge(*at("job_done", job))
                src = ps[:, bank_of(job), 0:P]
                dst = mix_out(u)
                if scale_mix:
                    ins = nc.vector.tensor_tensor(dst, dst, src, ALU.mult)
                else:
                    ins = nc.vector.tensor_copy(dst, src)
                ins.then_inc(*done("evac_dve", job))

            lag = lag_of(ph)
            for i in range(len(us) + lag + 2):
                if i < len(us):
                    top(us[i])
                if 1 <= i <= len(us):
                    norm(us[i - 1])
                if between and i < len(us):
                    between(i)
                if i >= lag + 2 and us[i - lag - 2][2] % 2:
                    leave(us[i - lag - 2])
                if mods_at(ph, i, 3):
                    dve_mod(dve, mods_at(ph, i, 3))

        def act_softmax(act, ph):
            us = joined(ph)

            def expo(u):
                n = seq[u]
                act.wait_ge(*at("nmax", u))
                w = before(u, probs_span)
                if w is not None:
                    act.wait_ge(*at("turned", (w, len(chunks_of(w)) - 1)))
                nc.scalar.activation(p_sbuf(u), s_psum(u), ACT.Exp, bias=nmax(u),
                                     accum_out=rsum(u)).then_inc(*done("probs", u))
                if has_sink(u):
                    nc.scalar.activation(esink(u), sink_col(u), ACT.Exp, bias=nmax(u)).then_inc(*done("sink_exp", u))

            def copy(u):
                n = seq[u]
                for c, blocks in enumerate(chunks_of(u)):
                    act.wait_ge(*at("turned", (u, c)))
                    if c == 0 and n >= 2:
                        w = by_seq[n - 2]
                        act.wait_ge(*at("job_done", pair_job(w if w[2] % 2 else (w[0], w[1], w[2] + 1))))
                    m = turn_at[(u, c)]
                    nc.scalar.activation(probsT[:, n % 2, blocks[0]:blocks[-1] + 1, :],
                                         ps[:, 4 + m % 2, 0:len(blocks) * P].rearrange("p (b q) -> p b q", q=P),
                                         ACT.Copy).then_inc(*done("probsT_ready", (u, c)))

            lag = lag_of(ph)
            for i in range(len(us) + lag):
                if i >= lag:
                    copy(us[i - lag])
                if i < len(us):
                    expo(us[i])
                if mods_at(ph, i, 1):
                    act_mod(act, mods_at(ph, i, 1))

        def act_heads(act, name, l, c, r, dst, scale=1.0, heads=True):
            job = (name, l, c, r) if r is not None else (name, l, c)
            n = CTX if r == 1 or name == "memk" else SEQ
            act.wait_ge(*at("job_done", job))
            for e in range(2):
                ins = nc.scalar.activation(dst[0:HD, 2 * (c % 2) + e, 0:n], ps[e * HD:(e + 1) * HD, bank_of(job), 0:n],
                                           ACT.Copy, scale=scale)
            ins.then_inc(*done("evac_act", job))

        def act_values(act, job, dst, tiles):
            act.wait_ge(*at("job_done", job))
            nc.scalar.activation(dst, ps[:, bank_of(job), 0:tiles * P].rearrange("p (t n) -> p t n", t=tiles),
                                 ACT.Copy).then_inc(*done("evac_act", job))

        def act_mod(act, lj):
            job = ("mod",) + lj
            act.wait_ge(*at("job_done", job))
            nc.scalar.activation(modrow[:, :], ps[:, bank_of(job), 0:P], ACT.Copy).then_inc(*done("evac_act", job))

        def dve_mod(dve, lj):
            l, j = lj
            job = ("modT", l, j)
            dve.wait_ge(*at("job_done", job))
            src = ps[:, bank_of(job), 0:P].rearrange("p (q x) -> p q x", q=4)
            for r in range(2):
                o = V_BMOD + 48 * l + 4 * j
                dst = modc[:, l, 4 * j:4 * j + 4, r]
                ins = nc.vector.tensor_tensor(dst, src[:, :, r], vec[:, o:o + 4], ALU.add)
            ins.then_inc(*done("evac_dve", job))
            dve.wait_ge(*at("evac_dve", job))
            if j // 2 in (1, 4):
                nc.vector.tensor_scalar(modc[:, l, 4 * j:4 * j + 4, :], modc[:, l, 4 * j:4 * j + 4, :], 1.0, None,
                                        ALU.add).then_inc(*done("modulation", (l, j)))

        def gate_diagonals(eng, engine, l, which):
            for r in range(2 if l == 0 else 1):
                for c in range(8):
                    if c >= 2:
                        eng.wait_ge(*diag_free(l, which, r, c - 2))
                    elif r > 0:
                        eng.wait_ge(*diag_free(l, which, r - 1, 6 + c))
                    g = modc[:, l, (16, 40)[which] + c, r:r + 1]
                    engine.tensor_scalar(modrow_diag(c), ident, g, None, ALU.mult).then_inc(*done(f"diag{which}", (l, which, r, c)))

        def act_gate_rows(act, l, which):
            for r in range(2 if l == 0 else 1):
                for half in range(2):
                    job = ("grow", l, which, r, half)
                    act.wait_ge(*at("job_done", job))
                    nc.scalar.activation(grow[:, r, half * 512:(half + 1) * 512], ps[:, bank_of(job), :],
                                         ACT.Copy).then_inc(*done("evac_act", job))

        def act_first_block(act, l):
            for c in range(8):
                job = ("gate", l, c)
                act.wait_ge(*at("job_done", job))
                nc.scalar.activation(mixT[:, c, :], ps[:, bank_of(job), :], ACT.Silu).then_inc(*done("evac_act", job))
                if l == 0 and c == 3:
                    for t in (NT, NT + 1):
                        act_head(act, ("plain", -1), t)
            nc.scalar.preload_act_table_set("natural_log_exp_and_others")
            job = ("misc", l)
            b = bank_of(job)
            act.wait_ge(*at("job_done", job))
            nc.scalar.activation(flog[0:HEADS, :], ps[0:HEADS, b, :], ACT.Identity,
                                 bias=vec[0:HEADS, V_BF + l:V_BF + l + 1]).then_inc(*done("f_logit", l))
            nc.scalar.activation(kr[HD:KROWS, :], ps[HD:KROWS, b, :], ACT.Copy).then_inc(*done("evac_act", job))
            act.wait_ge(*at("f_logit", l))
            nc.scalar.activation(fls[0:HEADS, 0, :], flog[0:HEADS, :], ACT.Abs).then_inc(*done("act_step", ("f0", l)))
            act.wait_ge(*at("act_step", ("f0", l)))
            nc.scalar.activation(fls[0:HEADS, 0, :], fls[0:HEADS, 0, :], ACT.Exp, scale=-1.0).then_inc(*done("act_step", ("f1", l)))
            act.wait_ge(*at("act_step", ("f1", l)))
            nc.scalar.activation(fls[0:HEADS, 0, :], fls[0:HEADS, 0, :], ACT.Ln, bias=one_col[0:HEADS]).then_inc(*done("f_log", l))
            for c in range(2):
                act_heads(act, "fq", l, c, None, qz, HD ** -0.5)
            for c in range(2):
                act_heads(act, "fk", l, c, None, kz)
            for c in range(2):
                act_values(act, ("fv", l, c), v[:, :, c * P:(c + 1) * P], NT)
            act_softmax(act, ("fox", l, 0))
            for c in range(2):
                act_heads(act, "sq", l, c, None, qz, HD ** -0.5)
            for c in range(2):
                act_heads(act, "sk", l, c, None, kz)
            for c in range(2):
                act_values(act, ("sv", l, c), v[:, :, c * P:(c + 1) * P], NT)
            act_stick(act, l)
            job = ("ckv", l, 0)
            act.wait_ge(*at("job_done", job))
            nc.scalar.activation(ckvT, ps[:, bank_of(job), :], ACT.Copy).then_inc(*done("evac_act", job))
            for c in range(2):
                job = ("cq", l, c)
                act.wait_ge(*at("job_done", job))
                nc.scalar.activation(cqT[:, c, :], ps[:, bank_of(job), :], ACT.Copy).then_inc(*done("evac_act", job))
            for i, (job, r) in enumerate(((("kvsum", l), KVR), (("qsum", l), QR))):
                act.wait_ge(*at("job_done", job))
                nc.scalar.activation(rms[:, i, :], ps[:, bank_of(job), :], ACT.Sqrt, scale=1.0 / r,
                                     bias=col[:, 51:52]).then_inc(*done("evac_act", job))
            for hh in range(HEADS):
                job = ("mk", l, hh)
                act.wait_ge(*at("job_done", job))
                nc.scalar.activation(kz[0:HD, hh, :], ps[0:HD, bank_of(job), :], ACT.Copy).then_inc(*done("evac_act", job))
            for half in range(2):
                job = ("mv", l, half)
                act.wait_ge(*at("job_done", job))
                nc.scalar.activation(v[:, 2 * half:2 * half + 2, :], ps[:, bank_of(job), :].rearrange("p (t n) -> p t n", t=2),
                                     ACT.Copy).then_inc(*done("evac_act", job))
            for hh in range(HEADS):
                job = ("mqu", l, hh)
                act.wait_ge(*at("job_done", job))
                nc.scalar.activation(qz[0:MLA_QK, hh, :], ps[0:MLA_QK, bank_of(job), :], ACT.Copy,
                                     scale=MLA_QK ** -0.5).then_inc(*done("evac_act", job))
            for lj in mods_of_mla(l):
                act_mod(act, lj)
            act_softmax(act, ("mla", l, 0))
            for c in range(2):
                act_heads(act, "mq", l, c, None, qz, HD ** -0.5)
            for c in range(2):
                act_heads(act, "memk", l, c, None, kz)
            for c in range(2):
                act_values(act, ("memv", l, c), v[:, 0:NC, c * P:(c + 1) * P], NC)
            act_softmax(act, ("mem", l, 0))
            st = ("first", l)
            nxt = ("plain", l + 1) if l + 1 < DEPTH else ("pre", 0)
            for t in range(NT):
                act_root(act, (st, t), LN_EPS)
                if t == NT - 1:
                    act_mod(act, mod_of_tail(l))
                act_head(act, nxt, t)

        one_col = col[:, 52:53]

        def act_stick(act, l):
            def softplus(n):
                hh, i = sb_unit(n)
                w = SEQ - i * P
                act.wait_ge(*at("sb_logits", (l, n)))
                if n >= 2:
                    act.wait_ge(*at("softplus_raw", (l, n - 2)))
                t = sbt[:, n % 2, 0:w]
                nc.scalar.activation(t, ps[:, n % 4, 0:w], ACT.Abs).then_inc(*done("act_step", ("s0", l, n)))
                act.wait_ge(*at("act_step", ("s0", l, n)))
                nc.scalar.activation(t, t, ACT.Exp, scale=-1.0).then_inc(*done("act_step", ("s1", l, n)))
                act.wait_ge(*at("act_step", ("s1", l, n)))
                nc.scalar.activation(t, t, ACT.Ln, bias=one_col).then_inc(*done("sb_log", (l, n)))

            def weights(n):
                hh, i = sb_unit(n)
                w = SEQ - i * P
                act.wait_ge(*at("sb_logw", (l, n)))
                if hh >= 2 and i == 3:
                    act.wait_ge(*at("job_done", ("sbpv", l, hh // 2 - 1)))
                nc.scalar.activation(sbw[:, hh % 2, sp_off[i]:sp_off[i] + w], ps[:, n % 4, 0:w],
                                     ACT.Exp).then_inc(*done("sb_exp", (l, n)))

            for n in range(4 * HEADS + 2):
                if n < 4 * HEADS:
                    softplus(n)
                if n >= 2:
                    weights(n - 2)
                if mods_at(("sb", l), n, 1):
                    act_mod(act, mods_at(("sb", l), n, 1))

        def dve_stick(dve, l):
            def softplus(n):
                hh, i = sb_unit(n)
                w = SEQ - i * P
                dve.wait_ge(*at("sb_log", (l, n)))
                if hh >= 2:
                    dve.wait_ge(*at("sb_logw", (l, 4 * (hh - 1) - 1)))
                o = sp_off[i]
                nc.vector.scalar_tensor_tensor(sp[:, hh % 2, o:o + w], ps[:, n % 4, 0:w], 0.0, sbt[:, n % 2, 0:w],
                                               ALU.max, ALU.add).then_inc(*done("softplus_raw", (l, n)))
                dve.wait_ge(*at("softplus_raw", (l, n)))
                nc.vector.tensor_tensor(sp[:, hh % 2, o:o + P], sp[:, hh % 2, o:o + P], cst(C_STRICT),
                                        ALU.mult).then_inc(*done("softplus", (l, n)))

            def weights(n):
                hh, i = sb_unit(n)
                o = sp_off[i]
                dve.wait_ge(*at("sb_exp", (l, n)))
                nc.vector.tensor_tensor(sbw[:, hh % 2, o:o + P], sbw[:, hh % 2, o:o + P], cst(C_BIG),
                                        ALU.min).then_inc(*done("sb_weights", (l, n)))

            def leave(p):
                job = ("sbpv", l, p)
                dve.wait_ge(*at("job_done", job))
                nc.vector.tensor_tensor(mixT[:, 2 + p, :], mixT[:, 2 + p, :], ps[:, bank_of(job), :],
                                        ALU.mult).then_inc(*done("evac_dve", job))

            for n in range(4 * HEADS + 3):
                if n < 4 * HEADS:
                    softplus(n)
                if 2 <= n < 4 * HEADS + 2:
                    weights(n - 2)
                if n >= 3 and sb_unit(n - 3) in ((1, 0), (3, 0)):
                    leave(sb_unit(n - 3)[0] // 2)
                if mods_at(("sb", l), n, 3):
                    dve_mod(dve, mods_at(("sb", l), n, 3))

        def dve_first_block(dve, l):
            if l == 0:
                dve.wait_ge(sem("vec_landed"), 16)
                dve.wait_ge(sem("const_landed"), 16)
                dve.wait_ge(sem("const_rest_landed"), 16)
            dve.wait_ge(*at("f_log", l))
            nc.vector.scalar_tensor_tensor(fls[0:HEADS, 0, :], flog[0:HEADS, :], 0.0, fls[0:HEADS, 0, :], ALU.min,
                                           ALU.subtract).then_inc(*done("dve_step", ("lf", l)))
            dve.wait_ge(*at("dve_step", ("lf", l)))
            nc.vector.tensor_tensor_scan(fls[0:HEADS, 1, :], const[0:HEADS, C_ONE:C_ONE + 1].broadcast_to([HEADS, SEQ]), fls[0:HEADS, 0, :], 0.0, ALU.mult,
                                         ALU.subtract).then_inc(*done("fcum", l))
            dve.wait_ge(*at("evac_act", ("gate", l, 7)))
            dve_softmax(dve, ("fox", l, 0), True)
            dve_stick(dve, l)
            for i, (name, job) in enumerate((("kv", ("kvsum", l)), ("q", ("qsum", l)))):
                dve.wait_ge(*at("evac_act", job))
                nc.vector.reciprocal(rms[:, i, :], rms[:, i, :]).then_inc(*done("dve_step", ("rm", l, i)))
                dve.wait_ge(*at("dve_step", ("rm", l, i)))
                if name == "kv":
                    g = vec[:, V_MKVG + l:V_MKVG + l + 1]
                    dve.wait_ge(*at("squares", (l, 2)))
                    ins = nc.vector.scalar_tensor_tensor(ckvT, ckvT, g, rms[:, i, :], ALU.mult, ALU.mult)
                else:
                    dve.wait_ge(*at("squares", (l, 1)))
                    for c in range(2):
                        g = vec[:, V_MQG + 2 * l + c:V_MQG + 2 * l + c + 1]
                        ins = nc.vector.scalar_tensor_tensor(cqT[:, c, :], cqT[:, c, :], g, rms[:, i, :], ALU.mult, ALU.mult)
                ins.then_inc(*done("rms_ready", (l, name)))
            R = slice(HD, KROWS)
            cos, sin = cst(C_COS, SEQ, R), cst(C_SIN, SEQ, R)
            for name, job, dst in [("k", ("krr", l), kr[R, :])] + [(hh, ("mqr", l, hh), qz[R, hh, :]) for hh in range(HEADS)]:
                dve.wait_ge(*at("job_done", job))
                nc.vector.tensor_tensor(rope_t[R, :], sin, ps[R, bank_of(job), :], ALU.mult).then_inc(*done("evac_dve", job))
                nc.vector.tensor_tensor(dst, dst, cos, ALU.mult).then_inc(*done("dve_step", ("rc", l, name)))
                dve.wait_ge(*at("evac_dve", job))
                dve.wait_ge(*at("dve_step", ("rc", l, name)))
                nc.vector.tensor_tensor(dst, dst, rope_t[R, :], ALU.add).then_inc(
                    *(done("kr_roped", l) if name == "k" else done("mla_q", (l, name))))
                dve.wait_ge(*(at("kr_roped", l) if name == "k" else at("mla_q", (l, name))))
            for lj in mods_of_mla(l):
                dve_mod(dve, lj)
            dve_softmax(dve, ("mla", l, 0), True)
            dve_softmax(dve, ("mem", l, 0), True)
            st = ("first", l)
            nxt = ("plain", l + 1) if l + 1 < DEPTH else ("pre", 0)
            for t in range(NT):
                dve_out(dve, st, t)
                dve_norm(dve, (st, t), res(t), res(t), rows_of(st),
                         final=("tile_ready", (nxt, t)) if nxt[0] == "plain" else None)
                if nxt[0] != "plain":
                    dve.wait_ge(*at("dve_step", ("b", (st, t))))
                dve_head(dve, nxt, t)
            dve_mod(dve, mod_of_tail(l))

        def act_conv_in(act, l):
            if l > 0:
                act.wait_ge(*at("dve_step", ("b", (("experts", l - 1), NT + NC - 1))))
            for c in range(2):
                job = ("a", l, c, 0)
                act.wait_ge(*at("job_done", job))
                nc.scalar.activation(hp[:, c, HALO:HALO + SEQ], ps[:, bank_of(job), :], ACT.Copy).then_inc(*done("evac_act", job))
            for c in range(2):
                job = ("g", l, c, 0)
                act.wait_ge(*at("job_done", job))
                nc.scalar.activation((glu, csd)[c], ps[:, bank_of(job), :], ACT.Sigmoid).then_inc(*done("evac_act", job))

        def dve_gated_unit(dve, l, r):
            n, src = ((SEQ, hp), (CTX, hpc))[r]
            dve.wait_ge(*at("halo", (l, r)))
            for c in range(2):
                dve.wait_ge(*at("evac_act", ("g", l, c, r)))
                x = src[:, c, HALO:HALO + n]
                g = gluc[:, c, :] if r else (glu, csd)[c]
                nc.vector.tensor_tensor(x, x, g, ALU.mult).then_inc(*done("glu", (l, r, c)))

        def dve_taps(dve, l, r, taps):
            n, src = ((SEQ, hp), (CTX, hpc))[r]
            for j in taps:
                for c in range(2):
                    o = V_CONVW + (2 * l + c) * TAPS + j
                    wj = vec[:, o:o + 1]
                    x = src[:, c, j:j + n]
                    if j == 0:
                        dve.wait_ge(*at("glu", (l, r, c)))
                        bo = V_CONVB + 2 * l + c
                        ins = nc.vector.tensor_scalar(acc[:, c, 0:n], x, wj, vec[:, bo:bo + 1], ALU.mult, ALU.add)
                    else:
                        dve.wait_ge(*at("dve_step", ("cv", l, r, j - 1, c)))
                        ins = nc.vector.scalar_tensor_tensor(acc[:, c, 0:n], x, wj, acc[:, c, 0:n], ALU.mult, ALU.add)
                    if j == TAPS - 1 and c == 1:
                        ins.then_inc(*done("conv_done", (l, r)))
                    else:
                        ins.then_inc(*done("dve_step", ("cv", l, r, j, c)))

        def dve_conv_centre(dve, l, r):
            n = (SEQ, CTX)[r]
            job = ("cmean", l, r)
            dve.wait_ge(*at("job_done", job))
            for c in range(2):
                ins = nc.vector.scalar_tensor_tensor(acc[:, c, 0:n], ps[:, bank_of(job), 0:n], -1.0 / 256, acc[:, c, 0:n],
                                                     ALU.mult, ALU.add)
            ins.then_inc(*done("evac_dve", job))
            dve.wait_ge(*at("evac_dve", job))
            nc.vector.tensor_tensor(csq[:, :, 0:n], acc[:, :, 0:n], acc[:, :, 0:n], ALU.mult).then_inc(*done("conv_sq", (l, r)))

        def dve_conv_scale(dve, l, r):
            n = (SEQ, CTX)[r]
            dve.wait_ge(*at("evac_act", ("cvar", l, r)))
            nc.vector.reciprocal(csd[:, 0:n], csd[:, 0:n]).then_inc(*done("dve_step", ("cr", l, r)))
            dve.wait_ge(*at("dve_step", ("cr", l, r)))
            for c in range(2):
                ins = nc.vector.tensor_tensor(acc[:, c, 0:n], acc[:, c, 0:n], csd[:, 0:n], ALU.mult)
            ins.then_inc(*done("conv_normed", (l, r)))

        def act_conv_root(act, l, r):
            n = (SEQ, CTX)[r]
            job = ("cvar", l, r)
            act.wait_ge(*at("job_done", job))
            nc.scalar.activation(csd[:, 0:n], ps[:, bank_of(job), 0:n], ACT.Sqrt, scale=1.0 / 256,
                                 bias=col[:, 51:52]).then_inc(*done("evac_act", job))

        def act_conv_out(act, l, r):
            n = (SEQ, CTX)[r]
            act.wait_ge(*at("conv_normed", (l, r)))
            dst = (mixT, mixcT)[r]
            for c in range(2):
                ins = nc.scalar.activation(dst[:, 6 + c, 0:n], acc[:, c, 0:n], ACT.Silu,
                                           scale=vec[:, V_CLNG + 2 * l + c:V_CLNG + 2 * l + c + 1],
                                           bias=vec[:, V_CLNB + 2 * l + c:V_CLNB + 2 * l + c + 1])
            ins.then_inc(*done("conv_out", (l, r)))

        def act_rope_in(act, l, name, c):
            job = (name, l, c, 0)
            act.wait_ge(*at("job_done", job))
            prev = {("aq", 0): ("ak", 0)}.get((name, c), (name, c - 1))
            if name == "aq":
                act.wait_ge(*at("roped", (l,) + prev))
            nc.scalar.activation(rt1, ps[:, bank_of(job), :], ACT.Copy,
                                 scale=HD ** -0.5 if name == "aq" else 1.0).then_inc(*done("evac_act", job))

        def dve_rope(dve, l, name, c):
            job = ("rot", l, name, c)
            dve.wait_ge(*at("job_done", job))
            nc.vector.tensor_tensor(rot_t[:, :], axial[:, SEQ:2 * SEQ], ps[:, bank_of(job), :],
                                    ALU.mult).then_inc(*done("evac_dve", job))
            nc.vector.tensor_tensor(rt1, rt1, axial[:, 0:SEQ], ALU.mult).then_inc(*done("dve_step", ("ro", l, name, c)))
            dve.wait_ge(*at("evac_dve", job))
            dve.wait_ge(*at("dve_step", ("ro", l, name, c)))
            dst = qz if name == "aq" else kz
            for e in range(2):
                R = slice(e * HD, (e + 1) * HD)
                ins = nc.vector.tensor_tensor(dst[0:HD, 2 * (c % 2) + e, :], rt1[R, :], rot_t[R, :], ALU.add)
            ins.then_inc(*done("roped", (l, name, c)))
            dve.wait_ge(*at("roped", (l, name, c)))

        axial = const[:, C_COS:C_COS + 2 * SEQ]

        def act_second_block(act, l):
            def q_job(c):
                act_rope_in(act, l, "aq", c)
                if l == 0:
                    act_heads(act, "aq", l, c, 1, QC, HD ** -0.5)

            act_conv_in(act, l)
            for t in range(NT, NT + NC):
                act_head(act, ("pre", l), t, root=False)
            if l == 0:
                act_conv_in_ctx(act, l)
            act_values(act, ("av", l, 0, 0), v[:, :, 0:P], NT)
            act_values(act, ("av", l, 0, 1), VC[:, :, 0:P], NC)
            for c in range(2):
                act_ctx_keys(act, l, ("bk", l, c, 1), 2 + 2 * c)
            for c in range(2):
                act_values(act, ("bv", l, c, 1), VC[:, :, P + c * P:P + (c + 1) * P], NC)
            act_rope_in(act, l, "ak", 0)
            if l == 0:
                act_conv_root(act, l, 0)
            act_ctx_keys(act, l, ("ak", l, 0, 1), 0)
            if l == 0:
                act_conv_out(act, l, 0)
                act_rope_in(act, l, "aq", 0)
                for c in range(2):
                    act_heads(act, "aq", l, c, 1, QC, HD ** -0.5)
            else:
                act_rope_in(act, l, "aq", 0)
                act_conv_root(act, l, 0)
            act_rope_in(act, l, "aq", 1)
            if l > 0:
                act_conv_out(act, l, 0)
            for part in range(2):
                if part == 1:
                    q_job(2)
                    if l == 0:
                        act_conv_root(act, l, 1)
                    q_job(3)
                    if l == 0:
                        act_conv_out(act, l, 1)
                act_softmax(act, ("wa", l, part))
            for c in range(2):
                act_heads(act, "bk", l, c, 0, kz)
            for c in range(2):
                act_values(act, ("bv", l, c, 0), v[:, :, c * P:(c + 1) * P], NT)
            for c in range(2):
                for r in streams(l, "bq"):
                    act_heads(act, "bq", l, c, r, (qz, QC)[r], HD ** -0.5)
            act_softmax(act, ("nb", l, 0))
            act_gate_rows(act, l, 0)
            st = ("mixer", l)
            tiles = list(range(NT + NC)) if l == 0 else list(range(NT))
            rt = ("route", l)

            def roots(t):
                act_root(act, (st, t), LN_EPS_2)
                act_root(act, (rt, t), LN_EPS_2)

            staggered(mixer_tiles(l), [
                (lambda t: act_head(act, rt, t, root=False), 1),
                (roots, 0),
                (lambda t: act_route(act, rt, t), 2),
                (lambda t: act_affinities(act, rt, t), 3)])
            act_gate_rows(act, l, 1)
            experts_act(act, l)
            act_moe_out(act, l)

        def act_conv_in_ctx(act, l):
            for c in range(2):
                job = ("a", l, c, 1)
                act.wait_ge(*at("job_done", job))
                nc.scalar.activation(hpc[:, c, HALO:HALO + CTX], ps[:, bank_of(job), 0:CTX], ACT.Copy).then_inc(*done("evac_act", job))
            for c in range(2):
                job = ("g", l, c, 1)
                act.wait_ge(*at("job_done", job))
                nc.scalar.activation(gluc[:, c, :], ps[:, bank_of(job), 0:CTX], ACT.Sigmoid).then_inc(*done("evac_act", job))

        mixcf = mixcT[:, :, :].rearrange("p a b -> p (a b)")
        hpc = mixcf[:, 0:2 * (CTX + 2 * HALO)].rearrange("p (c n) -> p c n", c=2)
        gluc = mixcf[:, 576:1088].rearrange("p (c n) -> p c n", c=2)

        def act_ctx_keys(act, l, job, first):
            act.wait_ge(*at("job_done", job))
            for e in range(2):
                ins = nc.scalar.activation(KC[0:HD, first + e, :], ps[e * HD:(e + 1) * HD, bank_of(job), 0:CTX], ACT.Copy)
            ins.then_inc(*done("evac_act", job))

        def dve_second_block(dve, l):
            if l == 0:
                dve.wait_ge(sem("axial_landed"), 16)
            dve_gated_unit(dve, l, 0)
            dve_taps(dve, l, 0, range(TAPS))
            early = 16

            def context_taps(i):
                dve_taps(dve, l, 1, range(early + i, min(early + i + 1, TAPS)))

            if l == 0:
                dve_conv_centre(dve, l, 0)
                dve_rope(dve, l, "ak", 0)
                dve_conv_scale(dve, l, 0)
                dve.wait_ge(*at("conv_out", (l, 0)))
                dve_gated_unit(dve, l, 1)
                dve_taps(dve, l, 1, range(early))
                dve_rope(dve, l, "aq", 0)
                dve_rope(dve, l, "aq", 1)
            else:
                dve_rope(dve, l, "ak", 0)
                dve_conv_centre(dve, l, 0)
                dve_rope(dve, l, "aq", 0)
                dve_conv_scale(dve, l, 0)
                dve_rope(dve, l, "aq", 1)

            for part in range(2):
                if part == 1:
                    if l == 0:
                        dve_conv_centre(dve, l, 1)
                    dve_rope(dve, l, "aq", 2)
                    if l == 0:
                        dve_conv_scale(dve, l, 1)
                    dve_rope(dve, l, "aq", 3)
                dve_softmax(dve, ("wa", l, part), False, context_taps if l == 0 and part == 0 else None)
            dve_softmax(dve, ("nb", l, 0), False)
            gate_diagonals(dve, nc.vector, l, 0)
            st = ("mixer", l)
            tiles = list(range(NT + NC)) if l == 0 else list(range(NT))
            def residual(t):
                dve_out(dve, st, t)
                dve_norm(dve, (st, t), res(t), res(t), rows_of(st))
                dve.wait_ge(*at("dve_step", ("b", (st, t))))
                dve_head(dve, ("route", l), t)

            staggered(mixer_tiles(l), [(residual, 0), (lambda t: dve_route(dve, ("route", l), t), 2),
                                       (lambda t: t == NT + NC - 1 and dve_topk(dve, l, 1), 4)])
            dve_topk(dve, l, 0)
            dve_slots(dve, l)
            experts_dve(dve, l)
            dve_moe_out(dve, l)

        for name in sem_names:
            sem(name)
        for s in range(EXPERT_SLOTS):
            sem(f"slot{s}")
        block = ctx.enter_context(nc.Block())

        @block.tensor
        def _(pe):
            pe.wait_ge(sem("const_landed"), 16)
            pe.wait_ge(*at("cond", 0))
            wide_jobs()
            for t in range(NT):
                pe_head(pe, ("plain", 0), t)
            for l in range(DEPTH):
                pe_first_block(pe, l)
            for l in range(DEPTH):
                if l > 0:
                    for t in range(NT):
                        pe_head(pe, ("pre", l), t)
                pe_second_block(pe, l)

        @block.scalar
        def _(act):
            act.dma_start(vec[:, :], a["vec"]).then_inc(sem("vec_landed"), 16)
            act.wait_ge(sem("vec_landed"), 16)
            act.wait_ge(*at("cond_zero", 0))
            nc.scalar.activation(cond[:, :, 0:2], vec[:, V_COND:V_COND + 2 * KD].rearrange("p (k r) -> p k r", r=2),
                                 ACT.Silu).then_inc(*done("cond", 0))
            act.wait_ge(*at("columns", 0))
            for t in range(NT):
                act_root(act, (("ln_in", 0), t), LN_EPS)
                act_head(act, ("plain", 0), t)
            for t in (NT, NT + 1):
                act_root(act, (("mem_ln", 0), t), LN_EPS)
            for l in range(DEPTH):
                act_first_block(act, l)
            for t in (NT, NT + 1):
                act_root(act, (("pre", 0), t), LN_EPS_2)
            for l in range(DEPTH):
                act_second_block(act, l)

        @block.vector
        def _(dve):
            nc.vector.memset(col[:, 50:51], LN_EPS)
            nc.vector.memset(col[:, 51:52], LN_EPS_2)
            nc.vector.memset(col[:, 52:53], 1.0).then_inc(*done("columns", 0))
            dve.wait_ge(*at("columns", 0))
            for st, nxt, tiles, rows in ((("ln_in", 0), ("plain", 0), range(NT), lnrow), (("mem_ln", 0), ("plain", -1), (NT, NT + 1), grow)):
                for t in tiles:
                    dve.wait_ge(sem(f"x_landed{t}"), 16)
                    if t in (0, NT):
                        dve.wait_ge(sem("in_rows_landed" if t == 0 else "mem_rows_landed"), 32)
                    dve_norm(dve, (st, t), res(t), res(t), (rows[:, 0, :], rows[:, 1, :]), final=("tile_ready", (nxt, t)))
            for l in range(DEPTH):
                dve_first_block(dve, l)
            for t in (NT, NT + 1):
                dve.wait_ge(sem("ctx_landed"), 16 * NC)
                dve_head(dve, ("pre", 0), t)
            for l in range(DEPTH):
                dve_second_block(dve, l)

        @block.gpsimd
        def _(pool):
            nc.gpsimd.memset(cond[:, :, :], 0.0).then_inc(*done("cond_zero", 0))
            nc.gpsimd.memset(kr[:, :], 0.0)
            rows_n = [0]

            def load_rows(st, g, b):
                pool.dma_start(lnrow[:, 0, :], g.partition_broadcast(P)).then_inc(sem("rows_landed"), 16)
                pool.dma_start(lnrow[:, 1, :], b.partition_broadcast(P)).then_inc(sem("rows_landed"), 16)
                rows_n[0] += 32
                marks[("rows_landed", st)] = rows_n[0]

            n_stored = [0]
            HR = slice(HD, KROWS)
            for l in range(DEPTH):
                if l > 0:
                    pool.wait_ge(*at("job_done", ("mv", l - 1, 1)))
                    pool.wait_ge(*at("job_done", ("mqu", l - 1, HEADS - 1)))
                if l == 0:
                    pool.wait_ge(*at("job_done", ("turn", ("plain", -1), NT + NC - 1, 1)))
                    nc.gpsimd.memset(wmisc, 0.0).then_inc(*done("misc_zero", 0))
                    pool.wait_ge(*at("misc_zero", 0))
                cols = w_cols(a["w_in"], l, O_FL, HEADS)
                for k in range(2):
                    kk = slice(4 * k, 4 * k + 4)
                    pool.dma_start(wmisc[:, kk, 0:HEADS], cols[:, kk, :]).then_inc(sem("misc_landed"), 16)
                    pool.dma_start(wmisc[:, kk, HD:KROWS], w_cols(a["w_in"], l, O_KR, ROPE)[:, kk, :]).then_inc(sem("misc_landed"), 16)
                pool.dma_start(wqup, a["w_mla_q_up"][l].rearrange("(k p) c -> p k c", p=P)).then_inc(sem("mla_landed"), 16)
                pool.dma_start(wkvup[:, :], a["w_mla_kv_up"][l]).then_inc(sem("mla_landed"), 16)
                if l > 0:
                    pool.wait_ge(*at("scores", (("mem", l - 1, 0), NT - 1, HEADS - 1)))
                nc.gpsimd.memset(qz[HR, :, :], 0.0).then_inc(*done("rows_zeroed", (l, 0)))
                nc.gpsimd.memset(kz[HR, :, :], 0.0).then_inc(*done("rows_zeroed", (l, 1)))
                pool.wait_ge(*at("rows_zeroed", (l, 1)))
                nc.gpsimd.memset(qz[HD:HD + 1, :, :], 1.0).then_inc(*done("fox_rows", l))
                pool.wait_ge(*at("fcum", l))
                for hh in range(HEADS):
                    pool.dma_start(kz[HD:HD + 1, hh, :], fls[hh:hh + 1, 1, :]).then_inc(sem("fcum_landed"), 16)
                pool.wait_ge(*at("scores", (("fox", l, 0), NT - 1, HEADS - 1)))
                pool.wait_ge(sem("fcum_landed"), 64 * (l + 1))
                nc.gpsimd.memset(qz[HR, :, :], 0.0)
                nc.gpsimd.memset(kz[HR, :, :], 0.0).then_inc(*done("zero_rows", ("sb", l)))
                pool.wait_ge(*at("evac_act", ("ckv", l, 0)))
                nc.gpsimd.tensor_tensor(sqT[:, 2, :], ckvT, ckvT, ALU.mult).then_inc(*done("squares", (l, 2)))
                for c in range(2):
                    pool.wait_ge(*at("evac_act", ("cq", l, c)))
                    nc.gpsimd.tensor_tensor(sqT[:, c, :], cqT[:, c, :], cqT[:, c, :], ALU.mult).then_inc(*done("squares", (l, c)))
                pool.wait_ge(*at("kr_roped", l))
                for hh in range(HEADS):
                    ins = nc.gpsimd.tensor_copy(kz[HR, hh, :], kr[HR, :])
                ins.then_inc(*done("kr_spread", l))
                pool.wait_ge(*at("scores", (("mla", l, 0), NT - 1, HEADS - 1)))
                nc.gpsimd.memset(qz[HR, :, :], 0.0)
                nc.gpsimd.memset(kz[HR, :, :], 0.0).then_inc(*done("zero_rows", ("mem", l)))
                load_rows(("first", l), a["ln_g"][l], a["ln_b"][l])
            for l in range(DEPTH):
                if l == 0:
                    pool.wait_ge(*at("mla_q", (DEPTH - 1, HEADS - 1)))
                    pool.dma_start(axial, a["axial"]).then_inc(sem("axial_landed"), 16)
                    pool.wait_ge(*at("job_done", ("memv", DEPTH - 1, 1)))
                    for t in range(NC):
                        pool.dma_start(hc[:, t, :], a["ctx_2"][t * P:(t + 1) * P, :]).then_inc(sem("ctx_landed"), 16)
                pool.dma_start(wr[:, :, :], a["w_router_2"][l].rearrange("(k p) e -> p k e", p=P)).then_inc(sem("router_landed"), 16)
                pool.wait_ge(*at("job_done", ("turn", ("pre", l), NT + NC - 1, 1)))
                nc.gpsimd.memset(hp[:, :, 0:HALO], 0.0)
                nc.gpsimd.memset(hp[:, :, HALO + SEQ:SEQ + 2 * HALO], 0.0).then_inc(*done("halo", (l, 0)))
                if l == 0:
                    nc.gpsimd.memset(hpc[:, :, 0:HALO], 0.0)
                    nc.gpsimd.memset(hpc[:, :, HALO + CTX:CTX + 2 * HALO], 0.0).then_inc(*done("halo", (l, 1)))
                pool.wait_ge(*at("halo", (l, streams(l, "a")[-1])))
                nc.gpsimd.memset(QC[HR, :, :], 0.0)
                nc.gpsimd.memset(KC[HR, :, :], 0.0)
                nc.gpsimd.memset(qz[HR, :, :], 0.0)
                nc.gpsimd.memset(kz[HR, :, :], 0.0).then_inc(*done("zero_rows", ("second", l)))
                for hh in range(HEADS):
                    if hh == 0:
                        pool.wait_ge(*at("conv_out", (l, streams(l, "a")[-1])))
                    b = bias_of(hh)
                    pool.dma_start(b[0:64, 0:960], a["nat_bias_2"][l, hh]).then_inc(sem("bias_landed"), 16)
                    pool.dma_start(b[64:P, 64:1024], a["nat_bias_2"][l, hh]).then_inc(sem("bias_landed"), 16)
                    pool.wait_ge(sem("bias_landed"), 32 * (HEADS * l + hh + 1))
                    pool.wait_ge(*at("zero_rows", ("second", l)))
                    rows14 = b[:, 64:960].rearrange("p (s k) -> p s k", k=64)
                    nc.gpsimd.tensor_tensor(rows14, rows14, cst(C_COLMASK, 64).unsqueeze(1).broadcast_to([P, 14, 64]),
                                            ALU.add).then_inc(*done("bias_ready", (l, hh)))
                pool.wait_ge(*at("scores", (("nb", l, 0), NT - 1, HEADS - 1)))
                load_rows(("mixer", l), a["ln1_g_2"][l], a["ln1_b_2"][l])
                tiles = list(range(NT + NC)) if l == 0 else list(range(NT))
                for t in mixer_tiles(l):
                    st = ("route", l)
                    pool.wait_ge(*at("tile_ready", (st, t)))
                    pool.dma_start(a["x_norm"][l][t * P:(t + 1) * P, :], xt[:, t % 2, :]).then_inc(sem("x_norm_stored"), 16)
                    n_stored[0] += 16
                    marks[("x_norm_stored", st, t)] = n_stored[0]
                    nc.gpsimd.tensor_scalar(res(t), res(t), ALPHA, None, ALU.mult).then_inc(*done("residual", (l, t)))
                    pool.wait_ge(*at("residual", (l, t)))
                    pool.dma_start(a["y_moe"][l][t * P:(t + 1) * P, :], res(t)).then_inc(sem("residual_stored"), 16)
                    pool.wait_ge(sem("x_norm_stored"), n_stored[0])
                marks[("x_norm_stored_all", l)] = n_stored[0]
                gate_diagonals(pool, nc.gpsimd, l, 1)
                experts_pool(pool, l, load_rows)
                for b in range(2):
                    pool.wait_ge(sem(f"gathered{b}"), known.get(("gather", l, b), 16) + 16 * ROUNDS)
                pool.wait_ge(sem("scattered"), known.get(("scatter_base", l), 0) + 16 * EXPERTS)
                for t in tiles:
                    pool.dma_start(res(t), a["y_moe"][l][t * P:(t + 1) * P, :]).then_inc(sem(f"y_landed{t}"), 16)
            for t in range(NT):
                pool.wait_ge(*at("out_ready", t))
                pool.dma_start(a["out"][t * P:(t + 1) * P, :], h[:, t, :]).then_inc(sem("out_stored"), 16)
            pool.wait_ge(sem("out_stored"), 16 * NT)

        @block.sync
        def _(sp_):
            for t in range(NT):
                sp_.dma_start(h[:, t, :], a["x"][t * P:(t + 1) * P, :]).then_inc(sem(f"x_landed{t}"), 16)
                if t == 0:
                    sp_.dma_start(lnrow[:, 0, :], a["ln_in_g"].partition_broadcast(P)).then_inc(sem("in_rows_landed"), 16)
                    sp_.dma_start(lnrow[:, 1, :], a["ln_in_b"].partition_broadcast(P)).then_inc(sem("in_rows_landed"), 16)
                    sp_.dma_start(const[:, 0:C_COS], a["const"][:, 0:C_COS]).then_inc(sem("const_landed"), 16)
            sp_.dma_start(const[:, C_COS:C_END], a["const"][:, C_COS:C_END]).then_inc(sem("const_rest_landed"), 16)
            sp_.dma_start(grow[:, 0, :], a["mem_ln_g"].partition_broadcast(P)).then_inc(sem("mem_rows_landed"), 16)
            sp_.dma_start(grow[:, 1, :], a["mem_ln_b"].partition_broadcast(P)).then_inc(sem("mem_rows_landed"), 16)
            for t in (NT, NT + 1):
                sp_.dma_start(hc[:, t - NT, :], a["mem"][(t - NT) * P:(t - NT + 1) * P, :]).then_inc(sem(f"x_landed{t}"), 16)
            mods = iter(mod_order)
            for l in range(DEPTH):
                for item in first_block_slots(l):
                    if item == "mod":
                        for _ in range(3):
                            ml, j = next(mods)
                            for q in range(4):
                                load_slot(sp_, ("mod", ml, 4 * j + q), w_cols(a["w_mod_2"], ml, (4 * j + q) * P))
                    else:
                        load_slot(sp_, *item)
            for l in range(DEPTH):
                for item in second_block_slots(l):
                    load_slot(sp_, *item)
                while len(slot_keys) % RING:
                    slot_keys.append(None)
                old_keys = [last_in_slot(s) for s in range(RING)]
                for s in range(EXPERT_SLOTS):
                    places[("moe_slot", l, s)] = 16 * slot_uses[s] if s < RING else 16 * EXPERTS * l
                base = known.get(("moe_k", (l, 0, 0, 0)), 1) - 1

                def slot_free(s):
                    if s < RING:
                        sp_.wait_ge(*at(*banks.get(("last", old_keys[s]), ("job_done", None))))
                    elif s == RING:
                        sp_.wait_ge(*at("job_done", ("out", ("mixer", l), mixer_tiles(l)[-1], 1)))
                        sp_.wait_ge(*at_last_store(l))
                    elif s == EXPERT_SLOTS - 4:
                        sp_.wait_ge(*at("job_done", ("route", ("route", l), mixer_tiles(l)[-1])))

                def body(i):
                    for u in range(2):
                        e = 2 * i + u
                        for m, w in enumerate((a["w_gate_2"], a["w_up_2"], a["w_down_2"])):
                            for k in range(KD):
                                s = KD * m + k
                                if first_round(i) and u == 0:
                                    slot_free(s)
                                else:
                                    sp_.wait_ge(sem("moe_k"), i * 48 + (base + EXPERT_SLOTS * (u - 1) + s + 1))
                                if first_round(i):
                                    src = w[l, e, k * P:(k + 1) * P, :]
                                else:
                                    src = w[l, bass.ds(e, 1), k * P:(k + 1) * P, :].rearrange("o p n -> (o p) n")
                                sp_.dma_start(expert_slot(s), src).then_inc(sem(f"slot{s}"), 16)

                body(0)
                with sp_.Fori(1, ROUNDS) as i:
                    body(i)
                for s in range(RING):
                    slot_uses[s] += EXPERTS
                slot_keys.extend(("moe_end", l, s) for s in range(RING))

    return marks, places, list(sems)


def program_inputs(inputs):
    f = {k: np.ascontiguousarray(np.asarray(x)) for k, x in inputs.items()}
    const, axial = shape_constants()
    out = {"const": const, "axial": axial}
    for k in ("ln_in_g", "ln_in_b", "mem_ln_g", "mem_ln_b", "w_in", "w_mla_q_up", "w_mla_kv_up", "w_mem_kv", "w_out",
              "ln_g", "ln_b", "w_mod_2", "w_in_2", "w_out_2", "ln1_g_2", "ln1_b_2", "w_router_2", "w_gate_2", "w_up_2",
              "w_down_2", "ln2_g_2", "ln2_b_2"):
        out[k] = f[k]
    out["x"], out["mem"], out["ctx_2"] = f["x"][0], f["mem"][0], f["ctx_2"][0]
    vec = np.zeros((P, V_END), np.float32)
    vec[:, V_BMOD:V_CONVW] = f["b_mod_2"].reshape(DEPTH * 48, P).T
    vec[:, V_CONVW:V_CONVB] = f["conv_w_2"].reshape(DEPTH, TAPS, 2, P).transpose(3, 0, 2, 1).reshape(P, -1)
    vec[:, V_CONVB:V_CLNG] = f["conv_b_2"].reshape(DEPTH * 2, P).T
    vec[:, V_CLNG:V_CLNB] = f["conv_ln_g_2"].reshape(DEPTH * 2, P).T
    vec[:, V_CLNB:V_MQG] = f["conv_ln_b_2"].reshape(DEPTH * 2, P).T
    vec[:, V_MQG:V_MKVG] = f["mla_q_norm_g"].reshape(DEPTH * 2, P).T
    vec[:, V_MKVG:V_BF] = f["mla_kv_norm_g"].T
    vec[0:HEADS, V_BF:V_SINK] = f["b_forget"].T
    vec[:, V_SINK:V_COND] = f["a_sink_2"].reshape(1, -1)
    both = np.stack([f["c_2"][0], f["c_ctx_2"]])
    vec[:, V_COND:V_END] = both.reshape(2, KD, P).transpose(2, 1, 0).reshape(P, -1)
    out["vec"] = vec
    q = np.arange(64)
    dc = np.clip(q[None, :] - q[:, None], -15, 15) + 15
    nb = f["nat_bias_2"][:, :, :, dc]
    out["nat_bias_2"] = np.ascontiguousarray(nb.transpose(0, 1, 3, 2, 4)).reshape(DEPTH, HEADS, 64, 15 * 64)
    return out


def declare(nc, arrays):
    a = {k: nc.dram_tensor(f"in_{k}", x.shape, mybir.dt.from_np(x.dtype), kind="ExternalInput").ap()
         for k, x in arrays.items()}
    a["out"] = nc.dram_tensor("out_0", (SEQ, D), F32, kind="ExternalOutput").ap()
    for name in ("x_norm", "y_moe"):
        a[name] = [nc.dram_tensor(f"{name}{l}", (P * tiles_of(l), D), F32, kind="Internal").ap() for l in range(DEPTH)]
    return a


def kernel(**inputs):
    import concourse.bacc as bacc
    from concourse.bass_utils import run_bass_kernel_spmd

    arrays = program_inputs(inputs)
    noted = ({}, {}, [])
    for _ in range(2):
        nc = bacc.Bacc("TRN2", target_bir_lowering=False, num_devices=1)
        noted = build_program(nc, declare(nc, arrays), *noted)
    r = run_bass_kernel_spmd(nc, [{f"in_{k}": x for k, x in arrays.items()}], core_ids=[0])
    return np.asarray(r.results[0]["out_0"]).reshape(1, SEQ, D)
```
